# Optimizing a Trainium2 kernel written in Bass

```python
import jax, jax.numpy as jnp
from jax import lax
import numpy as np
import math

D_MODEL = 1024
BATCH = 1
SEQ = 256
DEPTH = 2

GRID_W = 64
CTX_LEN = 256
N_MIXERS = 3
Q_BLOCK = 128
ROPE_THETA = 10000.0
NORM_EPS = 1e-6
N_MOD = 6
MLA_HEADS = 8
MLA_Q_LORA = 512
MLA_KV_LORA = 256
MLA_NOPE = 128
MLA_ROPE = 64
MLA_V = 128
CONV_WIDTH = 3
CONV_DIM = D_MODEL
GQA_HEADS = 16
GQA_KV_HEADS = 8
GQA_HEAD_DIM = 128
MOE_GROUPS = 4
MOE_EXPERTS_PER_GROUP = 8
MOE_EXPERTS = MOE_GROUPS * MOE_EXPERTS_PER_GROUP
MOE_TOP_K = 2
MOE_FF = 512
MOE_BLOCK = 128


def _n_layers_of(kind):
    return len(range(kind, DEPTH, N_MIXERS))

def _rmsnorm(x, g):
    xf = x.astype(jnp.float32)
    y = xf * lax.rsqrt(jnp.mean(xf * xf, axis=-1, keepdims=True) + NORM_EPS)
    return (y * g.astype(jnp.float32)).astype(x.dtype)

def _modulate(x, g, shift, scale):
    return _rmsnorm(x, g) * (1 + scale) + shift

def _rope_1d(x, pos):
    half = x.shape[-1] // 2
    inv_freq = ROPE_THETA ** (-jnp.arange(half, dtype=jnp.float32) / half)
    ang = pos.astype(jnp.float32)[:, None] * inv_freq[None, :]
    cos, sin = jnp.cos(ang)[:, None, :], jnp.sin(ang)[:, None, :]
    xf = x.astype(jnp.float32)
    x1, x2 = xf[..., :half], xf[..., half:]
    return jnp.concatenate([x1 * cos - x2 * sin, x1 * sin + x2 * cos], axis=-1).astype(x.dtype)

def _axial_rope(x, rows, cols):
    half = x.shape[-1] // 2
    return jnp.concatenate([_rope_1d(x[..., :half], rows), _rope_1d(x[..., half:], cols)], axis=-1)

def _attend(q, k, v, scale):
    B, n, H, dk = q.shape
    Hk, dv = k.shape[2], v.shape[-1]
    G = H // Hk
    nb = n // Q_BLOCK
    qb = q.reshape(B, nb, Q_BLOCK, Hk, G, dk).transpose(1, 0, 2, 3, 4, 5)

    def block(qblk):
        s = jnp.einsum("bqhgd,bkhd->bhgqk", qblk, k).astype(jnp.float32) * scale
        p = jax.nn.softmax(s, axis=-1).astype(v.dtype)
        return jnp.einsum("bhgqk,bkhd->bqhgd", p, v)

    o = lax.map(block, qb)
    return o.transpose(1, 0, 2, 3, 4, 5).reshape(B, n, H * dv)

def _mla_project(a, w_dq, g_q, w_uq, w_dkv, g_kv, w_ukv, pos, want_q):
    B, n, _ = a.shape
    ckv = a @ w_dkv
    c_kv = _rmsnorm(ckv[..., :MLA_KV_LORA], g_kv)
    k_pe = ckv[..., MLA_KV_LORA:][:, :, None, :]
    kv = (c_kv @ w_ukv).reshape(B, n, MLA_HEADS, MLA_NOPE + MLA_V)
    k_nope, v = kv[..., :MLA_NOPE], kv[..., MLA_NOPE:]
    if pos is not None:
        k_pe = _axial_rope(k_pe, *pos)
    k = jnp.concatenate([k_nope, jnp.broadcast_to(k_pe, (B, n, MLA_HEADS, MLA_ROPE))], axis=-1)
    q = None
    if want_q:
        cq = _rmsnorm(a @ w_dq, g_q)
        q = (cq @ w_uq).reshape(B, n, MLA_HEADS, MLA_NOPE + MLA_ROPE)
        if pos is not None:
            q = jnp.concatenate([q[..., :MLA_NOPE], _axial_rope(q[..., MLA_NOPE:], *pos)], axis=-1)
    return q, k, v

def _mla(a_lat, a_ctx, pos, ctx_out, w_dq, g_q, w_uq, w_dkv, g_kv, w_ukv, w_o):
    scale = (MLA_NOPE + MLA_ROPE) ** -0.5
    q_l, k_l, v_l = _mla_project(a_lat, w_dq, g_q, w_uq, w_dkv, g_kv, w_ukv, pos, True)
    q_c, k_c, v_c = _mla_project(a_ctx, w_dq, g_q, w_uq, w_dkv, g_kv, w_ukv, None, ctx_out)
    k_all = jnp.concatenate([k_c, k_l], axis=1)
    v_all = jnp.concatenate([v_c, v_l], axis=1)
    y_lat = _attend(q_l, k_all, v_all, scale) @ w_o
    y_ctx = _attend(q_c, k_c, v_c, scale) @ w_o if ctx_out else None
    return y_lat, y_ctx

def _short_conv_seq(a, w_in, conv_w, w_out):
    bcu = a @ w_in
    b_gate, c_gate, u = jnp.split(bcu, 3, axis=-1)
    z = lax.conv_general_dilated(
        c_gate * u, conv_w[:, None, :], window_strides=(1,),
        padding=[((CONV_WIDTH - 1) // 2, (CONV_WIDTH - 1) // 2)],
        dimension_numbers=("NWC", "WIO", "NWC"), feature_group_count=CONV_DIM)
    return (b_gate * z) @ w_out

def _short_conv(a_lat, a_ctx, ctx_out, w_in, conv_w, w_out):
    y_lat = _short_conv_seq(a_lat, w_in, conv_w, w_out)
    y_ctx = _short_conv_seq(a_ctx, w_in, conv_w, w_out) if ctx_out else None
    return y_lat, y_ctx

def _gqa_project(a, w_qkv, q_g, k_g, pos, want_q):
    B, n, _ = a.shape
    dq = GQA_HEADS * GQA_HEAD_DIM
    dkv = GQA_KV_HEADS * GQA_HEAD_DIM
    kv = a @ w_qkv[:, dq:]
    k = _rmsnorm(kv[..., :dkv].reshape(B, n, GQA_KV_HEADS, GQA_HEAD_DIM), k_g)
    v = kv[..., dkv:].reshape(B, n, GQA_KV_HEADS, GQA_HEAD_DIM)
    if pos is not None:
        k = _axial_rope(k, *pos)
    q = None
    if want_q:
        q = _rmsnorm((a @ w_qkv[:, :dq]).reshape(B, n, GQA_HEADS, GQA_HEAD_DIM), q_g)
        if pos is not None:
            q = _axial_rope(q, *pos)
    return q, k, v

def _gqa(a_lat, a_ctx, pos, ctx_out, w_qkv, q_g, k_g, w_o):
    scale = GQA_HEAD_DIM ** -0.5
    q_l, k_l, v_l = _gqa_project(a_lat, w_qkv, q_g, k_g, pos, True)
    q_c, k_c, v_c = _gqa_project(a_ctx, w_qkv, q_g, k_g, None, ctx_out)
    k_all = jnp.concatenate([k_c, k_l], axis=1)
    v_all = jnp.concatenate([v_c, v_l], axis=1)
    y_lat = _attend(q_l, k_all, v_all, scale) @ w_o
    y_ctx = _attend(q_c, k_c, v_c, scale) @ w_o if ctx_out else None
    return y_lat, y_ctx

def _hier_moe(h, w_group, b_group, w_expert, b_expert, w_gate, w_up, w_down):
    T, D = h.shape
    hf = h.astype(jnp.float32)
    g_prob = jax.nn.softmax(hf @ w_group.astype(jnp.float32), axis=-1)
    g_sel = jnp.argmax(g_prob + b_group.astype(jnp.float32), axis=-1)
    g_w = jnp.take_along_axis(g_prob, g_sel[:, None], axis=-1)
    e_logits = (hf @ w_expert.astype(jnp.float32)).reshape(T, MOE_GROUPS, MOE_EXPERTS_PER_GROUP)
    e_prob = jax.nn.softmax(jnp.take_along_axis(e_logits, g_sel[:, None, None], axis=1)[:, 0], axis=-1)
    e_bias = b_expert.astype(jnp.float32).reshape(MOE_GROUPS, MOE_EXPERTS_PER_GROUP)[g_sel]
    _, top_idx = lax.top_k(e_prob + e_bias, MOE_TOP_K)
    top_w = jnp.take_along_axis(e_prob, top_idx, axis=-1)
    top_w = top_w / jnp.sum(top_w, axis=-1, keepdims=True) * g_w
    expert_id = g_sel[:, None] * MOE_EXPERTS_PER_GROUP + top_idx

    A = T * MOE_TOP_K
    eid = expert_id.reshape(A)
    tok = jnp.arange(A, dtype=jnp.int32) // MOE_TOP_K
    wts = top_w.reshape(A)
    order = jnp.argsort(eid)
    e_s, tok_s, w_s = eid[order], tok[order], wts[order]
    counts = jnp.bincount(eid, length=MOE_EXPERTS)
    starts = jnp.cumsum(counts) - counts
    padded = (counts + MOE_BLOCK - 1) // MOE_BLOCK * MOE_BLOCK
    pends = jnp.cumsum(padded)
    pstarts = pends - padded
    dest = pstarts[e_s] + (jnp.arange(A, dtype=jnp.int32) - starts[e_s])
    nb = -(-A // MOE_BLOCK) + MOE_EXPERTS
    xp = jnp.zeros((nb * MOE_BLOCK, D), h.dtype).at[dest].set(h[tok_s])
    blk_e = jnp.clip(jnp.searchsorted(pends, jnp.arange(nb, dtype=jnp.int32) * MOE_BLOCK, side="right"),
                     0, MOE_EXPERTS - 1)

    def expert_block(args):
        xb, e = args
        return (jax.nn.silu(xb @ w_gate[e]) * (xb @ w_up[e])) @ w_down[e]

    yp = lax.map(expert_block, (xp.reshape(nb, MOE_BLOCK, D), blk_e)).reshape(nb * MOE_BLOCK, D)
    return jax.ops.segment_sum(yp[dest] * w_s[:, None].astype(h.dtype), tok_s, num_segments=T)

def _normal(k, shape, scale):
    return jax.random.normal(k, shape, jnp.float32) * scale

def first_inputs(seed: int = 0) -> dict:
    key = jax.random.key(seed)
    ks = iter(jax.random.split(key, 40))
    D = D_MODEL
    nA, nB, nC = _n_layers_of(0), _n_layers_of(1), _n_layers_of(2)
    dq = GQA_HEADS * GQA_HEAD_DIM
    dkv = GQA_KV_HEADS * GQA_HEAD_DIM
    return {
        "x": _normal(next(ks), (BATCH, SEQ, D), 1.0),
        "c": _normal(next(ks), (BATCH, D), 1.0),
        "ctx": _normal(next(ks), (BATCH, CTX_LEN, D), 1.0),
        "c_ctx": _normal(next(ks), (D,), 1.0),
        "w_mod": _normal(next(ks), (DEPTH, D, N_MOD * D), 0.5 * D ** -0.5),
        "b_mod": _normal(next(ks), (DEPTH, N_MOD * D), 0.02),
        "norm_mix_g": 1.0 + _normal(next(ks), (DEPTH, D), 0.05),
        "norm_ffn_g": 1.0 + _normal(next(ks), (DEPTH, D), 0.05),
        "mla_w_dq": _normal(next(ks), (nA, D, MLA_Q_LORA), D ** -0.5),
        "mla_g_q": 1.0 + _normal(next(ks), (nA, MLA_Q_LORA), 0.05),
        "mla_w_uq": _normal(next(ks), (nA, MLA_Q_LORA, MLA_HEADS * (MLA_NOPE + MLA_ROPE)), MLA_Q_LORA ** -0.5),
        "mla_w_dkv": _normal(next(ks), (nA, D, MLA_KV_LORA + MLA_ROPE), D ** -0.5),
        "mla_g_kv": 1.0 + _normal(next(ks), (nA, MLA_KV_LORA), 0.05),
        "mla_w_ukv": _normal(next(ks), (nA, MLA_KV_LORA, MLA_HEADS * (MLA_NOPE + MLA_V)), MLA_KV_LORA ** -0.5),
        "mla_w_o": _normal(next(ks), (nA, MLA_HEADS * MLA_V, D), (MLA_HEADS * MLA_V) ** -0.5),
        "conv_w_in": _normal(next(ks), (nB, D, 3 * CONV_DIM), D ** -0.5),
        "conv_w": _normal(next(ks), (nB, CONV_WIDTH, CONV_DIM), CONV_WIDTH ** -0.5),
        "conv_w_out": _normal(next(ks), (nB, CONV_DIM, D), CONV_DIM ** -0.5),
        "gqa_w_qkv": _normal(next(ks), (nC, D, dq + 2 * dkv), D ** -0.5),
        "gqa_q_norm_g": 1.0 + _normal(next(ks), (nC, GQA_HEAD_DIM), 0.05),
        "gqa_k_norm_g": 1.0 + _normal(next(ks), (nC, GQA_HEAD_DIM), 0.05),
        "gqa_w_o": _normal(next(ks), (nC, dq, D), dq ** -0.5),
        "moe_w_group": _normal(next(ks), (DEPTH, D, MOE_GROUPS), D ** -0.5),
        "moe_b_group": _normal(next(ks), (DEPTH, MOE_GROUPS), 0.01),
        "moe_w_expert": _normal(next(ks), (DEPTH, D, MOE_EXPERTS), D ** -0.5),
        "moe_b_expert": _normal(next(ks), (DEPTH, MOE_EXPERTS), 0.01),
        "moe_w_gate": _normal(next(ks), (DEPTH, MOE_EXPERTS, D, MOE_FF), D ** -0.5),
        "moe_w_up": _normal(next(ks), (DEPTH, MOE_EXPERTS, D, MOE_FF), D ** -0.5),
        "moe_w_down": _normal(next(ks), (DEPTH, MOE_EXPERTS, MOE_FF, D), MOE_FF ** -0.5),
        "final_norm_g": 1.0 + _normal(next(ks), (D,), 0.05),
    }

def first_block(x, c, ctx, c_ctx, w_mod, b_mod, norm_mix_g, norm_ffn_g,
              mla_w_dq, mla_g_q, mla_w_uq, mla_w_dkv, mla_g_kv, mla_w_ukv, mla_w_o,
              conv_w_in, conv_w, conv_w_out,
              gqa_w_qkv, gqa_q_norm_g, gqa_k_norm_g, gqa_w_o,
              moe_w_group, moe_b_group, moe_w_expert, moe_b_expert, moe_w_gate, moe_w_up, moe_w_down,
              final_norm_g):
    B, S, D = x.shape
    L = ctx.shape[1]
    ROWS = S // GRID_W
    rows = jnp.repeat(jnp.arange(ROWS, dtype=jnp.int32), GRID_W)
    cols = jnp.tile(jnp.arange(GRID_W, dtype=jnp.int32), ROWS)
    pos = (rows, cols)
    cond_lat = jax.nn.silu(c)
    cond_ctx = jax.nn.silu(c_ctx)[None]
    h = ctx
    for i in range(DEPTH):
        kind, j = i % N_MIXERS, i // N_MIXERS
        ctx_out = i < DEPTH - 1
        mod_l = (cond_lat @ w_mod[i] + b_mod[i])[:, None, :]
        mod_c = (cond_ctx @ w_mod[i] + b_mod[i])[:, None, :]
        sh1, sc1, g1, sh2, sc2, g2 = jnp.split(mod_l, N_MOD, axis=-1)
        csh1, csc1, cg1, csh2, csc2, cg2 = jnp.split(mod_c, N_MOD, axis=-1)
        a_lat = _modulate(x, norm_mix_g[i], sh1, sc1)
        a_ctx = _modulate(h, norm_mix_g[i], csh1, csc1)
        if kind == 0:
            y_lat, y_ctx = _mla(a_lat, a_ctx, pos, ctx_out, mla_w_dq[j], mla_g_q[j], mla_w_uq[j],
                                mla_w_dkv[j], mla_g_kv[j], mla_w_ukv[j], mla_w_o[j])
        elif kind == 1:
            y_lat, y_ctx = _short_conv(a_lat, a_ctx, ctx_out, conv_w_in[j], conv_w[j], conv_w_out[j])
        else:
            y_lat, y_ctx = _gqa(a_lat, a_ctx, pos, ctx_out, gqa_w_qkv[j], gqa_q_norm_g[j],
                                gqa_k_norm_g[j], gqa_w_o[j])
        x = x + g1 * y_lat
        f_lat = _modulate(x, norm_ffn_g[i], sh2, sc2)
        moe_args = (moe_w_group[i], moe_b_group[i], moe_w_expert[i], moe_b_expert[i],
                    moe_w_gate[i], moe_w_up[i], moe_w_down[i])
        if ctx_out:
            h = h + cg1 * y_ctx
            f_ctx = _modulate(h, norm_ffn_g[i], csh2, csc2)
            tokens = jnp.concatenate([f_lat.reshape(B * S, D), f_ctx.reshape(B * L, D)], axis=0)
            y = _hier_moe(tokens, *moe_args)
            x = x + g2 * y[:B * S].reshape(B, S, D)
            h = h + cg2 * y[B * S:].reshape(B, L, D)
        else:
            y = _hier_moe(f_lat.reshape(B * S, D), *moe_args)
            x = x + g2 * y.reshape(B, S, D)
    return _rmsnorm(x, final_norm_g)


N_A_LAYERS = DEPTH // 2
N_B_LAYERS = DEPTH - N_A_LAYERS
RMS_EPS = 1e-6
GATED_NORM_EPS = 1e-5

SSM_EXPAND = 2
SSM_D_INNER = SSM_EXPAND * D_MODEL
SSM_HEAD_DIM = 64
SSM_N_HEADS = SSM_D_INNER // SSM_HEAD_DIM
SSM_N_GROUPS = 8
SSM_D_STATE = 128
SSM_CONV = 4
SSM_CHUNK = 128
SSM_CONV_DIM = SSM_D_INNER + 2 * SSM_N_GROUPS * SSM_D_STATE
SSM_IN_DIM = SSM_D_INNER + SSM_CONV_DIM + SSM_N_HEADS

ATT_PATTERNS = ((128, 1), (512, 4), (2048, 16))
ATT_N_GROUPS = len(ATT_PATTERNS)
ATT_HEAD_DIM = 128
ATT_HEADS_PER_GROUP = 8
ATT_KV_HEADS_PER_GROUP = 2
ATT_Q_DIM = ATT_N_GROUPS * ATT_HEADS_PER_GROUP * ATT_HEAD_DIM
ATT_KV_DIM = ATT_N_GROUPS * ATT_KV_HEADS_PER_GROUP * ATT_HEAD_DIM
ATT_OUT_DIM = ATT_HEADS_PER_GROUP * ATT_HEAD_DIM
ROPE_DIM = ATT_HEAD_DIM // 4
ROPE_THETA_2 = 500000.0

FFN_DIM = 2816
FFN_CONV = 3


def _rms_norm(x, w, eps=RMS_EPS):
    xf = x.astype(jnp.float32)
    y = xf * lax.rsqrt(jnp.mean(xf * xf, axis=-1, keepdims=True) + eps)
    return (y * w.astype(jnp.float32)).astype(x.dtype)

def _causal_depthwise_conv(x, w):
    width, ch = w.shape
    return lax.conv_general_dilated(
        x, w[:, None, :].astype(x.dtype), window_strides=(1,),
        padding=((width - 1, 0),), dimension_numbers=('NWC', 'WIO', 'NWC'),
        feature_group_count=ch)

def _partial_rotary(x, positions):
    half = ROPE_DIM // 2
    inv_freq = jnp.power(jnp.float32(ROPE_THETA_2), -jnp.arange(0, ROPE_DIM, 2, dtype=jnp.float32) / ROPE_DIM)
    ang = positions.astype(jnp.float32)[:, None] * inv_freq[None, :]
    cos = jnp.cos(ang)[None, :, None, :]
    sin = jnp.sin(ang)[None, :, None, :]
    xf = x.astype(jnp.float32)
    x1, x2, rest = xf[..., :half], xf[..., half:ROPE_DIM], xf[..., ROPE_DIM:]
    out = jnp.concatenate([x1 * cos - x2 * sin, x2 * cos + x1 * sin, rest], axis=-1)
    return out.astype(x.dtype)

def _ssd_chunked(x, dt, a, b_in, c_in):
    bsz, seq, nh, hp = x.shape
    ng, ns = b_in.shape[2], b_in.shape[3]
    hg = nh // ng
    nc, L = seq // SSM_CHUNK, SSM_CHUNK
    xc = (x.astype(jnp.float32) * dt[..., None]).reshape(bsz, nc, L, ng, hg, hp)
    adt = (dt * a).reshape(bsz, nc, L, ng, hg).transpose(0, 1, 3, 4, 2)
    a_cs = jnp.cumsum(adt, axis=-1)
    bc = b_in.astype(jnp.float32).reshape(bsz, nc, L, ng, ns)
    cc = c_in.astype(jnp.float32).reshape(bsz, nc, L, ng, ns)
    tril = jnp.tril(jnp.ones((L, L), dtype=bool))
    seg = a_cs[..., :, None] - a_cs[..., None, :]
    decay = jnp.exp(jnp.where(tril, seg, -jnp.inf))
    cb = jnp.einsum('bclgn,bcsgn->bcgls', cc, bc)
    y_diag = jnp.einsum('bcgls,bcghls,bcsghp->bclghp', cb, decay, xc)
    decay_states = jnp.exp(a_cs[..., -1:] - a_cs)
    states = jnp.einsum('bclgn,bcghl,bclghp->bcghpn', bc, decay_states, xc)
    chunk_decay = jnp.exp(a_cs[..., -1])

    def step(h, inp):
        st, dec = inp
        return h * dec[..., None, None] + st, h

    h0 = jnp.zeros((bsz, ng, hg, hp, ns), jnp.float32)
    _, prev = lax.scan(step, h0, (jnp.moveaxis(states, 1, 0), jnp.moveaxis(chunk_decay, 1, 0)))
    prev = jnp.moveaxis(prev, 0, 1)
    y_off = jnp.einsum('bclgn,bcghpn,bcghl->bclghp', cc, prev, jnp.exp(a_cs))
    return (y_diag + y_off).reshape(bsz, seq, nh, hp)

def _mamba2_mixer(h, w_in, conv_w, conv_b, dt_bias, a_log, d_skip, norm_w, w_out):
    bsz, seq, _ = h.shape
    zxbcdt = h @ w_in.astype(h.dtype)
    z = zxbcdt[..., :SSM_D_INNER]
    xbc = zxbcdt[..., SSM_D_INNER:SSM_D_INNER + SSM_CONV_DIM]
    dt_raw = zxbcdt[..., SSM_D_INNER + SSM_CONV_DIM:]
    xbc = jax.nn.silu(_causal_depthwise_conv(xbc, conv_w) + conv_b.astype(h.dtype))
    gn = SSM_N_GROUPS * SSM_D_STATE
    xs = xbc[..., :SSM_D_INNER].reshape(bsz, seq, SSM_N_HEADS, SSM_HEAD_DIM)
    b_in = xbc[..., SSM_D_INNER:SSM_D_INNER + gn].reshape(bsz, seq, SSM_N_GROUPS, SSM_D_STATE)
    c_in = xbc[..., SSM_D_INNER + gn:].reshape(bsz, seq, SSM_N_GROUPS, SSM_D_STATE)
    dt = jax.nn.softplus(dt_raw.astype(jnp.float32) + dt_bias.astype(jnp.float32))
    a = -jnp.exp(a_log.astype(jnp.float32))
    y = _ssd_chunked(xs, dt, a, b_in, c_in)
    y = y + xs.astype(jnp.float32) * d_skip.astype(jnp.float32)[:, None]
    y = y.reshape(bsz, seq, SSM_D_INNER) * jax.nn.silu(z.astype(jnp.float32))
    yg = y.reshape(bsz, seq, SSM_N_GROUPS, SSM_D_INNER // SSM_N_GROUPS)
    yg = yg * lax.rsqrt(jnp.mean(yg * yg, axis=-1, keepdims=True) + GATED_NORM_EPS)
    y = yg.reshape(bsz, seq, SSM_D_INNER) * norm_w.astype(jnp.float32)
    return y.astype(h.dtype) @ w_out.astype(h.dtype)

def _shared_kv(x, kv_norm, w_kv, positions):
    bsz, seq, _ = x.shape
    kv = (_rms_norm(x, kv_norm) @ w_kv.astype(x.dtype)).reshape(
        bsz, seq, 2, ATT_N_GROUPS * ATT_KV_HEADS_PER_GROUP, ATT_HEAD_DIM)
    k = _partial_rotary(kv[:, :, 0], positions).reshape(bsz, seq, ATT_N_GROUPS, ATT_KV_HEADS_PER_GROUP, ATT_HEAD_DIM)
    v = kv[:, :, 1].reshape(bsz, seq, ATT_N_GROUPS, ATT_KV_HEADS_PER_GROUP, ATT_HEAD_DIM)
    return k, v

def _dilated_group_attention(q, k, v, window, dilation):
    bsz, seq, n_heads, hd = q.shape
    n_kv = k.shape[2]
    rep = n_heads // n_kv
    blk = window // dilation
    n_sub = seq // dilation
    n_blk = -(-n_sub // blk)
    n_pad = n_blk * blk

    def to_blocks(t):
        t = jnp.moveaxis(t.reshape(bsz, n_sub, dilation, *t.shape[2:]), 2, 1)
        pad = [(0, 0)] * t.ndim
        pad[2] = (0, n_pad - n_sub)
        t = jnp.pad(t, pad)
        return t.reshape(bsz, dilation, n_blk, blk, *t.shape[3:])

    def with_prev(t):
        prev = jnp.pad(t[:, :, :-1], ((0, 0), (0, 0), (1, 0), (0, 0), (0, 0), (0, 0)))
        return jnp.concatenate([prev, t], axis=3)

    qb = to_blocks(q.astype(jnp.float32)).reshape(bsz, dilation, n_blk, blk, n_kv, rep, hd)
    kb = with_prev(to_blocks(k.astype(jnp.float32)))
    vb = with_prev(to_blocks(v.astype(jnp.float32)))
    scores = jnp.einsum('brnqhgd,brnshd->brnhgqs', qb, kb) * (hd ** -0.5)
    q_idx = jnp.arange(blk)[:, None]
    s_idx = jnp.arange(2 * blk)[None, :]
    rel = q_idx + blk - s_idx
    band = (rel >= 0) & (rel <= blk)
    has_prev = (jnp.arange(n_blk) > 0)[:, None, None] | (s_idx >= blk)[None]
    mask = band[None] & has_prev
    scores = jnp.where(mask[:, None, None], scores, -jnp.inf)
    m = jnp.max(scores, axis=-1, keepdims=True)
    p = jnp.exp(scores - m)
    denom = jnp.sum(p, axis=-1)
    lse = jnp.transpose(m[..., 0] + jnp.log(denom), (0, 1, 2, 5, 3, 4))
    out = jnp.einsum('brnhgqs,brnshd->brnqhgd', p, vb) / jnp.transpose(denom, (0, 1, 2, 5, 3, 4))[..., None]

    def from_blocks(t):
        t = t.reshape(bsz, dilation, n_pad, n_heads, *t.shape[6:])[:, :, :n_sub]
        return jnp.moveaxis(t, 1, 2).reshape(bsz, seq, n_heads, *t.shape[4:])

    return from_blocks(out), from_blocks(lse)

def _dilated_mixer(h, k_sh, v_sh, w_q, w_o, positions):
    bsz, seq, _ = h.shape
    q = (h @ w_q.astype(h.dtype)).reshape(bsz, seq, ATT_N_GROUPS * ATT_HEADS_PER_GROUP, ATT_HEAD_DIM)
    q = _partial_rotary(q, positions).reshape(bsz, seq, ATT_N_GROUPS, ATT_HEADS_PER_GROUP, ATT_HEAD_DIM)
    outs, lses = [], []
    for g, (window, dilation) in enumerate(ATT_PATTERNS):
        o_g, lse_g = _dilated_group_attention(q[:, :, g], k_sh[:, :, g], v_sh[:, :, g], window, dilation)
        outs.append(o_g)
        lses.append(lse_g)
    wts = jax.nn.softmax(jnp.stack(lses, axis=0), axis=0)
    o = jnp.einsum('gbsh,gbshd->bshd', wts, jnp.stack(outs, axis=0))
    return o.reshape(bsz, seq, ATT_OUT_DIM).astype(h.dtype) @ w_o.astype(h.dtype)

def _conv_ffn(h, w_up, conv_w, w_down):
    u = _causal_depthwise_conv(h @ w_up.astype(h.dtype), conv_w)
    gate, val = u[..., :FFN_DIM], u[..., FFN_DIM:]
    return (jax.nn.silu(gate) * val) @ w_down.astype(h.dtype)

def second_inputs(seed: int = 0) -> dict:
    key = jax.random.key(seed)
    ks = jax.random.split(key, 24)
    f32 = jnp.float32
    out_scale = (2.0 * DEPTH) ** -0.5

    def nrm(k, shape, scale):
        return jax.random.normal(k, shape, f32) * scale

    x = nrm(ks[0], (BATCH, SEQ, D_MODEL), 1.0)
    a_norm = 1.0 + nrm(ks[1], (N_A_LAYERS, D_MODEL), 0.02)
    ssm_w_in = nrm(ks[2], (N_A_LAYERS, D_MODEL, SSM_IN_DIM), D_MODEL ** -0.5)
    ssm_conv_w = nrm(ks[3], (N_A_LAYERS, SSM_CONV, SSM_CONV_DIM), SSM_CONV ** -0.5)
    ssm_conv_b = nrm(ks[4], (N_A_LAYERS, SSM_CONV_DIM), 0.02)
    dt0 = jnp.exp(jax.random.uniform(ks[5], (N_A_LAYERS, SSM_N_HEADS), f32, math.log(1e-3), math.log(1e-1)))
    ssm_dt_bias = dt0 + jnp.log(-jnp.expm1(-dt0))
    ssm_a_log = jnp.log(jax.random.uniform(ks[6], (N_A_LAYERS, SSM_N_HEADS), f32, 1.0, 16.0))
    ssm_d = 1.0 + nrm(ks[7], (N_A_LAYERS, SSM_N_HEADS), 0.02)
    ssm_norm = 1.0 + nrm(ks[8], (N_A_LAYERS, SSM_D_INNER), 0.02)
    ssm_w_out = nrm(ks[9], (N_A_LAYERS, SSM_D_INNER, D_MODEL), SSM_D_INNER ** -0.5 * out_scale)
    kv_norm = 1.0 + nrm(ks[10], (D_MODEL,), 0.02)
    w_kv = nrm(ks[11], (D_MODEL, 2 * ATT_KV_DIM), D_MODEL ** -0.5)
    b_norm = 1.0 + nrm(ks[12], (N_B_LAYERS, D_MODEL), 0.02)
    att_w_q = nrm(ks[13], (N_B_LAYERS, D_MODEL, ATT_Q_DIM), D_MODEL ** -0.5)
    att_w_o = nrm(ks[14], (N_B_LAYERS, ATT_OUT_DIM, D_MODEL), ATT_OUT_DIM ** -0.5 * out_scale)
    ffn_norm = 1.0 + nrm(ks[15], (DEPTH, D_MODEL), 0.02)
    ffn_w_up = nrm(ks[16], (DEPTH, D_MODEL, 2 * FFN_DIM), D_MODEL ** -0.5)
    ffn_conv_w = nrm(ks[17], (DEPTH, FFN_CONV, 2 * FFN_DIM), FFN_CONV ** -0.5)
    ffn_w_down = nrm(ks[18], (DEPTH, FFN_DIM, D_MODEL), FFN_DIM ** -0.5 * out_scale)
    final_norm = 1.0 + nrm(ks[19], (D_MODEL,), 0.02)
    return {'x': x, 'a_norm': a_norm, 'ssm_w_in': ssm_w_in, 'ssm_conv_w': ssm_conv_w,
            'ssm_conv_b': ssm_conv_b, 'ssm_dt_bias': ssm_dt_bias, 'ssm_a_log': ssm_a_log,
            'ssm_d': ssm_d, 'ssm_norm': ssm_norm, 'ssm_w_out': ssm_w_out, 'kv_norm': kv_norm,
            'w_kv': w_kv, 'b_norm': b_norm, 'att_w_q': att_w_q, 'att_w_o': att_w_o,
            'ffn_norm': ffn_norm, 'ffn_w_up': ffn_w_up, 'ffn_conv_w': ffn_conv_w,
            'ffn_w_down': ffn_w_down, 'final_norm': final_norm}

def second_block(x, a_norm, ssm_w_in, ssm_conv_w, ssm_conv_b, ssm_dt_bias, ssm_a_log, ssm_d,
              ssm_norm, ssm_w_out, kv_norm, w_kv, b_norm, att_w_q, att_w_o,
              ffn_norm, ffn_w_up, ffn_conv_w, ffn_w_down, final_norm):
    positions = jnp.arange(x.shape[1], dtype=jnp.int32)
    k_sh, v_sh = None, None
    for layer in range(DEPTH):
        if layer < N_A_LAYERS:
            i = layer
            x = x + _mamba2_mixer(_rms_norm(x, a_norm[i]), ssm_w_in[i], ssm_conv_w[i], ssm_conv_b[i],
                                  ssm_dt_bias[i], ssm_a_log[i], ssm_d[i], ssm_norm[i], ssm_w_out[i])
        else:
            if layer == N_A_LAYERS:
                k_sh, v_sh = _shared_kv(x, kv_norm, w_kv, positions)
            j = layer - N_A_LAYERS
            x = x + _dilated_mixer(_rms_norm(x, b_norm[j]), k_sh, v_sh, att_w_q[j], att_w_o[j], positions)
        x = x + _conv_ffn(_rms_norm(x, ffn_norm[layer]), ffn_w_up[layer], ffn_conv_w[layer], ffn_w_down[layer])
    return _rms_norm(x, final_norm)


def setup_inputs(seed=0):
    out = dict(first_inputs(seed))
    for name, value in second_inputs(seed + 1).items():
        if name != "x":
            out[name + "_2"] = value
    return out


def reference(
    x, c, ctx, c_ctx, w_mod, b_mod, norm_mix_g, norm_ffn_g, mla_w_dq, mla_g_q, mla_w_uq,
    mla_w_dkv, mla_g_kv, mla_w_ukv, mla_w_o, conv_w_in, conv_w, conv_w_out, gqa_w_qkv,
    gqa_q_norm_g, gqa_k_norm_g, gqa_w_o, moe_w_group, moe_b_group, moe_w_expert, moe_b_expert,
    moe_w_gate, moe_w_up, moe_w_down, final_norm_g, a_norm_2, ssm_w_in_2, ssm_conv_w_2,
    ssm_conv_b_2, ssm_dt_bias_2, ssm_a_log_2, ssm_d_2, ssm_norm_2, ssm_w_out_2, kv_norm_2,
    w_kv_2, b_norm_2, att_w_q_2, att_w_o_2, ffn_norm_2, ffn_w_up_2, ffn_conv_w_2, ffn_w_down_2,
    final_norm_2,
):
    x = first_block(
        x, c, ctx, c_ctx, w_mod, b_mod, norm_mix_g, norm_ffn_g, mla_w_dq, mla_g_q, mla_w_uq,
        mla_w_dkv, mla_g_kv, mla_w_ukv, mla_w_o, conv_w_in, conv_w, conv_w_out, gqa_w_qkv,
        gqa_q_norm_g, gqa_k_norm_g, gqa_w_o, moe_w_group, moe_b_group, moe_w_expert,
        moe_b_expert, moe_w_gate, moe_w_up, moe_w_down, final_norm_g,
    )
    return second_block(
        x, a_norm_2, ssm_w_in_2, ssm_conv_w_2, ssm_conv_b_2, ssm_dt_bias_2, ssm_a_log_2,
        ssm_d_2, ssm_norm_2, ssm_w_out_2, kv_norm_2, w_kv_2, b_norm_2, att_w_q_2, att_w_o_2,
        ffn_norm_2, ffn_w_up_2, ffn_conv_w_2, ffn_w_down_2, final_norm_2,
    )


_drawn_inputs = setup_inputs


def setup_inputs(seed=0):
    import zlib

    import numpy as np

    out = dict(_drawn_inputs(seed))
    spreads = {}
    factors = {'mla_g_q': 8.0,
     'mla_g_kv': 5.9,
     'a_norm_2': 3.796,
     'ssm_conv_b_2': 4.102,
     'ssm_d_2': 53.328,
     'ssm_norm_2': 5.718,
     'kv_norm_2': 8.0,
     'b_norm_2': 8.0,
     'ffn_norm_2': 5.367}
    for name, (base, spread) in spreads.items():
        noise = np.random.default_rng([zlib.crc32(name.encode()), seed]).standard_normal(out[name].shape)
        drawn = base * np.exp(spread * noise) if base else spread * noise
        out[name] = __import__('jax').numpy.asarray(drawn.astype(out[name].dtype))
    for name, factor in factors.items():
        out[name] = (out[name] * factor).astype(out[name].dtype)
    return out
```

```python
from contextlib import ExitStack

import numpy as np

import concourse.bass as bass
from concourse import mybir
from concourse.alu_op_type import AluOpType as ALU

F32 = mybir.dt.float32
I32 = mybir.dt.int32
U32 = mybir.dt.uint32
ACT = mybir.ActivationFunctionType
AX = mybir.AxisListType

P = 128
BANK = 512
SLOT = 4096
RING = 6

D = 1024
KD = D // P
SEQ = 256
CTX = 256
N_MOD = 6
GRID_W = 64
MLA_HEADS = 8
MLA_NOPE = 128
MLA_ROPE = 64
MLA_V = 128
MLA_Q_LORA = 512
MLA_KV_LORA = 256
ROPE_THETA = 10000.0
NORM_EPS = 1e-6
GROUPS = 4
PER_GROUP = 8
EXPERTS = GROUPS * PER_GROUP
FF = 512
KF = FF // P
CONV_W = 3
D_INNER = 2048
HEAD_P = 64
HEADS = D_INNER // HEAD_P
SSM_G = 8
STATE = 128
HG = HEADS // SSM_G
SSM_CONV = 4
CHUNK = 128
GATED_EPS = 1e-5
PATTERNS = ((128, 1), (512, 4), (2048, 16))
N_PAT = len(PATTERNS)
ATT_HEADS = 8
ATT_KV = 2
ATT_D = 128
ROPE_DIM = ATT_D // 4
ROPE_THETA_2 = 500000.0
FFN = 2816
KFF = FFN // P
FFN_CONV = 3
CAP = (96, 80)
NEG = -1e30
BIG = 3.0e38


def column_layout():
    parts = [("cond", (KD, 2)), ("b_mod", (2, N_MOD * KD)), ("norm_mix", (2, KD)), ("norm_ffn", (2, KD)),
             ("g_q", (MLA_Q_LORA // P,)), ("g_kv", (MLA_KV_LORA // P,)), ("conv_w", (KD, CONV_W)),
             ("final_1", (KD,)), ("a_norm", (KD,)), ("ssm_conv_w", (32, SSM_CONV)), ("ssm_conv_b", (32,)),
             ("ssm_norm", (16,)), ("kv_norm", (KD,)), ("b_norm", (KD,)), ("ffn_norm", (2, KD)),
             ("ffn_conv_w", (2, 2 * KFF, FFN_CONV)), ("final_2", (KD,)), ("token", (4,))]
    at, out = 0, {}
    for name, shape in parts:
        out[name] = (at, shape)
        at += int(np.prod(shape))
    return out, at


def row_layout():
    parts = [("route_bias_0", GROUPS + EXPERTS), ("route_bias_1", GROUPS + EXPERTS), ("first_4", GROUPS),
             ("first_8", PER_GROUP), ("count", P), ("dt_bias", HEADS), ("a_log", HEADS), ("d_skip", HEADS)]
    at, out = 0, {}
    for name, n in parts:
        out[name] = (at, n)
        at += n
    return out, at


MATS = ["ident", "ones_1024", "ones_512", "ones_256", "ones", "before", "upto"]


def att_keys(qt):
    return (qt + 1) * P


class Counter:

    def __init__(self, sem, step=1):
        self.sem, self.step, self.n, self.base, self.per, self.loop = sem, step, 0, 0, 0, None

    def raised(self, loop):
        self.enter(loop)
        self.n += self.step
        return Mark(self, self.n, self.loop)

    def enter(self, loop):
        if self.loop is not loop:
            assert loop is not None
            self.loop, self.base, self.n = loop, self.n, 0
            loop.counters.append(self)

    def now(self):
        return Mark(self, self.n, self.loop)


class Mark:

    def __init__(self, counter, off, loop, frame=None):
        self.counter, self.off, self.loop = counter, off, loop

    def value(self, index, shift):
        if self.loop is None:
            return self.off
        base, per = self.loop.frames[self.counter]
        if index is None:
            return base + self.off + per * (self.loop.trips - 1)
        const = base + self.off + per * shift
        assert const > 0, self.counter.sem
        return index * per + const if per else const


class Later:

    mark = None

    def set(self, mark):
        self.mark = mark


class Loop:

    def __init__(self, shape):
        self.shape, self.trips = shape, int(np.prod(shape))
        self.counters, self.frames = [], {}


class Lane:

    def __init__(self, program, name, sem):
        self.program, self.name, self.items, self.done = program, name, [], Counter(sem)
        self.in_order = name in ("act", "dve", "pool")
        self.waited = {}

    def wait(self, *marks):
        for m in marks:
            if m is None:
                continue
            if isinstance(m, Later):
                self.items.append(("wait", m, -1))
                continue
            key = (m.counter, m.loop)
            if m.off <= self.waited.get(key, 0):
                continue
            self.waited[key] = m.off
            self.items.append(("wait", m, 0))

    def do(self, fn, *marks, inc=None, mark=True, loose=False):
        self.wait(*marks)
        if self.in_order and not loose:
            self.wait(self.done.now())
        counter = (inc or self.done) if mark else None
        self.items.append(("op", fn, counter))
        return counter.raised(self.program.loop) if counter else None

    def chain(self, fn, *marks, inc=None):
        return self.do(fn, *marks, self.done.now(), inc=inc)

    def replay(self, engine, items=None, index=None, indices=None):
        for item in (self.items if items is None else items):
            kind = item[0]
            if kind == "wait":
                mark = item[1].mark if isinstance(item[1], Later) else item[1]
                here = index if mark.loop is not None and mark.loop is self.running else None
                value = mark.value(here, item[2])
                if isinstance(value, int) and value <= 0:
                    continue
                engine.wait_ge(mark.counter.sem, value)
            elif kind == "op":
                got = item[1](engine, indices)
                if item[2] is not None:
                    got.then_inc(item[2].sem, item[2].step)
            elif kind == "loop":
                _, loop, body = item
                outer, self.running = self.running, loop
                if len(loop.shape) == 1:
                    with engine.Fori(0, loop.shape[0], 1) as i:
                        self.replay(engine, body, i, (i,))
                else:
                    with engine.Fori(0, loop.shape[0], 1) as a:
                        with engine.Fori(0, loop.shape[1], 1) as b:
                            self.replay(engine, body, a * loop.shape[1] + b, (a, b))
                self.running = outer
            elif kind == "if":
                _, flag, body = item
                self.flag = value = engine.value_load(flag, min_val=0, max_val=4096)
                with engine.If(value > 0):
                    self.replay(engine, body)

            elif kind == "either":
                _, yes, no, counter = item
                with engine.If(self.flag > 0):
                    yes(engine).then_inc(counter.sem, counter.step)
                with engine.Else():
                    no(engine).then_inc(counter.sem, counter.step)

    def either(self, yes, no, *marks, inc):
        self.wait(*marks, self.done.now())
        self.items.append(("either", yes, no, inc))
        return inc.raised(self.program.loop)

    running = None
    flag = None


class Program:

    def __init__(self, nc, ctx):
        self.nc, self.ctx, self.loop = nc, ctx, None
        self.pe, self.act, self.dve, self.pool, self.sp = (
            Lane(self, n, self.semaphore("done_" + n)) for n in ("pe", "act", "dve", "pool", "sp"))
        self.lanes = [self.pe, self.act, self.dve, self.pool, self.sp]
        self.bank_at = 0
        self.bank_free = [[] for _ in range(8)]

    def semaphore(self, name):
        return self.ctx.enter_context(self.nc.semaphore(name))

    def counter(self, name, step=16):
        return Counter(self.semaphore(name), step)

    def meet(self, *extra):
        marks = [lane.done.now() for lane in self.lanes[:4]]
        for lane in self.lanes[:4]:
            lane.wait(*marks, *extra)
        self.bank_free = [[] for _ in range(8)]

    def bank(self):
        b = self.bank_at
        self.bank_at = (b + 1) % 8
        self.pe.wait(*self.bank_free[b])
        self.bank_free[b] = []
        return b

    def loop_begin(self, *shape):
        assert self.loop is None
        self.loop = Loop(shape)
        self.outer = [lane.items for lane in self.lanes]
        for lane in self.lanes:
            lane.items, lane.waited = [], {}
            if lane.in_order:
                lane.last = Later()
                lane.wait(lane.last)
        return self.loop

    def loop_end(self):
        loop, self.loop = self.loop, None
        for lane in self.lanes:
            if lane.in_order:
                lane.last.set(lane.done.now())
        for c in loop.counters:
            loop.frames[c] = (c.base, c.n)
            c.per, c.n, c.loop = c.n, c.base + c.n * loop.trips, None
        for lane, items in zip(self.lanes, self.outer):
            body, lane.items, lane.waited = lane.items, items, {}
            if body:
                items.append(("loop", loop, body))

    def branch_begin(self, name):
        self.saved = [(lane.items, lane.done, lane.waited) for lane in self.lanes]
        for lane in self.lanes:
            lane.items, lane.waited = [], {}
            lane.done = Counter(self.semaphore(name + "_" + lane.name))

    def branch_end(self, flag):
        for lane, (items, done, waited) in zip(self.lanes, self.saved):
            body, lane.items, lane.done, lane.waited = lane.items, items, done, waited
            items.append(("if", flag, body))


class Ring:

    def __init__(self, g):
        self.g = g
        nc = g.nc
        self.slots = [g.ctx.enter_context(nc.sbuf_tensor(f"ring_{i}", [P, SLOT], F32)) for i in range(RING)]
        self.landed = [g.counter(f"landed_{i}") for i in range(RING)]
        self.free = g.counter("ring_free", 1)
        self.total, self.loop, self.here = 0, None, 0

    def load(self, *pieces):
        g = self.g
        if g.loop is not self.loop:
            self.total += self.here * (self.loop.trips if self.loop else 1)
            self.loop, self.here = g.loop, 0
        if g.loop is not None:
            self.free.enter(g.loop)
            assert self.free.base == self.total
        number = self.total + self.here
        slot = number % RING
        off = self.here + 1 - RING + (self.total if g.loop is None else 0)
        if number >= RING:
            g.sp.items.append(("wait", Mark(self.free, off, g.loop), 0))
        views = []
        for shape, first, source, *part in pieces:
            n = int(np.prod(shape))
            view = self.slots[slot][:, first:first + n]
            if len(shape) > 1:
                names = " ".join("abc"[:len(shape)])
                view = view.rearrange(f"p ({names}) -> p {names}", **dict(zip("abc", shape[:-1])))
            to = part[0](view) if part else view
            mark = g.sp.do(lambda e, i, v=to, s=source: e.dma_start(v, s(i)), inc=self.landed[slot])
            views.append(view)
        self.here += 1
        return views, mark


class Arena:

    def __init__(self, tensor, size):
        self.tensor, self.size, self.at = tensor, size, 0

    def take(self, *shape):
        n = int(np.prod(shape))
        view = self.tensor[:, self.at:self.at + n]
        self.at += n
        assert self.at <= self.size, (self.at, self.size)
        if len(shape) > 1:
            names = " ".join("abc"[:len(shape)])
            view = view.rearrange(f"p ({names}) -> p {names}", **dict(zip("abc", shape[:-1])))
        return view


def along(ap, n):
    return ap.unsqueeze(len(ap.shape)).broadcast_to([*ap.shape, n])


def across(ap, n, dim=1):
    shape = list(ap.shape)
    return ap.unsqueeze(dim).broadcast_to([*shape[:dim], n, *shape[dim:]])


class Kernel:
    def __init__(self, nc, ctx, a, stop=None):
        self.nc, self.a, self.stop = nc, a, stop
        self.g = g = Program(nc, ctx)
        self.pe, self.act, self.dve, self.pool, self.sp = g.lanes
        self.ring = Ring(g)

        def sb(name, shape, dt=F32):
            return ctx.enter_context(nc.sbuf_tensor(name, shape, dt))

        self.sb = sb
        self.psum = [ctx.enter_context(nc.psum_tensor(f"bank_{i}", [P, BANK], F32)) for i in range(8)]
        self.layout, ncol = column_layout()
        self.row_at, nrow = row_layout()
        self.cols, self.rows = sb("cols", [P, ncol]), sb("rows", [P, nrow])
        self.mats = sb("mats", [P, len(MATS), P])
        self.X = sb("residual", [P, KD, SEQ + CTX])
        self.A = sb("normed", [P, KD, SEQ + CTX])
        self.rstd = sb("rstd", [P, SEQ + CTX])
        self.mod = sb("mod", [P, 2, N_MOD * KD, 2])
        self.gain = sb("gain", [P, 2, 2, KD, 2])
        self.arena_size = 17600
        self.arena_tensor = sb("arena", [P, self.arena_size])
        self.loads = g.counter("loads")

    def col(self, name):
        at, shape = self.layout[name]
        view = self.cols[:, at:at + int(np.prod(shape))]
        if len(shape) > 1:
            names = " ".join("abc"[:len(shape)])
            view = view.rearrange(f"p ({names}) -> p {names}", **dict(zip("abc", shape[:-1])))
        return view

    def row(self, name):
        at, n = self.row_at[name]
        return self.rows[:, at:at + n]

    def mat(self, name):
        return self.mats[:, MATS.index(name), :]

    def stage(self):
        self.g.meet()
        return Arena(self.arena_tensor, self.arena_size)

    def fetch(self, out, source, *marks):
        return self.act.do(lambda e, i: e.dma_start(out, source), *marks, inc=self.loads)

    def mm(self, out, lhsT, rhs, start, stop, mark=False, inc=None, wait=(), shared=False):
        return self.pe.do(lambda e, i: e.matmul(out, lhsT, rhs, start=start, stop=stop, skip_group_check=shared),
                          *wait, inc=inc, mark=mark)

    def product(self, out, lhs, rhs, n_k, last=None, wait=()):
        self.pe.wait(*wait)
        for k in range(n_k):
            end = k == n_k - 1
            m = self.mm(out, lhs(k), rhs(k), k == 0, end, mark=end, inc=last if end else None)
        return m

    def turn(self, out, in_, rows=P, mark=False, wait=()):
        return self.pe.do(lambda e, i: e.transpose(out, in_, self.mats[0:rows, 0, 0:rows]), *wait, mark=mark)

    def tt(self, lane, out, a, b, op, *marks, chain=False):
        f = lane.chain if chain else lane.do
        return f(lambda e, i: e.tensor_tensor(out, a, b, op), *marks)

    def ts(self, lane, out, a, s1, s2, op0, op1, *marks, chain=False):
        f = lane.chain if chain else lane.do
        if s2 is None:
            return f(lambda e, i: e.tensor_scalar(out, a, s1, None, op0), *marks)
        return f(lambda e, i: e.tensor_scalar(out, a, s1, s2, op0, op1), *marks)

    def stt(self, out, a, s, b, op0, op1, *marks, chain=False):
        f = self.dve.chain if chain else self.dve.do
        return f(lambda e, i: e.scalar_tensor_tensor(out, a, s, b, op0, op1), *marks)

    def fn(self, out, a, func, *marks, bias=0.0, scale=1.0, total=None, chain=False):
        f = self.act.chain if chain else self.act.do
        return f(lambda e, i: e.activation(out, a, func, bias=bias, scale=scale, accum_out=total), *marks)

    def copy(self, lane, out, a, *marks, chain=False):
        f = lane.chain if chain else lane.do
        if lane is self.act:
            return f(lambda e, i: e.activation(out, a, ACT.Copy), *marks)
        return f(lambda e, i: e.tensor_copy(out, a), *marks)

    def mean_square(self, src, n_k, T, width, eps, scratch, *marks):
        g, b = self.g, self.g.bank()
        out = self.psum[b][:, 0:T]
        ones = self.mat(f"ones_{width}")
        for k in range(n_k):
            m = self.fn(scratch[:, k, 0:T], src[:, k, 0:T], ACT.Square, *marks)
            end = self.mm(out, ones, scratch[:, k, 0:T], k == 0, k == n_k - 1, mark=k == n_k - 1, wait=(m,))
        m = self.ts(self.dve, self.rstd[:, 0:T], out, eps, None, ALU.add, None, end)
        g.bank_free[b] = [m]
        m = self.fn(self.rstd[:, 0:T], self.rstd[:, 0:T], ACT.Sqrt, m)
        return self.dve.do(lambda e, i: e.reciprocal(self.rstd[:, 0:T], self.rstd[:, 0:T]), m)

    def scaled(self, dst, src, gain, T, n_k, stat):
        for k in range(n_k):
            m = self.stt(dst[:, k, 0:T], src[:, k, 0:T], gain[:, k:k + 1], self.rstd[:, 0:T],
                         ALU.mult, ALU.mult, stat)
        return m

    def modulated(self, layer, which, T):
        stat = self.mean_square(self.X, KD, T, D, NORM_EPS, self.A)
        stat_pe = self.pe.done.now()
        shift = 0 if which == 0 else 3
        marks = []
        for k in range(KD):
            for c in range(T // SEQ):
                cols = slice(c * SEQ, (c + 1) * SEQ)
                m = self.stt(self.A[:, k, cols], self.X[:, k, cols], self.gain[:, layer, which, k, c:c + 1],
                             self.rstd[:, cols], ALU.mult, ALU.mult, stat, stat_pe)
                marks.append(self.fn(self.A[:, k, cols], self.A[:, k, cols], ACT.Identity, m,
                                     bias=self.mod[:, layer, shift * KD + k, c:c + 1]))
        return marks[-1]

    def simple_norm(self, gain, dst=None, T=SEQ):
        dst = self.A if dst is None else dst
        stat = self.mean_square(self.X, KD, T, D, NORM_EPS, dst)
        return self.scaled(dst, self.X, gain, T, KD, stat)

    def weights(self, source, n_k, first, n):
        w = source.rearrange("(k p) n -> p k n", p=P)[:, :, first:first + n]
        (view,), mark = self.ring.load(((n_k, n), 0, lambda i: w))
        return view, mark

    def linear(self, source, n_k, n_out, rhs, T, evac, *marks, width=512):
        for first in range(0, n_out, width):
            w, landed = self.weights(source, n_k, first, min(width, n_out - first))
            tiles = min(width, n_out - first) // P
            for t in range(tiles):
                b = self.g.bank()
                out = self.psum[b][:, 0:T]
                m = self.product(out, lambda k: w[:, k, t * P:(t + 1) * P], rhs, n_k,
                                 last=self.ring.free if t == tiles - 1 else None, wait=(landed, *marks))
                self.g.bank_free[b] = [evac(first // P + t, out, m)]

    def add_gated(self, layer, j):
        def evac(m, out, mark):
            for c in range(out.shape[1] // SEQ):
                cols = slice(c * SEQ, (c + 1) * SEQ)
                last = self.stt(self.X[:, m, cols], out[:, cols], self.mod[:, layer, j * KD + m, c:c + 1],
                                self.X[:, m, cols], ALU.mult, ALU.add, mark)
            return last
        return evac

    def add_plain(self, m, out, mark):
        return self.tt(self.dve, self.X[:, m, 0:SEQ], out, self.X[:, m, 0:SEQ], ALU.add, mark)

    def start(self):
        a = self.a
        self.g.loaded = self.fetch(self.cols[:, :], a["cols"])
        self.fetch(self.rows[:, :], a["rows"].partition_broadcast(P) if len(a["rows"].shape) == 1
                   else a["rows"].broadcast_to([P, a["rows"].shape[1]]))
        self.fetch(self.mats[:, :, :], a["mats"])
        self.fetch(self.X[:, :, 0:SEQ], a["xT"].rearrange("(k p) t -> p k t", p=P))
        m = self.fetch(self.X[:, :, SEQ:SEQ + CTX], a["ctxT"].rearrange("(k p) t -> p k t", p=P))
        for lane in (self.pe, self.act, self.dve, self.pool):
            lane.wait(m)
        cond = self.col("cond")
        self.silu_cond = self.sb("silu_cond", [P, KD, 2])
        self.cond_mark = self.fn(self.silu_cond[:, :, :], cond, ACT.Silu)

    def modulation(self, layer):
        b = self.g.bank()
        n_tiles = N_MOD * KD
        out = self.psum[b][:, 0:2 * n_tiles].rearrange("p (m c) -> p m c", c=2)
        for first in range(0, N_MOD * D, 512):
            w, landed = self.weights(self.a["w_mod"][layer], KD, first, 512)
            for t in range(4):
                m = self.product(out[:, first // P + t, :], lambda k: w[:, k, t * P:(t + 1) * P],
                                 lambda k: self.silu_cond[:, k, :], KD, last=self.ring.free if t == 3 else None,
                                 wait=(landed, self.cond_mark))
        mod = self.mod[:, layer, :, :]
        m = self.tt(self.dve, mod, out, along(self.col("b_mod")[:, layer, :], 2), ALU.add, m)
        self.g.bank_free[b] = [m]
        for which, (j, norm) in enumerate(((1, "norm_mix"), (4, "norm_ffn"))):
            self.stt(self.gain[:, layer, which, :, :], mod[:, j * KD:(j + 1) * KD, :], 1.0,
                     along(self.col(norm)[:, layer, :], 2), ALU.add, ALU.mult, m)
        self.act.wait(m)

    def mla(self):
        g, a, T = self.g, self.a, SEQ + CTX
        ar = self.stage()
        CQ = ar.take(4, T)
        ar.at = 0
        score_buf = [ar.take(BANK) for _ in range(4)]
        CKV, KPE, QN, QR = ar.take(2, T), ar.take(2, T), ar.take(MLA_HEADS, T), ar.take(MLA_HEADS // 2, T)
        V, KN, PT = ar.take(4, MLA_HEADS * P), ar.take(2, T), ar.take(4, SEQ)
        PTC = ar.take(2, CTX)
        cos, sin, rot = ar.take(SEQ), ar.take(SEQ), ar.take(P)
        small = ar.take(3, 8)
        raw = KN[:, 0, :]
        tables = self.fetch(cos, a["tables"][:, 0:SEQ], self.act.done.now(), self.dve.done.now(), self.pe.done.now())
        self.fetch(sin, a["tables"][:, SEQ:2 * SEQ])
        tables = self.fetch(rot, a["tables"][:, 2 * SEQ:2 * SEQ + P])
        scale = float(MLA_NOPE + MLA_ROPE) ** -0.5
        zero = self.pool.do(lambda e, i: e.memset(KPE, 0.0))
        ready = self.modulated(0, 0, T)
        rhs = lambda k: self.A[:, k, :]

        self.linear(a["mla_w_dq"][0], KD, MLA_Q_LORA, rhs, T,
                    lambda m, out, mark: self.copy(self.dve, CQ[:, m, :], out, mark), ready)
        wd = a["mla_w_dkv"][0].rearrange("(k p) n -> p k n", p=P)
        n_kv = MLA_KV_LORA
        pe_cols = lambda i: wd[:, :, n_kv:n_kv + MLA_ROPE]
        (w, w_pe, _), landed = self.ring.load(
            ((KD, n_kv), 0, lambda i: wd[:, :, 0:n_kv]),
            ((KD, P), KD * n_kv, pe_cols, lambda v: v[:, :, 0:MLA_ROPE]),
            ((KD, P), KD * n_kv, pe_cols, lambda v: v[:, :, MLA_ROPE:P]))
        for m in range(3):
            b = g.bank()
            out = self.psum[b][:, :]
            if m < 2:
                end = self.product(out, lambda k: w[:, k, m * P:(m + 1) * P], rhs, KD, wait=(landed, ready))
                g.bank_free[b] = [self.copy(self.dve, CKV[:, m, :], out, end)]
            else:
                end = self.product(out, lambda k: w_pe[:, k, :], rhs, KD, last=self.ring.free)
                k_raw = self.copy(self.act, raw, out, end)
                g.bank_free[b] = [k_raw]

        kv_done, squares_read = self.dve.done.now(), None
        for buf, n_k, gain in ((CQ, 4, "g_q"), (CKV, 2, "g_kv")):
            stat = self.mean_square(buf, n_k, T, n_k * P, NORM_EPS, QN, kv_done, squares_read)
            done = self.scaled(buf, buf, self.col(gain), T, n_k, stat)
            squares_read = self.pe.done.now()
        self.act.wait(squares_read)
        self.dve.wait(squares_read)

        def rotate(src, mark):
            b = g.bank()
            out = self.psum[b][:, 0:SEQ]
            end = self.mm(out, rot, src[:, 0:SEQ], True, True, mark=True, wait=(mark, tables))
            m = self.tt(self.dve, turned[:, :], out, sin, ALU.mult, end, chain=True)
            g.bank_free[b] = [m]
            m2 = self.tt(self.dve, src[:, 0:SEQ], src[:, 0:SEQ], cos, ALU.mult, end)
            return self.tt(self.dve, src[:, 0:SEQ], src[:, 0:SEQ], turned[:, :], ALU.add, chain=True)

        turned = self.rstd[:, 0:SEQ]
        k_rot = rotate(raw, k_raw)
        half = MLA_ROPE
        self.copy(self.dve, KPE[0:half, 0, :], raw[0:half, :], zero, k_rot)
        k_pe = self.copy(self.dve, KPE[half:P, 1, :], raw[half:P, :])

        hw = MLA_NOPE + MLA_ROPE
        wq = a["mla_w_uq"][0].rearrange("(k p) (h c) -> p k h c", p=P, c=hw)
        q_marks = []
        for c in range(2):
            pieces = []
            heads = slice(4 * c, 4 * c + 4)
            for k in range(4):
                pieces.append(((4, 768), 0, lambda i, k=k, heads=heads: wq[:, k, heads, 0:MLA_NOPE],
                               lambda v, k=k: v[:, k, 0:512].rearrange("p (h c) -> p h c", h=4)))
                pieces.append(((4, 768), 0, lambda i, k=k, heads=heads: wq[:, k, heads, MLA_NOPE:hw],
                               lambda v, k=k: v[:, k, 512:768].rearrange("p (h c) -> p h c", h=4)))
            (w, *_), landed = self.ring.load(*pieces)
            for t in range(6):
                b = g.bank()
                out = self.psum[b][:, :]
                end = self.product(out, lambda k: w[:, k, t * P:(t + 1) * P], lambda k: CQ[:, k, :], 4,
                                   last=self.ring.free if t == 5 else None, wait=(landed, done))
                dst = QN[:, 4 * c + t, :] if t < 4 else QR[:, 2 * c + t - 4, :]
                m = self.fn(dst, out, ACT.Copy, end, scale=scale)
                g.bank_free[b] = [m]
                if t >= 4:
                    m = rotate(dst, m)
                q_marks.append(m)
        self.pe.wait(self.act.done.now(), self.dve.done.now())

        wkv = a["mla_w_ukv"][0].rearrange("(k p) n -> p k n", p=P)
        (w,), landed = self.ring.load(((2, 2 * MLA_HEADS * P), 0, lambda i: wkv))
        w_heads = w.rearrange("p k (h j c) -> p k h j c", j=2, c=P)
        for t in range(T // P):
            for n in range(2):
                b = g.bank()
                end = self.product(self.psum[b][:, :], lambda k: CKV[:, k, t * P:(t + 1) * P],
                                   lambda k: w_heads[:, k, 4 * n:4 * n + 4, 1, :], 2, wait=(landed,))
                v_mark = self.copy(self.act, V[:, t, n * 512:(n + 1) * 512], self.psum[b][:, :], end)
                g.bank_free[b] = [v_mark]

        OT = self.A
        score_free = [None] * 4
        kn_free = [k_pe, k_pe]
        pt_free = [None, None]

        def scores(h):
            b = g.bank()
            kn = KN[:, h % 2, :]
            end = self.product(self.psum[b][:, :], lambda k: w_heads[:, k, h, 0, :], lambda k: CKV[:, k, :], 2,
                               last=self.ring.free if h == MLA_HEADS - 1 else None)
            m = self.copy(self.dve, kn, self.psum[b][:, :], end, kn_free[h % 2])
            g.bank_free[b] = [m]
            self.pe.wait(m)
            probs = []
            for q in range(T // P):
                lat = q < SEQ // P
                keys = slice(0, T) if lat else slice(SEQ, T)
                n = T if lat else CTX
                if q != 3:
                    b = g.bank()
                at = 0 if q != 3 else CTX
                out = self.psum[b][:, at:at + n]
                self.mm(out, QN[:, h, q * P:(q + 1) * P], kn[:, keys], True, False)
                end = self.mm(out, QR[:, h // 2, q * P:(q + 1) * P], KPE[:, h % 2, keys], False, True, mark=True)
                probs.append((q, b, out, n, end))
            kn_free[h % 2] = end
            return probs

        def softmax(probs):
            marks = []
            for q, b, out, n, e1 in probs:
                e1 = e1 if q < 2 else probs[3][4]
                buf = score_buf[q][:, 0:n]
                top, total, inv = small[:, 0, q:q + 1], small[:, 1, q:q + 1], small[:, 2, q:q + 1]
                m = self.dve.do(lambda e, i, o=top, s=out: e.tensor_reduce(o, s, AX.X, ALU.max, negate=True),
                                e1, self.act.done.now())
                m = self.fn(buf, out, ACT.Exp, m, score_free[q], bias=top, total=total)
                g.bank_free[b] = [m]
                m = self.dve.do(lambda e, i, o=inv, s=total: e.reciprocal(o, s), m)
                marks.append(self.ts(self.dve, buf, buf, inv, None, ALU.mult, None, chain=True))
            return marks

        def values(h, marks):
            for q in range(2):
                b = g.bank()
                for k in range(4):
                    end = self.turn(self.psum[b][:, k * P:(k + 1) * P], score_buf[q][:, k * P:(k + 1) * P],
                                    mark=k == 3, wait=(marks[q],))
                score_free[q] = end
                m = self.copy(self.act, PT[:, :, q * P:(q + 1) * P],
                              self.psum[b][:, :].rearrange("p (k q) -> p k q", k=4), end, pt_free[0])
                g.bank_free[b] = [m]
            b = g.bank()
            for q in range(2):
                for k in range(2):
                    end = self.turn(self.psum[b][:, (2 * q + k) * P:(2 * q + k + 1) * P],
                                    score_buf[2 + q][:, k * P:(k + 1) * P], mark=k == 1, wait=(marks[2 + q],))
                score_free[2 + q] = end
            mc = self.copy(self.act, PTC.rearrange("p k (q c) -> p q k c", q=2),
                           self.psum[b][:, :].rearrange("p (q k c) -> p q k c", q=2, k=2), end, pt_free[1])
            g.bank_free[b] = [mc]
            b = g.bank()
            for k in range(4):
                self.mm(self.psum[b][:, 0:SEQ], V[:, k, h * P:(h + 1) * P], PT[:, k, :], k == 0, k == 3,
                        wait=(m, v_mark))
            for k in range(2):
                end = self.mm(self.psum[b][:, SEQ:T], V[:, 2 + k, h * P:(h + 1) * P], PTC[:, k, :], k == 0, k == 1,
                              mark=k == 1, wait=(mc,))
            pt_free[0] = pt_free[1] = end
            m = self.copy(self.dve, OT[:, h, :], self.psum[b][:, :], end)
            g.bank_free[b] = [m]
            return m

        marks = softmax(scores(0))
        for h in range(MLA_HEADS):
            after = scores(h + 1) if h + 1 < MLA_HEADS else None
            out_mark = values(h, marks)
            marks = softmax(after) if after else None
        self.linear(a["mla_w_o"][0], KD, D, lambda k: OT[:, k, :], T, self.add_gated(0, 2), out_mark)

    def conv_mixer(self):
        g, a, T = self.g, self.a, SEQ
        ar = self.stage()
        B, C, V, Z = ar.take(KD, T), ar.take(KD, T), ar.take(2, T + 2), ar.take(KD, T)
        pads = self.pool.do(lambda e, i: e.memset(V, 0.0))
        ready = self.modulated(1, 0, T)
        taps = self.col("conv_w")
        state = {0: pads, 1: pads}

        def evac(m, out, mark):
            part, m = divmod(m, KD)
            if part < 2:
                m = self.copy(self.act, (B, C)[part][:, m, :], out, mark)
                state["bc"] = m
                return m
            v = V[:, m % 2, :]
            end = self.tt(self.dve, v[:, 1:T + 1], out, C[:, m, :], ALU.mult, mark, state["bc"], state[m % 2])
            z = Z[:, m, :]
            self.ts(self.dve, z, v[:, 0:T], taps[:, m, 0:1], None, ALU.mult, None, chain=True)
            self.stt(z, v[:, 1:T + 1], taps[:, m, 1:2], z, ALU.mult, ALU.add, chain=True)
            self.stt(z, v[:, 2:T + 2], taps[:, m, 2:3], z, ALU.mult, ALU.add, chain=True)
            state["z"] = self.tt(self.dve, z, z, B[:, m, :], ALU.mult, chain=True)
            state[m % 2] = state["z"]
            return end

        self.linear(a["conv_w_in"][0], KD, 3 * D, lambda k: self.A[:, k, 0:T], T, evac, ready)
        self.linear(a["conv_w_out"][0], KD, D, lambda k: Z[:, k, :], T, self.add_gated(1, 2), state["z"])

    def first_max(self, score, order, n, tmp, out):
        top, eq = tmp
        nt = score.shape[1]
        self.dve.chain(lambda e, i: e.tensor_reduce(top, score, AX.X, ALU.max))
        self.tt(self.dve, eq, score, along(top, n), ALU.is_equal, chain=True)
        self.tt(self.dve, eq, eq, across(order, nt), ALU.mult, chain=True)
        self.dve.chain(lambda e, i: e.tensor_reduce(top, eq, AX.X, ALU.max))
        return self.tt(self.dve, out, eq, along(top, n), ALU.is_equal, chain=True)

    def moe(self, layer, T, cap):
        g, a, ring = self.g, self.a, self.ring
        NT = T // P
        n_blocks = -(-T // cap)
        f_rows = self.nc.dram_tensor(f"f_rows_{layer}", [T, D], F32, kind="Internal").ap()
        y_rows = self.nc.dram_tensor(f"y_rows_{layer}", [n_blocks * EXPERTS * cap, D], F32, kind="Internal").ap()
        s_yout = [g.counter(f"y_out_{layer}_{j}") for j in range(2)]
        s_gather = [g.counter(f"gather_{layer}_{j}") for j in range(2)]
        s_back = [g.counter(f"back_{layer}_{j}") for j in range(2)]

        ar = self.stage()
        index_i = ar.take(n_blocks * EXPERTS + 2).bitcast(I32)
        index_u = ar.take(2)
        weight = [ar.take(NT) for _ in range(2)]
        dest = [ar.take(NT) for _ in range(2)]
        flag = ar.take(1)
        pos = [ar.take(NT) for _ in range(2)]
        chosen = ar.take(2, NT * EXPERTS)
        work = ar.at
        W = ar.take(KD, GROUPS + EXPERTS)
        router = self.fetch(W[:, :, 0:GROUPS], a["moe_w_group"][layer].rearrange("(k p) n -> p k n", p=P),
                            *[l.done.now() for l in g.lanes[:4]])
        router = self.fetch(W[:, :, GROUPS:], a["moe_w_expert"][layer].rearrange("(k p) n -> p k n", p=P))
        ready = self.modulated(layer, 1, T)

        n_log = GROUPS + EXPERTS
        b = g.bank()
        for t in range(NT):
            end = self.product(self.psum[b][:, t * n_log:(t + 1) * n_log], lambda k: self.A[:, k, t * P:(t + 1) * P],
                               lambda k: W[:, k, :], KD, wait=(router, ready))
        logits = ar.take(NT, n_log)
        m_log = self.copy(self.dve, logits, self.psum[b][:, 0:NT * n_log].rearrange("p (t n) -> p t n", n=n_log), end)
        g.bank_free[b] = [m_log]

        rows = ar.take(2, D)
        sent = []
        for t in range(NT):
            for half in range(2):
                b = g.bank()
                for j in range(4):
                    end = self.turn(self.psum[b][:, j * P:(j + 1) * P],
                                    self.A[:, 4 * half + j, t * P:(t + 1) * P], mark=j == 3)
                at = rows[:, t % 2, half * 512:(half + 1) * 512]
                m = self.copy(self.act, at, self.psum[b][:, :], end, sent[t - 2] if t >= 2 else None)
                g.bank_free[b] = [m]
            sent.append(self.act.do(lambda e, i, t=t: e.dma_start(f_rows[t * P:(t + 1) * P, :], rows[:, t % 2, :]),
                                    m, inc=s_yout[t % 2]))
        rows_out = sent[-2:]

        bias = self.row(f"route_bias_{layer}")
        dve, act = self.dve, self.act

        def softmax(x, n, top, total):
            dve.chain(lambda e, i: e.tensor_reduce(top, x, AX.X, ALU.max))
            m = self.tt(dve, x, x, along(top, n), ALU.subtract, chain=True)
            m = self.fn(x, x, ACT.Exp, m)
            dve.chain(lambda e, i: e.tensor_reduce(total, x, AX.X, ALU.add), m)
            dve.chain(lambda e, i: e.reciprocal(total, total))
            self.tt(dve, x, x, along(total, n), ALU.mult, chain=True)

        def reduced(out, x):
            return dve.chain(lambda e, i: e.tensor_reduce(out, x, AX.X, ALU.add))

        gp, gs, g_hot = logits[:, :, 0:GROUPS], ar.take(NT, GROUPS), ar.take(NT, GROUPS)
        el = logits[:, :, GROUPS:].rearrange("p t (g e) -> p t g e", g=GROUPS)
        top, total, g_w = ar.take(NT), ar.take(NT), ar.take(NT)
        softmax(gp, GROUPS, top, total)
        self.tt(dve, gs, gp, across(bias[:, 0:GROUPS], NT), ALU.add, chain=True)
        eq4 = ar.take(NT, GROUPS)
        self.first_max(gs, self.row("first_4"), GROUPS, (top, eq4), g_hot)
        self.tt(dve, gs, gp, g_hot, ALU.mult, chain=True)
        reduced(g_w, gs)

        picked = ar.take(NT, EXPERTS).rearrange("p t (g e) -> p t g e", g=GROUPS)
        ep, e_bias, e_sc, eq8 = (ar.take(NT, PER_GROUP) for _ in range(4))
        hot = [ar.take(NT, PER_GROUP) for _ in range(2)]
        wide_hot = along(g_hot, PER_GROUP)
        e_rows = across(bias[:, GROUPS:].rearrange("p (g e) -> p g e", g=GROUPS), NT)
        for src, out in ((el, ep), (e_rows, e_bias)):
            self.tt(dve, picked, src, wide_hot, ALU.mult, chain=True)
            reduced(out, picked.rearrange("p t g e -> p t e g"))
        softmax(ep, PER_GROUP, top, total)
        self.tt(dve, e_sc, ep, e_bias, ALU.add, chain=True)
        self.first_max(e_sc, self.row("first_8"), PER_GROUP, (top, eq8), hot[0])
        self.ts(dve, eq8, hot[0], -1.0, 1.0, ALU.mult, ALU.add, chain=True)
        self.tt(dve, e_sc, e_sc, eq8, ALU.mult, chain=True)
        self.stt(e_sc, hot[0], -BIG, e_sc, ALU.mult, ALU.add, chain=True)
        self.first_max(e_sc, self.row("first_8"), PER_GROUP, (top, eq8), hot[1])
        for j in range(2):
            self.tt(dve, eq8, ep, hot[j], ALU.mult, chain=True)
            reduced(weight[j], eq8)
        self.tt(dve, total, weight[0], weight[1], ALU.add, chain=True)
        dve.chain(lambda e, i: e.reciprocal(total, total))
        self.tt(dve, total, total, g_w, ALU.mult, chain=True)
        for j in range(2):
            self.tt(dve, weight[j], weight[j], total, ALU.mult, chain=True)
        for j in range(2):
            out = chosen[:, j, :].rearrange("p (t g e) -> p t g e", t=NT, g=GROUPS)
            self.tt(dve, out, wide_hot, across(hot[j], GROUPS, 2), ALU.mult, chain=True)
        both = ar.take(NT, EXPERTS)
        flat = both.rearrange("p t e -> p (t e)")
        m_both = self.tt(dve, flat, chosen[:, 0, :], chosen[:, 1, :], ALU.add, chain=True)

        b = g.bank()
        for t in range(NT):
            out = self.psum[b][:, t * EXPERTS:(t + 1) * EXPERTS]
            for s in range(t):
                self.mm(out, self.mat("ones"), both[:, s, :], s == 0, False, wait=(m_both,))
            self.mm(out, self.mat("before"), both[:, t, :], t == 0, True, wait=(m_both,))
        out = self.psum[b][:, NT * EXPERTS:(NT + 1) * EXPERTS]
        for t in range(NT):
            end = self.mm(out, self.mat("ones"), both[:, t, :], t == 0, t == NT - 1, mark=t == NT - 1)
        ranks, loads = ar.take(NT, EXPERTS), ar.take(EXPERTS)
        self.copy(dve, ranks.rearrange("p t e -> p (t e)"), self.psum[b][:, 0:NT * EXPERTS], end)
        m = self.copy(dve, loads, out)
        g.bank_free[b] = [m]
        most = ar.take(1)
        dve.chain(lambda e, i: e.tensor_reduce(most, loads, AX.X, ALU.max))
        self.ts(dve, most, most, -float(cap), 0.0, ALU.add, ALU.max, chain=True)
        flag_mark = self.copy(dve, flag.bitcast(I32), most, chain=True)
        tmp = ar.take(NT, EXPERTS)
        step = ar.take(NT)
        count = self.row("count")
        for j in range(2):
            mine = chosen[:, j, :].rearrange("p (t e) -> p t e", t=NT)
            self.tt(dve, tmp, ranks, mine, ALU.mult, chain=True)
            reduced(pos[j], tmp)
            self.tt(dve, tmp, mine, across(count[:, 0:EXPERTS], NT), ALU.mult, chain=True)
            reduced(step, tmp)
            self.stt(dest[j], step, float(cap), pos[j], ALU.mult, ALU.add, chain=True)
            for n in range(1, n_blocks):
                self.ts(dve, step, pos[j], float(n * cap), float((EXPERTS - 1) * cap), ALU.is_ge, ALU.mult, chain=True)
                self.tt(dve, dest[j], dest[j], step, ALU.add, chain=True)
            self.copy(dve, dest[j].bitcast(I32), dest[j], chain=True)

        slot = ar.take(2, NT * cap)
        named = ar.take(2, NT * EXPERTS)
        for j in range(2):
            for t in range(NT):
                mine = chosen[:, j, t * EXPERTS:(t + 1) * EXPERTS]
                self.ts(dve, named[:, j, t * EXPERTS:(t + 1) * EXPERTS], mine, self.col("token")[:, t:t + 1], None,
                        ALU.mult, None)

        def index_block(n):
            for j in range(2):
                for t in range(NT):
                    m = self.ts(dve, slot[:, j, t * cap:(t + 1) * cap], count[:, 0:cap], float(n * cap),
                                pos[j][:, t:t + 1], ALU.add, ALU.is_equal, chain=True)
            b = g.bank()
            out = self.psum[b][0:cap, 0:EXPERTS]
            for j in range(2):
                for t in range(NT):
                    last = j == 1 and t == NT - 1
                    end = self.mm(out, slot[:, j, t * cap:(t + 1) * cap], named[:, j, t * EXPERTS:(t + 1) * EXPERTS],
                                  j == 0 and t == 0, last, mark=last, wait=(m,))
            m = self.copy(dve, index_i[0:cap, n * EXPERTS:(n + 1) * EXPERTS], out, end)
            g.bank_free[b] = [m]
            return m
        zeroed = self.pool.do(lambda e, i: e.memset(index_i, 0))
        self.dve.wait(zeroed)
        index_mark = index_block(0)

        keep = ar.at
        xe, xt = ar.take(2, D), ar.take(2, KD * cap)
        ht, yb, act_h = ar.take(2, KF * cap), ar.take(2, D), ar.take(KF * cap)
        gate, up = (a[n][layer].rearrange("x (k p) n -> x p k n", p=P) for n in ("moe_w_gate", "moe_w_up"))
        down = a["moe_w_down"][layer].rearrange("x (k p) n -> x p k n", p=P)
        index_buf = index_u.bitcast(I32)
        offset = bass.IndirectOffsetOnAxis
        per_bank = min(KD, BANK // cap)
        n_turned = -(-KD // per_bank)

        def gather(j, column, counter, *marks):
            m = self.pool.do(lambda e, i: e.tensor_copy(index_buf[0:cap, j:j + 1], index_i[0:cap, column(i)]), *marks)
            self.pool.items.append(("op", lambda e, i: e.drain(), None))
            return self.pool.do(lambda e, i: e.indirect_dma_start(
                out=xe[0:cap, j, :], out_offset=None, in_=f_rows,
                in_offset=offset(ap=index_buf[0:cap, j:j + 1].bitcast(U32), axis=0)), inc=counter, loose=True)

        def turned(j, gathered, banks, *marks):
            self.pe.wait(*marks)
            for n, b in enumerate(banks):
                lo, hi = n * per_bank, min(KD, (n + 1) * per_bank)
                for k in range(lo, hi):
                    end = self.turn(self.psum[b][:, (k - lo) * cap:(k - lo + 1) * cap],
                                    xe[0:cap, j, k * P:(k + 1) * P], rows=cap, mark=k == hi - 1, wait=(gathered,))
                m = self.copy(dve, xt[:, j, lo * cap:hi * cap], self.psum[b][:, 0:(hi - lo) * cap], end)
            return m, end

        def expert(j, x_ready, w, landed, frees, between, h_before, y_before, stored):
            bg, bu, b0, b1 = 4, 5, 6, 7
            self.pe.wait(x_ready, h_before)
            ends = []
            for which, b in ((0, bg), (1, bu)):
                for n in range(KF):
                    ends.append(self.product(self.psum[b][:, n * cap:(n + 1) * cap],
                                lambda k: w[which][:, k, n * P:(n + 1) * P],
                                lambda k: xt[:, j, k * cap:(k + 1) * cap], KD,
                                last=frees if n == KF - 1 else None, wait=(landed[which],)))
            hs = ht[:, j, :]
            m = self.fn(act_h, self.psum[bg][:, 0:KF * cap], ACT.Silu, ends[KF - 1], h_before)
            h_ready = self.tt(dve, hs, act_h, self.psum[bu][:, 0:KF * cap], ALU.mult, m, ends[-1])
            between()
            self.pe.wait(landed[2], h_ready, *y_before)
            out = []
            for n, (b, lane) in enumerate(((b0, dve), (b1, act))):
                end = self.product(self.psum[b][0:cap, :], lambda k: hs[:, k * cap:(k + 1) * cap],
                                   lambda k: w[2][:, k, n * 512:(n + 1) * 512], KF, last=frees if n else None)
                out.append(self.copy(lane, yb[0:cap, j, n * 512:(n + 1) * 512], self.psum[b][0:cap, :], end, stored))
            return h_ready, tuple(out)

        def store(j, row, counter, *marks):
            return act.do(lambda e, i: e.dma_start(y_rows[row(i), :], yb[0:cap, j, :]), *marks, inc=counter)

        tb = [[0, 1][:n_turned], [2, 3][:n_turned]]
        g.meet(*rows_out)
        gathered = gather(0, lambda i: slice(0, 1), s_gather[0], index_mark)
        turned(0, gathered, tb[0])
        gather(1, lambda i: slice(1, 2), s_gather[1])
        g.meet()

        g.loop_begin(EXPERTS // 2)
        carried = {n: Later() for n in ("gathered1", "x_ready0", "turned0", "h1", "y1a", "y1b", "store0", "store1")}
        wait_for = [dict(h_before=carried["h1"], y_before=(carried["y1a"], carried["y1b"]), stored=carried["store0"]),
                    None]
        x_ready = [carried["x_ready0"], None]
        gathered0 = gather(0, lambda i: bass.ds(i[0] * 2 + 2, 1), s_gather[0], carried["turned0"])
        for j in range(2):
            pieces, landed = [], []
            for view, shape in ((gate, (KD, FF)), (up, (KD, FF)), (down, (KF, D))):
                (v,), mark = ring.load((shape, 0, lambda i, view=view, j=j:
                                        view[bass.ds(i[0] * 2 + j, 1)].rearrange("x p k n -> p (x k) n")))
                pieces.append(v)
                landed.append(mark)

            def between(j=j):
                if j == 0:
                    x_ready[1], _ = turned(1, carried["gathered1"], tb[1])
                else:
                    m, end = turned(0, gathered0, tb[0])
                    carried["x_ready0"].set(m)
                    carried["turned0"].set(end)

            h, y = expert(j, x_ready[j], pieces, landed, ring.free, between, **wait_for[j])
            stored = store(j, lambda i, j=j: bass.ds(i[0] * (2 * cap) + j * cap, cap), s_yout[j], *y)
            carried[f"store{j}"].set(stored)
            if j == 0:
                carried["gathered1"].set(gather(1, lambda i: bass.ds(i[0] * 2 + 3, 1), s_gather[1], x_ready[1]))
                wait_for[1] = dict(h_before=h, y_before=y, stored=carried["store1"])
            else:
                carried["h1"].set(h)
                carried["y1a"].set(y[0])
                carried["y1b"].set(y[1])
        g.loop_end()
        y_out = [s_yout[0].now(), s_yout[1].now()]
        g.meet(*y_out, s_gather[0].now(), s_gather[1].now())

        all_free = ring.free.now()
        before = [lane.done.now() for lane in g.lanes[:4]]
        name = f"more_{layer}"
        for lane in g.lanes:
            lane.wait(flag_mark)
        g.branch_begin(name)
        banks_before, g.bank_free = g.bank_free, [[] for _ in range(8)]
        self.sp.wait(all_free, *before)
        for n in range(1, n_blocks):
            index_block(n)
        self.copy(act, act_h[:, 0:1], self.col("token")[:, 0:1])
        self.pool.do(lambda e, i: e.memset(xe, 0.0))
        marks = [lane.done.now() for lane in g.lanes[:4]]
        for lane in g.lanes:
            lane.wait(*marks)
        m_landed, m_gather, m_out = (g.counter(f"{name}_{n}") for n in ("landed", "gathered", "y_out"))
        g.loop_begin(n_blocks - 1, EXPERTS)
        products_before = Later()
        self.sp.wait(products_before)
        linear_index = lambda i: i[0] * EXPERTS + i[1]
        views = []
        for slot_no, (view, shape) in enumerate(((gate, (KD, FF)), (up, (KD, FF)), (down, (KF, D)))):
            v = ring.slots[slot_no][:, :].rearrange("p (k n) -> p k n", k=shape[0])
            landed = self.sp.do(lambda e, i, v=v, view=view: e.dma_start(
                v, view[bass.ds(i[1], 1)].rearrange("x p k n -> p (x k) n")), inc=m_landed)
            views.append(v)
        gathered = gather(0, lambda i: bass.ds(linear_index(i) + EXPERTS, 1), m_gather)
        x_mark, _ = turned(0, gathered, tb[0])
        h, y = expert(0, x_mark, views, [landed] * 3, None, lambda: None, None, (), None)
        out = store(0, lambda i: bass.ds(linear_index(i) * cap + EXPERTS * cap, cap), m_out, *y)
        products_before.set(self.pe.done.now())
        marks = [lane.done.now() for lane in g.lanes[:4]]
        for lane in g.lanes[:4]:
            lane.wait(*marks, out, gathered)
        g.loop_end()
        g.bank_free = banks_before
        g.branch_end(flag[0:1, 0:1].bitcast(I32))

        ar.at = keep
        ga = [[ar.take(D) for _ in range(2)] for _ in range(2)]
        self.pool.wait(*y_out)
        free = [None, None]
        for t in range(NT):
            pair = ga[t % 2]
            for j in range(2):
                def fetch_rows(e, source, j=j, t=t, o=pair[j]):
                    return e.indirect_dma_start(out=o, out_offset=None, in_=source, in_offset=offset(
                        ap=dest[j][:, t:t + 1].bitcast(U32), axis=0))
                back = self.pool.either(lambda e, f=fetch_rows: f(e, y_rows),
                                        lambda e, f=fetch_rows: f(e, y_rows[0:EXPERTS * cap, :]),
                                        free[t % 2], inc=s_back[t % 2])
            self.ts(dve, pair[0], pair[0], weight[0][:, t:t + 1], None, ALU.mult, None, back)
            m = self.stt(pair[0], pair[1], weight[1][:, t:t + 1], pair[0], ALU.mult, ALU.add, chain=True)
            for half in range(2):
                b = g.bank()
                for k in range(4):
                    end = self.turn(self.psum[b][:, k * P:(k + 1) * P],
                                    pair[0][:, (4 * half + k) * P:(4 * half + k + 1) * P], mark=k == 3, wait=(m,))
                for k in range(4):
                    kk = 4 * half + k
                    at = self.X[:, kk, t * P:(t + 1) * P]
                    c = t * P // SEQ
                    m2 = self.stt(at, self.psum[b][:, k * P:(k + 1) * P], self.mod[:, layer, 5 * KD + kk, c:c + 1], at,
                                  ALU.mult, ALU.add, end)
                g.bank_free[b] = [m2]
            free[t % 2] = end

    def ssm(self):
        g, a, T, ring = self.g, self.a, SEQ, self.ring
        dve, act, pool, pe = self.dve, self.act, self.pool, self.pe
        NC = T // CHUNK
        ar = self.stage()
        Z, XBC = ar.take(NC, D_INNER), ar.take(32, T)
        keep = ar.at
        pad_w = SSM_CONV - 1
        PB, acc = ar.take(4, T + pad_w), ar.take(2, T)
        dt, acs, eacs, adt = (ar.take(NC, HEADS) for _ in range(4))
        t1, t2, tail = ar.take(NC, HEADS), ar.take(NC, HEADS), ar.take(HEADS)
        neg_a = ar.take(HEADS)
        pads = pool.do(lambda e, i: e.memset(PB, 0.0))
        ready = self.simple_norm(self.col("a_norm"))
        w_in = a["ssm_w_in_2"][0]
        A = self.A

        for n in range(D_INNER // 512):
            w, landed = self.weights(w_in, KD, n * 512, 512)
            for c in range(NC):
                b = g.bank()
                end = self.product(self.psum[b][:, :], lambda k: A[:, k, c * P:(c + 1) * P], lambda k: w[:, k, :], KD,
                                   last=ring.free if c == NC - 1 else None, wait=(landed, ready))
                m = self.fn(Z[:, c, n * 512:(n + 1) * 512], self.psum[b][:, :], ACT.Silu, end)
                g.bank_free[b] = [m]

        taps, cb = self.col("ssm_conv_w"), self.col("ssm_conv_b")
        conv_free, acc_free = [pads] * 4, [None] * 2

        def evac(m, out, mark):
            s = m % 4
            end = self.copy(act, PB[:, s, pad_w:], out, mark, conv_free[s])
            buf = acc[:, m % 2, :]
            self.ts(dve, buf, PB[:, s, 0:T], taps[:, m, 0:1], None, ALU.mult, None, end, acc_free[m % 2])
            for j in range(1, SSM_CONV):
                done = self.stt(buf, PB[:, s, j:j + T], taps[:, m, j:j + 1], buf, ALU.mult, ALU.add, chain=True)
            conv_free[s] = done
            acc_free[m % 2] = self.fn(XBC[:, m, :], buf, ACT.Silu, done, bias=cb[:, m:m + 1])
            return end

        self.linear(w_in[:, D_INNER:], KD, 4096, lambda k: A[:, k, 0:T], T, evac, ready)

        wv = w_in.rearrange("(k p) n -> p k n", p=P)[:, :, D_INNER + 4096:D_INNER + 4096 + HEADS]
        (w,), landed = ring.load(((KD, HEADS), 0, lambda i: wv))
        b = g.bank()
        for c in range(NC):
            end = self.product(self.psum[b][:, c * HEADS:(c + 1) * HEADS], lambda k: A[:, k, c * P:(c + 1) * P],
                               lambda k: w[:, k, :], KD, last=ring.free if c == NC - 1 else None, wait=(landed,))
        raw = self.psum[b][:, 0:NC * HEADS].rearrange("p (c h) -> p c h", c=NC)
        m = self.tt(dve, dt, raw, across(self.row("dt_bias"), NC), ALU.add, end)
        g.bank_free[b] = [m]
        self.ts(dve, t1, dt, -1.0, None, ALU.mult, None, chain=True)
        m = self.tt(dve, t1, t1, dt, ALU.max, chain=True)
        m = self.fn(t1, t1, ACT.Exp, m, scale=-1.0)
        u = self.ts(dve, t2, t1, 1.0, None, ALU.add, None, m)
        m = self.fn(acs, t2, ACT.Ln, u)
        self.ts(dve, adt, t2, -1.0, None, ALU.add, None, chain=True)
        self.tt(dve, adt, t1, adt, ALU.subtract, chain=True)
        dve.chain(lambda e, i: e.reciprocal(t2, t2), m)
        self.tt(dve, adt, adt, t2, ALU.mult, chain=True)
        self.tt(dve, adt, adt, acs, ALU.add, m, chain=True)
        self.stt(dt, dt, 0.0, adt, ALU.max, ALU.add, chain=True)
        ma = self.fn(neg_a, self.row("a_log"), ACT.Exp)
        self.ts(dve, neg_a, neg_a, -1.0, None, ALU.mult, None, ma)
        m_adt = self.tt(dve, adt, dt, across(neg_a, NC), ALU.mult, chain=True)

        b = g.bank()
        flat = lambda v: v.rearrange("p c h -> p (c h)")
        self.mm(self.psum[b][:, 0:NC * HEADS], self.mat("upto"), flat(adt), True, True, wait=(m_adt,))
        end = self.mm(self.psum[b][:, 128:128 + HEADS], self.mat("ones"), adt[:, 0, :], True, True, mark=True)
        m_acs = self.copy(dve, flat(acs), self.psum[b][:, 0:NC * HEADS], end)
        m = self.tt(dve, tail, self.psum[b][:, 128:128 + HEADS], acs[:, 0, :], ALU.subtract, chain=True)
        g.bank_free[b] = [m]
        m_tail = self.fn(tail, tail, ACT.Exp, m)
        m_eacs = self.fn(eacs, acs, ACT.Exp, m_acs)
        conv_done = act.done.now()
        dve_done = dve.done.now()

        g.meet()
        save = (dt, acs, eacs, adt, tail)
        XS = A[:, :, :].rearrange("p k t -> p (k t)").rearrange("p (c n) -> p c n", c=NC)
        BT = PB.rearrange("p a b -> p (a b)")[:, 0:SSM_G * STATE]
        XC = [ar.take(SSM_G, HG * HEAD_P), self.X[:, :, SEQ:]]
        for c in range(NC):
            for q in range(4):
                b = g.bank()
                for j in range(4):
                    end = self.turn(self.psum[b][:, j * P:(j + 1) * P], XBC[:, 4 * q + j, c * P:(c + 1) * P], mark=j == 3)
                m = self.copy(act, XS[:, c, q * 512:(q + 1) * 512], self.psum[b][:, :], end)
                g.bank_free[b] = [m]
            xs = XS[:, c, :].rearrange("p (h d) -> p h d", h=HEADS)
            by_group = lambda v: v.rearrange("p g (h d) -> p g h d", d=HEAD_P)
            m = self.tt(dve, by_group(XC[c]), by_group(XS[:, c, :].rearrange("p (g n) -> p g n", g=SSM_G)),
                        along(dt[:, c, :].rearrange("p (g h) -> p g h", g=SSM_G), HEAD_P), ALU.mult, m)
            m_skip = self.tt(pool, xs, xs, along(self.row("d_skip"), HEAD_P), ALU.mult, m)
        m_xc = m
        for q in range(2):
            b = g.bank()
            for j in range(4):
                end = self.turn(self.psum[b][:, j * P:(j + 1) * P], XBC[:, 16 + 4 * q + j, 0:P], mark=j == 3)
            m_bt = self.copy(act, BT[:, q * 512:(q + 1) * 512], self.psum[b][:, :], end)
            g.bank_free[b] = [m_bt]

        mask = ar.take(CHUNK)
        m_mask = self.fetch(mask, a["ssm_mask"])
        work = XBC[:, 0:16, :].rearrange("p m t -> p (m t)")
        cut = lambda n, w: work[:, n * w:(n + 1) * w]
        R = [cut(0, 512), cut(1, 512)]
        E = [cut(2, 512), cut(3, 512)]
        CB = [cut(16, 128), cut(17, 128)]
        XD, PREV, YO = cut(9, 256), cut(10, 256), cut(11, 256)
        pe.wait(m_xc, m_bt)
        r_free, e_free, cb_free = [None] * 2, [None] * 2, [None] * 2
        step = 0
        xd_free = prev_free = None
        last_turn = pe.done.now()
        for lane in (dve, pool, act):
            lane.wait(last_turn)
        for grp in range(SSM_G):
            hs = slice(grp * HG, (grp + 1) * HG)
            ch = slice(grp * HG * HEAD_P, (grp + 1) * HG * HEAD_P)
            for c in range(NC):
                s = step % 2
                step += 1
                bt, ct = XBC[:, 16 + grp, c * P:(c + 1) * P], XBC[:, 24 + grp, c * P:(c + 1) * P]
                b = g.bank()
                end = self.mm(self.psum[b][:, 0:P], bt, ct, True, True, mark=True)
                m_cb = self.copy(act, CB[s], self.psum[b][:, 0:P], end, cb_free[s])
                g.bank_free[b] = [m_cb]
                r4 = R[s].rearrange("p (h t) -> p h t", h=HG)
                m = self.tt(pool, r4, across(self.mat("upto"), HG), along(adt[:, c, hs], P), ALU.mult, r_free[s])
                b = g.bank()
                end = self.mm(self.psum[b][:, :], self.mat("ones"), R[s], True, True, mark=True, wait=(m,))
                r_free[s] = end
                e4 = E[s].rearrange("p (h t) -> p h t", h=HG)
                m = self.tt(dve, e4, self.psum[b][:, :].rearrange("p (h t) -> p h t", h=HG),
                            along(acs[:, c, hs], P), ALU.subtract, end, e_free[s])
                g.bank_free[b] = [m]
                m = self.tt(dve, e4, e4, across(mask, HG), ALU.add, m_mask, chain=True)
                m = self.fn(E[s], E[s], ACT.Exp, m)
                m = self.tt(dve, e4, e4, across(CB[s], HG), ALU.mult, m, m_cb)
                cb_free[s] = m
                b = g.bank()
                for h in range(HG):
                    end = self.mm(self.psum[b][:, h * HEAD_P:(h + 1) * HEAD_P], E[s][:, h * P:(h + 1) * P],
                                  XC[c][:, grp, h * HEAD_P:(h + 1) * HEAD_P], True, True, mark=h == HG - 1, wait=(m,))
                e_free[s] = end
                y = XS[:, c, ch]
                if c == 0:
                    m = self.tt(dve, y, self.psum[b][:, 0:256], y, ALU.add, end, m_skip)
                    g.bank_free[b] = [m]
                    m = self.tt(dve, XD.rearrange("p (h d) -> p h d", h=HG),
                                XC[0][:, grp, :].rearrange("p (h d) -> p h d", h=HG), along(tail[:, hs], HEAD_P),
                                ALU.mult, m_tail, xd_free)
                    b = g.bank()
                    end = self.mm(self.psum[b][:, 0:256], BT[:, grp * STATE:(grp + 1) * STATE], XD, True, True,
                                  mark=True, wait=(m,))
                    xd_free = end
                    m_prev = self.copy(act, PREV, self.psum[b][:, 0:256], end, prev_free)
                    g.bank_free[b] = [m_prev]
                else:
                    m = self.tt(dve, y, self.psum[b][:, 0:256], y, ALU.add, end, m_skip)
                    g.bank_free[b] = [m]
                    b = g.bank()
                    end = self.mm(self.psum[b][:, 0:256], ct, PREV, True, True, mark=True, wait=(m_prev,))
                    prev_free = end
                    self.tt(dve, YO.rearrange("p (h d) -> p h d", h=HG),
                            self.psum[b][:, 0:256].rearrange("p (h d) -> p h d", h=HG), along(eacs[:, 1, hs], HEAD_P),
                            ALU.mult, end, m_eacs)
                    g.bank_free[b] = [dve.done.now()]
                    self.tt(dve, y, y, YO, ALU.add, chain=True)

        ss = t1.rearrange("p c h -> p (c h)")[:, 0:NC * SSM_G].rearrange("p (c g) -> p c g", c=NC)
        pe_last = pe.done.now()
        for c in range(NC):
            self.tt(dve, XS[:, c, :], XS[:, c, :], Z[:, c, :], ALU.mult, chain=True)
            m = dve.done.now()
            m = self.fn(XC[c], XS[:, c, :].rearrange("p (g n) -> p g n", g=SSM_G), ACT.Square, m, pe_last)
            dve.do(lambda e, i, c=c: e.tensor_reduce(
                ss[:, c, :], XC[c], AX.X, ALU.add), m)
        m = self.ts(dve, ss, ss, 1.0 / 256.0, GATED_EPS, ALU.mult, ALU.add, chain=True)
        dve.do(lambda e, i: e.reciprocal(ss, ss), self.fn(ss, ss, ACT.Sqrt, m))
        for c in range(NC):
            y = XS[:, c, :].rearrange("p (g n) -> p g n", g=SSM_G)
            m = self.tt(dve, y, y, along(ss[:, c, :], 256), ALU.mult, chain=True)
        YT = Z.rearrange("p c n -> p (c n)").rearrange("p (m t) -> p m t", m=16)
        gain = self.col("ssm_norm")
        for q in range(8):
            b = g.bank()
            for j in range(2):
                for c in range(NC):
                    end = self.turn(self.psum[b][:, (2 * j + c) * P:(2 * j + c + 1) * P],
                                    XS[:, c, (2 * q + j) * P:(2 * q + j + 1) * P], mark=j and c, wait=(m,))
            for j in range(2):
                m2 = self.ts(dve, YT[:, 2 * q + j, :], self.psum[b][:, 2 * j * P:(2 * j + 2) * P],
                             gain[:, 2 * q + j:2 * q + j + 1], None, ALU.mult, None, end)
            g.bank_free[b] = [m2]
        self.linear(a["ssm_w_out_2"][0], 16, D, lambda k: YT[:, k, :], T, self.add_plain, m2, width=256)

    def ffn(self, layer):
        g, a, T, ring = self.g, self.a, SEQ, self.ring
        dve, act = self.dve, self.act
        ar = self.stage()
        pad = FFN_CONV - 1
        H, PB, acc = ar.take(KFF, T), ar.take(4, 2, T + pad), ar.take(4, 2, T)
        pads = self.pool.do(lambda e, i: e.memset(PB, 0.0))
        ready = self.simple_norm(self.col("ffn_norm")[:, layer, :])
        w_up = a["ffn_w_up_2"][layer].rearrange("(k p) (j n) -> p k j n", p=P, j=2)
        taps = self.col("ffn_conv_w")
        pb_free, acc_free = [pads] * 4, [None] * 4
        for n in range(KFF // 2):
            (wg, wv), landed = ring.load(
                ((KD, 256), 0, lambda i, n=n: w_up[:, :, 0, n * 256:(n + 1) * 256]),
                ((KD, 256), KD * 256, lambda i, n=n: w_up[:, :, 1, n * 256:(n + 1) * 256]))
            for t in range(2):
                m = 2 * n + t
                s = m % 4
                b = g.bank()
                for j, w in enumerate((wg, wv)):
                    end = self.product(self.psum[b][:, j * T:(j + 1) * T], lambda k: w[:, k, t * P:(t + 1) * P],
                                       lambda k: self.A[:, k, 0:T], KD,
                                       last=ring.free if t == 1 and j == 1 else None, wait=(landed, ready))
                mark = self.copy(act, PB[:, s, :, pad:], self.psum[b][:, :].rearrange("p (j t) -> p j t", j=2),
                                 end, pb_free[s])
                g.bank_free[b] = [mark]
                for j in range(2):
                    buf, w3 = acc[:, s, j, :], taps[:, layer, j * KFF + m, :]
                    self.ts(dve, buf, PB[:, s, j, 0:T], w3[:, 0:1], None, ALU.mult, None, mark, acc_free[s])
                    for q in (1, 2):
                        done = self.stt(buf, PB[:, s, j, q:q + T], w3[:, q:q + 1], buf, ALU.mult, ALU.add, chain=True)
                    if j == 0:
                        silu = self.fn(buf, buf, ACT.Silu, done)
                pb_free[s] = done
                acc_free[s] = self.tt(self.pool, H[:, m, :], acc[:, s, 0, :], acc[:, s, 1, :], ALU.mult, silu, done)
        h_ready = acc_free[1], acc_free[(KFF - 1) % 4]
        self.pe.wait(*[m for f in g.bank_free for m in f])
        w_down = a["ffn_w_down_2"][layer].rearrange("(k p) n -> p k n", p=P)
        for first in range(0, KFF, 4):
            n_k = min(4, KFF - first)
            (w,), landed = ring.load(((n_k, D), 0, lambda i, f=first, n=n_k: w_down[:, f:f + n, :]))
            for m in range(KD):
                for k in range(n_k):
                    last = m == KD - 1 and k == n_k - 1
                    end = self.mm(self.psum[m][:, 0:T], w[:, k, m * P:(m + 1) * P], H[:, first + k, :],
                                  first + k == 0, first + k == KFF - 1, mark=last, inc=ring.free,
                                  wait=(landed, acc_free[(KFF - 1) % 4]))
        for m in range(KD):
            g.bank_free[m] = [self.add_plain(m, self.psum[m][:, 0:T], end)]
        g.bank_at = 0

    def dilated(self):
        g, a, T, ring = self.g, self.a, SEQ, self.ring
        dve, act, pool, pe = self.dve, self.act, self.pool, self.pe
        ar = self.stage()
        n_kv = N_PAT * ATT_KV
        Q, K, V = ar.take(N_PAT * ATT_HEADS, T), ar.take(n_kv, T), ar.take(2, n_kv * ATT_D)
        cos, sin, rot = ar.take(2, T), ar.take(2, T), ar.take(P)
        widths = [N_PAT * att_keys(q) for q in range(2)]
        mask = ar.take(sum(widths))
        S = [ar.take(w) for w in widths]
        turned = ar.take(2, T)
        small = ar.take(3, 2)
        A = self.A.rearrange("p k t -> p (k t)")
        AK, AQ = (A[:, j * KD * T:(j + 1) * KD * T].rearrange("p (k t) -> p k t", k=KD) for j in range(2))
        for j in range(2):
            self.fetch(cos[:, j, :], a["tables"][:, 640:640 + T])
            self.fetch(sin[:, j, :], a["tables"][:, 896:896 + T])
        self.fetch(rot, a["tables"][:, 1152:1152 + P])
        tables = self.fetch(mask, a["att_mask"])
        stat = self.mean_square(self.X, KD, T, D, NORM_EPS, AK)
        self.scaled(AK, self.X, self.col("kv_norm"), T, KD, stat)
        ready = self.scaled(AQ, self.X, self.col("b_norm"), T, KD, stat)
        R = ROPE_DIM

        def rotary(two, mark):
            b = g.bank()
            end = self.mm(self.psum[b][:, :], rot, two.rearrange("p m t -> p (m t)"), True, True, mark=True,
                          wait=(mark, tables))
            out = self.psum[b][0:R, :].rearrange("p (m t) -> p m t", m=2)
            m = self.tt(dve, turned[0:R], out, sin[0:R], ALU.mult, end, chain=True)
            g.bank_free[b] = [m]
            self.tt(dve, two[0:R], two[0:R], cos[0:R], ALU.mult, end)
            return self.tt(dve, two[0:R], two[0:R], turned[0:R], ALU.add, chain=True)

        def heads(w, landed, n, rhs, dst, scale, last):
            for t in range(0, n, 2):
                b = g.bank()
                for j in range(2):
                    end = self.product(self.psum[b][:, j * T:(j + 1) * T], lambda k: w[:, k, (t + j) * P:(t + j + 1) * P],
                                       rhs, KD, last=ring.free if last and t + j == n - 1 else None,
                                       wait=(landed, ready))
                two = dst[:, t:t + 2, :]
                m = self.fn(two, self.psum[b][:, :].rearrange("p (m t) -> p m t", m=2), ACT.Copy, end, scale=scale)
                g.bank_free[b] = [m]
                waiting.append((two, m))
                if len(waiting) > 1:
                    rotary(*waiting.pop(0))

        def tokens(w, landed, cols, dst_at, last):
            n = cols.stop - cols.start
            for c in range(2):
                b = g.bank()
                end = self.product(self.psum[b][:, 0:n], lambda k: AK[:, k, c * P:(c + 1) * P], lambda k: w[:, k, cols],
                                   KD, last=ring.free if last and c == 1 else None, wait=(landed, ready))
                m = self.copy(act, V[:, c, dst_at:dst_at + n], self.psum[b][:, 0:n], end)
                g.bank_free[b] = [m]
            return m

        waiting = []
        k_rhs, q_rhs = (lambda k: AK[:, k, :]), (lambda k: AQ[:, k, :])
        w, landed = self.weights(a["w_kv_2"], KD, 0, 512)
        heads(w, landed, 4, k_rhs, K[:, 0:4, :], 1.0, True)
        w, landed = self.weights(a["w_kv_2"], KD, 512, 512)
        heads(w, landed, 2, k_rhs, K[:, 4:6, :], 1.0, False)
        tokens(w, landed, slice(256, 512), 0, True)
        w, landed = self.weights(a["w_kv_2"], KD, 1024, 512)
        tokens(w, landed, slice(0, 512), 256, True)
        for c in range(6):
            w, landed = self.weights(a["att_w_q_2"][0], KD, c * 512, 512)
            heads(w, landed, 4, q_rhs, Q[:, 4 * c:4 * c + 4, :], float(ATT_D) ** -0.5, True)
        rotary(*waiting.pop(0))
        g.meet()

        OT = AQ
        PT = [AK.rearrange("p k t -> p (k t)")[:, 0:widths[0]], AK.rearrange("p k t -> p (k t)")[:, widths[0]:sum(widths)]]
        s_free, pt_free = [None, None], [None, None]

        def scores(h, q):
            kv, n = h // (ATT_HEADS // ATT_KV), att_keys(q)
            banks, at = [], 0
            for p in range(N_PAT):
                if (at + n) > BANK or p == 0:
                    b, at = g.bank(), 0
                    banks.append([b, p, 0])
                end = self.mm(self.psum[b][:, at:at + n], Q[:, p * ATT_HEADS + h, q * P:(q + 1) * P],
                              K[:, p * ATT_KV + kv, 0:n], True, True, mark=True)
                at += n
                banks[-1][2] = at
            base = 0 if q == 0 else widths[0]
            for b, p, w in banks:
                lo = p * n
                m = self.tt(dve, S[q][:, lo:lo + w], self.psum[b][:, 0:w], mask[:, base + lo:base + lo + w], ALU.add,
                            end, s_free[q])
                g.bank_free[b] = [m]
            top, total, inv = (small[:, j, q:q + 1] for j in range(3))
            m = dve.chain(lambda e, i: e.tensor_reduce(top, S[q], AX.X, ALU.max, negate=True))
            m = self.fn(S[q], S[q], ACT.Exp, m, bias=top, total=total)
            dve.do(lambda e, i: e.reciprocal(inv, total), m)
            return self.ts(dve, S[q], S[q], inv, None, ALU.mult, None, chain=True)

        def values(h, q, mark):
            kv, n_b = h // (ATT_HEADS // ATT_KV), q + 1
            blocks = N_PAT * n_b
            for lo in range(0, blocks, 4):
                b = g.bank()
                hi = min(blocks, lo + 4)
                for j in range(lo, hi):
                    end = self.turn(self.psum[b][:, (j - lo) * P:(j - lo + 1) * P], S[q][:, j * P:(j + 1) * P],
                                    mark=j == hi - 1, wait=(mark,))
                m = self.copy(act, PT[q][:, lo * P:hi * P], self.psum[b][:, 0:(hi - lo) * P], end, pt_free[q])
                g.bank_free[b] = [m]
            s_free[q] = end
            b = g.bank()
            for j in range(blocks):
                p, c = divmod(j, n_b)
                at = (p * ATT_KV + kv) * ATT_D
                end = self.mm(self.psum[b][:, 0:P], V[:, c, at:at + ATT_D], PT[q][:, j * P:(j + 1) * P],
                              j == 0, j == blocks - 1, mark=j == blocks - 1, wait=(m,))
            pt_free[q] = end
            m = self.copy(dve, OT[:, h, q * P:(q + 1) * P], self.psum[b][:, 0:P], end)
            g.bank_free[b] = [m]
            return m

        order = [(h, q) for h in range(ATT_HEADS) for q in range(2)]
        before = scores(*order[0])
        for n, (h, q) in enumerate(order):
            after = scores(*order[n + 1]) if n + 1 < len(order) else None
            out_mark = values(h, q, before)
            before = after
        self.linear(a["att_w_o_2"][0], KD, D, lambda k: OT[:, k, :], T, self.add_plain, out_mark)

    def finish(self):
        self.stage()
        m = self.simple_norm(self.col("final_2"))
        out = self.g.counter("result")
        y = self.a["y"].rearrange("(k p) t -> p k t", p=P)
        m = self.act.do(lambda e, i: e.dma_start(y, self.A[:, :, 0:SEQ]), m, inc=out)
        for lane in self.g.lanes:
            lane.wait(m)

    def between_networks(self):
        self.stage()
        stat = self.mean_square(self.X, KD, SEQ, D, NORM_EPS, self.A)
        self.scaled(self.X, self.X, self.col("final_1"), SEQ, KD, stat)

    def emit(self):
        with self.nc.Block() as block:
            for name, lane in zip(("tensor", "scalar", "vector", "gpsimd", "sync"), self.g.lanes):
                {"tensor": block.tensor, "scalar": block.scalar, "vector": block.vector,
                 "gpsimd": block.gpsimd, "sync": block.sync}[name](lambda e, lane=lane: lane.replay(e))


def build(nc, a, stop=None):
    with ExitStack() as ctx:
        k = Kernel(nc, ctx, a)
        k.start()
        k.modulation(0)
        stages = [k.mla, lambda: k.moe(0, SEQ + CTX, CAP[0]), lambda: k.modulation(1), k.conv_mixer,
                  lambda: k.moe(1, SEQ, CAP[1]), k.between_networks, k.ssm, lambda: k.ffn(0), k.dilated,
                  lambda: k.ffn(1), k.finish]
        for f in stages[:stop]:
            f()
        if stop is not None:
            k.stage()
            out = k.g.counter("dump")
            m = k.act.do(lambda e, i: e.dma_start(a["dump"].rearrange("(k p) t -> p k t", p=P), k.X[:, :, :]), inc=out)
            for lane in k.g.lanes:
                lane.wait(m)
        k.emit()


_WEIGHTS = ["w_mod", "mla_w_dq", "mla_w_uq", "mla_w_dkv", "mla_w_ukv", "mla_w_o", "conv_w_in", "conv_w_out",
            "moe_w_group", "moe_w_expert", "moe_w_gate", "moe_w_up", "moe_w_down", "ssm_w_in_2", "ssm_w_out_2",
            "w_kv_2", "att_w_q_2", "att_w_o_2", "ffn_w_up_2", "ffn_w_down_2"]


def _constants():
    f = np.float32
    i = np.arange(P)
    mats = np.stack([np.eye(P, dtype=f), np.full((P, P), 1 / 1024, f), np.full((P, P), 1 / 512, f),
                     np.full((P, P), 1 / 256, f), np.ones((P, P), f), (i[:, None] < i[None, :]).astype(f),
                     (i[:, None] <= i[None, :]).astype(f)], axis=1)
    t = np.arange(SEQ)
    tables = np.zeros((P, 1280), f)

    def rotary(at, d, pos, inv_freq, x, half):
        angle = pos.astype(f) * inv_freq[x % half]
        tables[d, at:at + SEQ] = np.cos(angle)
        tables[d, at + SEQ:at + 2 * SEQ] = np.sin(angle)
        if x < half:
            tables[d + half, at + 2 * SEQ + d] = -1
        else:
            tables[d - half, at + 2 * SEQ + d] = 1

    half = MLA_ROPE // 4
    inv = (f(ROPE_THETA) ** (-np.arange(half, dtype=f) / half)).astype(f)
    for d in range(P):
        x = d % MLA_ROPE
        rotary(0, d, t // GRID_W if x < MLA_ROPE // 2 else t % GRID_W, inv, x % (2 * half), half)
    half = ROPE_DIM // 2
    inv = (f(ROPE_THETA_2) ** (-np.arange(0, ROPE_DIM, 2, dtype=f) / ROPE_DIM)).astype(f)
    for d in range(ROPE_DIM):
        rotary(640, d, t, inv, d, half)
    masks = []
    for q in range(2):
        back = (q * P + i)[:, None] - np.arange(att_keys(q))[None, :]
        for window, dilation in PATTERNS:
            masks.append(np.where((back >= 0) & (back <= window) & (back % dilation == 0), 0, NEG))
    return {"mats": mats, "tables": tables, "att_mask": np.concatenate(masks, axis=1).astype(f),
            "ssm_mask": np.where(i[:, None] <= i[None, :], 0, NEG).astype(f)}


def _vectors(v):
    f = np.float32
    tiles = lambda x: np.moveaxis(x.reshape(*x.shape[:-1], -1, P), -1, 0)
    taps = lambda x: np.moveaxis(tiles(x), -2, -1)
    parts = {"cond": np.stack([tiles(v["c"][0]), tiles(v["c_ctx"])], -1), "b_mod": tiles(v["b_mod"]),
             "norm_mix": tiles(v["norm_mix_g"]), "norm_ffn": tiles(v["norm_ffn_g"]), "g_q": tiles(v["mla_g_q"][0]),
             "g_kv": tiles(v["mla_g_kv"][0]), "conv_w": taps(v["conv_w"][0]), "final_1": tiles(v["final_norm_g"]),
             "a_norm": tiles(v["a_norm_2"][0]), "ssm_conv_w": taps(v["ssm_conv_w_2"][0]),
             "ssm_conv_b": tiles(v["ssm_conv_b_2"][0]), "ssm_norm": tiles(v["ssm_norm_2"][0]),
             "kv_norm": tiles(v["kv_norm_2"]), "b_norm": tiles(v["b_norm_2"][0]), "ffn_norm": tiles(v["ffn_norm_2"]),
             "ffn_conv_w": taps(v["ffn_conv_w_2"]), "final_2": tiles(v["final_norm_2"]),
             "token": np.arange(P * 4, dtype=f).reshape(4, P).T}
    cols = np.concatenate([parts[n].reshape(P, -1) for n in column_layout()[0]], axis=1)
    rows = {"first_4": np.arange(GROUPS, 0, -1, dtype=f), "first_8": np.arange(PER_GROUP, 0, -1, dtype=f),
            "count": np.arange(P, dtype=f), "dt_bias": v["ssm_dt_bias_2"][0], "a_log": v["ssm_a_log_2"][0],
            "d_skip": v["ssm_d_2"][0]}
    for j in range(2):
        rows[f"route_bias_{j}"] = np.concatenate([v["moe_b_group"][j], v["moe_b_expert"][j]])
    return cols, np.concatenate([rows[n] for n in row_layout()[0]])[None, :]


def arrays_of(inputs):
    v = {k: np.asarray(x) for k, x in inputs.items()}
    arrays = {n: v[n] for n in _WEIGHTS}
    arrays |= _constants()
    arrays["cols"], arrays["rows"] = _vectors(v)
    arrays["xT"], arrays["ctxT"] = v["x"][0].T, v["ctx"][0].T
    return {k: np.ascontiguousarray(x) for k, x in arrays.items()}


def kernel(**inputs):
    import concourse.bacc as bacc
    from concourse.bass_utils import run_bass_kernel_spmd

    nc = bacc.Bacc("TRN2", target_bir_lowering=False, num_devices=1)
    arrays, a = {}, {}
    for name, x in arrays_of(inputs).items():
        arrays[f"in_{name}"] = x
        a[name] = nc.dram_tensor(f"in_{name}", x.shape, mybir.dt.from_np(x.dtype), kind="ExternalInput").ap()
    a["y"] = nc.dram_tensor("y", [D, SEQ], F32, kind="ExternalOutput").ap()
    build(nc, a)
    got = run_bass_kernel_spmd(nc, [arrays], core_ids=[0]).results[0]["y"]
    return np.ascontiguousarray(np.asarray(got).T)[None]
```

```python
from contextlib import ExitStack

import numpy as np

import concourse.bass as bass
from concourse import mybir
from concourse.alu_op_type import AluOpType as ALU

F32 = mybir.dt.float32
I32 = mybir.dt.int32
U32 = mybir.dt.uint32
ACT = mybir.ActivationFunctionType
AX = mybir.AxisListType

P = 128
BANK = 512
SLOT = 4096
RING = 6

D = 1024
KD = D // P
SEQ = 256
CTX = 256
N_MOD = 6
GRID_W = 64
MLA_HEADS = 8
MLA_NOPE = 128
MLA_ROPE = 64
MLA_V = 128
MLA_Q_LORA = 512
MLA_KV_LORA = 256
ROPE_THETA = 10000.0
NORM_EPS = 1e-6
GROUPS = 4
PER_GROUP = 8
EXPERTS = GROUPS * PER_GROUP
FF = 512
KF = FF // P
CONV_W = 3
D_INNER = 2048
HEAD_P = 64
HEADS = D_INNER // HEAD_P
SSM_G = 8
STATE = 128
HG = HEADS // SSM_G
SSM_CONV = 4
CHUNK = 128
GATED_EPS = 1e-5
PATTERNS = ((128, 1), (512, 4), (2048, 16))
N_PAT = len(PATTERNS)
ATT_HEADS = 8
ATT_KV = 2
ATT_D = 128
ROPE_DIM = ATT_D // 4
ROPE_THETA_2 = 500000.0
FFN = 2816
KFF = FFN // P
FFN_CONV = 3
CAP = (96, 80)
NEG = -1e30
BIG = 3.0e38


def column_layout():
    parts = [("cond", (KD, 2)), ("b_mod", (2, N_MOD * KD)), ("norm_mix", (2, KD)), ("norm_ffn", (2, KD)),
             ("g_q", (MLA_Q_LORA // P,)), ("g_kv", (MLA_KV_LORA // P,)), ("conv_w", (KD, CONV_W)),
             ("final_1", (KD,)), ("a_norm", (KD,)), ("ssm_conv_w", (32, SSM_CONV)), ("ssm_conv_b", (32,)),
             ("ssm_norm", (16,)), ("kv_norm", (KD,)), ("b_norm", (KD,)), ("ffn_norm", (2, KD)),
             ("ffn_conv_w", (2, 2 * KFF, FFN_CONV)), ("final_2", (KD,)), ("token", (4,))]
    at, out = 0, {}
    for name, shape in parts:
        out[name] = (at, shape)
        at += int(np.prod(shape))
    return out, at


def row_layout():
    parts = [("route_bias_0", GROUPS + EXPERTS), ("route_bias_1", GROUPS + EXPERTS), ("first_4", GROUPS),
             ("first_8", PER_GROUP), ("count", P), ("dt_bias", HEADS), ("a_log", HEADS), ("d_skip", HEADS)]
    at, out = 0, {}
    for name, n in parts:
        out[name] = (at, n)
        at += n
    return out, at


MATS = ["ident", "ones_1024", "ones_512", "ones_256", "ones", "before", "upto"]


def att_keys(qt):
    return (qt + 1) * P


class Counter:

    def __init__(self, sem, step=1):
        self.sem, self.step, self.n, self.base, self.per, self.loop = sem, step, 0, 0, 0, None

    def raised(self, loop):
        self.enter(loop)
        self.n += self.step
        return Mark(self, self.n, self.loop)

    def enter(self, loop):
        if self.loop is not loop:
            assert loop is not None
            self.loop, self.base, self.n = loop, self.n, 0
            loop.counters.append(self)

    def now(self):
        return Mark(self, self.n, self.loop)


class Mark:

    def __init__(self, counter, off, loop, frame=None):
        self.counter, self.off, self.loop = counter, off, loop

    def value(self, index, shift):
        if self.loop is None:
            return self.off
        base, per = self.loop.frames[self.counter]
        if index is None:
            return base + self.off + per * (self.loop.trips - 1)
        const = base + self.off + per * shift
        assert const > 0, self.counter.sem
        return index * per + const if per else const


class Later:

    mark = None

    def set(self, mark):
        self.mark = mark


class Loop:

    def __init__(self, shape):
        self.shape, self.trips = shape, int(np.prod(shape))
        self.counters, self.frames = [], {}


class Lane:

    def __init__(self, program, name, sem):
        self.program, self.name, self.items, self.done = program, name, [], Counter(sem)
        self.in_order = name in ("act", "dve", "pool")
        self.waited = {}

    def wait(self, *marks):
        for m in marks:
            if m is None:
                continue
            if isinstance(m, Later):
                self.items.append(("wait", m, -1))
                continue
            key = (m.counter, m.loop)
            if m.off <= self.waited.get(key, 0):
                continue
            self.waited[key] = m.off
            self.items.append(("wait", m, 0))

    def do(self, fn, *marks, inc=None, mark=True, loose=False):
        self.wait(*marks)
        if self.in_order and not loose:
            self.wait(self.done.now())
        counter = (inc or self.done) if mark else None
        self.items.append(("op", fn, counter))
        return counter.raised(self.program.loop) if counter else None

    def chain(self, fn, *marks, inc=None):
        return self.do(fn, *marks, self.done.now(), inc=inc)

    def replay(self, engine, items=None, index=None, indices=None):
        for item in (self.items if items is None else items):
            kind = item[0]
            if kind == "wait":
                mark = item[1].mark if isinstance(item[1], Later) else item[1]
                here = index if mark.loop is not None and mark.loop is self.running else None
                value = mark.value(here, item[2])
                if isinstance(value, int) and value <= 0:
                    continue
                engine.wait_ge(mark.counter.sem, value)
            elif kind == "op":
                got = item[1](engine, indices)
                if item[2] is not None:
                    got.then_inc(item[2].sem, item[2].step)
            elif kind == "loop":
                _, loop, body = item
                outer, self.running = self.running, loop
                if len(loop.shape) == 1:
                    with engine.Fori(0, loop.shape[0], 1) as i:
                        self.replay(engine, body, i, (i,))
                else:
                    with engine.Fori(0, loop.shape[0], 1) as a:
                        with engine.Fori(0, loop.shape[1], 1) as b:
                            self.replay(engine, body, a * loop.shape[1] + b, (a, b))
                self.running = outer
            elif kind == "if":
                _, flag, body = item
                self.flag = value = engine.value_load(flag, min_val=0, max_val=4096)
                with engine.If(value > 0):
                    self.replay(engine, body)

            elif kind == "either":
                _, yes, no, counter = item
                with engine.If(self.flag > 0):
                    yes(engine).then_inc(counter.sem, counter.step)
                with engine.Else():
                    no(engine).then_inc(counter.sem, counter.step)

    def either(self, yes, no, *marks, inc):
        self.wait(*marks, self.done.now())
        self.items.append(("either", yes, no, inc))
        return inc.raised(self.program.loop)

    running = None
    flag = None


class Program:

    def __init__(self, nc, ctx):
        self.nc, self.ctx, self.loop = nc, ctx, None
        self.pe, self.act, self.dve, self.pool, self.sp = (
            Lane(self, n, self.semaphore("done_" + n)) for n in ("pe", "act", "dve", "pool", "sp"))
        self.lanes = [self.pe, self.act, self.dve, self.pool, self.sp]
        self.bank_at = 0
        self.bank_free = [[] for _ in range(8)]
        self.reserved = set()

    def semaphore(self, name):
        return self.ctx.enter_context(self.nc.semaphore(name))

    def counter(self, name, step=16):
        return Counter(self.semaphore(name), step)

    def meet(self, *extra):
        marks = [lane.done.now() for lane in self.lanes[:4]]
        for lane in self.lanes[:4]:
            lane.wait(*marks, *extra)
        self.bank_free = [[] for _ in range(8)]

    def bank(self):
        while self.bank_at in self.reserved:
            self.bank_at = (self.bank_at + 1) % 8
        b = self.bank_at
        self.bank_at = (b + 1) % 8
        assert self.bank_free[b] is not None, "its readers aren't queued yet"
        self.pe.wait(*self.bank_free[b])
        self.bank_free[b] = None
        return b

    def loop_begin(self, *shape):
        assert self.loop is None
        self.loop = Loop(shape)
        self.outer = [lane.items for lane in self.lanes]
        for lane in self.lanes:
            lane.items, lane.waited = [], {}
            if lane.in_order:
                lane.last = Later()
                lane.wait(lane.last)
        return self.loop

    def loop_end(self):
        loop, self.loop = self.loop, None
        for lane in self.lanes:
            if lane.in_order:
                lane.last.set(lane.done.now())
        for c in loop.counters:
            loop.frames[c] = (c.base, c.n)
            c.per, c.n, c.loop = c.n, c.base + c.n * loop.trips, None
        for lane, items in zip(self.lanes, self.outer):
            body, lane.items, lane.waited = lane.items, items, {}
            if body:
                items.append(("loop", loop, body))

    def branch_begin(self, name):
        self.saved = [(lane.items, lane.done, lane.waited) for lane in self.lanes]
        for lane in self.lanes:
            lane.items, lane.waited = [], {}
            lane.done = Counter(self.semaphore(name + "_" + lane.name))

    def branch_end(self, flag):
        for lane, (items, done, waited) in zip(self.lanes, self.saved):
            body, lane.items, lane.done, lane.waited = lane.items, items, done, waited
            items.append(("if", flag, body))


class Ring:

    def __init__(self, g):
        self.g = g
        nc = g.nc
        self.slots = [g.ctx.enter_context(nc.sbuf_tensor(f"ring_{i}", [P, SLOT], F32)) for i in range(RING)]
        self.landed = [g.counter(f"landed_{i}") for i in range(RING)]
        self.frees = [g.counter(f"ring_free_{i}", 1) for i in range(RING)]
        self.free = None
        self.total, self.loop, self.here = 0, None, 0

    def load(self, *pieces):
        g = self.g
        if g.loop is not self.loop:
            self.total += self.here * (self.loop.trips if self.loop else 1)
            self.loop, self.here = g.loop, 0
        number = self.total + self.here
        slot = number % RING
        self.free = self.frees[slot]
        if g.loop is not None:
            assert self.here < RING
            self.free.enter(g.loop)
        else:
            assert self.free.n == number // RING, "the slot's last reader isn't queued yet"
        if number >= RING:
            g.sp.items.append(("wait", self.free.now(), 0))
        views = []
        for shape, first, source, *part in pieces:
            n = int(np.prod(shape))
            view = self.slots[slot][:, first:first + n]
            if len(shape) > 1:
                names = " ".join("abc"[:len(shape)])
                view = view.rearrange(f"p ({names}) -> p {names}", **dict(zip("abc", shape[:-1])))
            to = part[0](view) if part else view
            mark = g.sp.do(lambda e, i, v=to, s=source: e.dma_start(v, s(i)), inc=self.landed[slot])
            views.append(view)
        self.here += 1
        return views, mark


class Arena:

    def __init__(self, tensor, size):
        self.tensor, self.size, self.at = tensor, size, 0

    def take(self, *shape):
        n = int(np.prod(shape))
        view = self.tensor[:, self.at:self.at + n]
        self.at += n
        assert self.at <= self.size, (self.at, self.size)
        if len(shape) > 1:
            names = " ".join("abc"[:len(shape)])
            view = view.rearrange(f"p ({names}) -> p {names}", **dict(zip("abc", shape[:-1])))
        return view


def along(ap, n):
    return ap.unsqueeze(len(ap.shape)).broadcast_to([*ap.shape, n])


def across(ap, n, dim=1):
    shape = list(ap.shape)
    return ap.unsqueeze(dim).broadcast_to([*shape[:dim], n, *shape[dim:]])


class Modulation:

    def __init__(self, k, layer, first=0):
        self.k, self.layer, self.first, self.at = k, layer, first, first
        self.rows, self.rows_free, self.waiting = [], [], None
        self.bank = k.g.bank()
        k.g.reserved.add(self.bank)

    def use(self, rows, *marks):
        self.turn_last()
        self.rows, self.rows_free = rows, [None, None]
        self.k.act.wait(*marks)

    def steps(self, n):
        k, g = self.k, self.k.g
        for _ in range(n):
            at = self.at
            self.at += 1
            w, landed = k.weights(k.a["w_mod"][self.layer], KD, at * 512, 512)
            b = g.bank()
            end = k.product(k.psum[b][0:2, :], lambda i: k.silu_cond[:, i, :], lambda i: w[:, i, :], KD,
                            last=k.ring.free, wait=(landed,))
            row = self.rows[at % 2]
            m = k.copy(k.act, row[0:2, :], k.psum[b][0:2, :], end, self.rows_free[at % 2])
            g.bank_free[b] = [m]
            self.turn_last()
            self.waiting = (at, row, m)

    def turn_last(self):
        k = self.k
        if self.waiting is None:
            return
        at, row, m = self.waiting
        for t in range(4):
            tile = (4 * at + t) * 2
            self.end = k.turn(k.psum[self.bank][:, tile:tile + 2], row[0:2, t * P:(t + 1) * P], rows=2,
                              mark=t == 3, wait=(m,))
        self.rows_free[at % 2] = self.end
        self.waiting = None

    def close(self):
        k, g = self.k, self.k.g
        self.turn_last()
        tiles = slice(4 * self.first, 4 * self.at)
        out = k.psum[self.bank][:, 2 * tiles.start:2 * tiles.stop].rearrange("p (m c) -> p m c", c=2)
        mod = k.mod[:, self.layer, :, :]
        m = k.tt(k.dve, mod[:, tiles, :], out, along(k.col("b_mod")[:, self.layer, tiles], 2), ALU.add, self.end)
        g.bank_free[self.bank] = [m]
        g.reserved.remove(self.bank)
        for which, (j, norm) in enumerate(((1, "norm_mix"), (4, "norm_ffn"))):
            if tiles.start <= j * KD and (j + 1) * KD <= tiles.stop:
                k.stt(k.gain[:, self.layer, which, :, :], mod[:, j * KD:(j + 1) * KD, :], 1.0,
                      along(k.col(norm)[:, self.layer, :], 2), ALU.add, ALU.mult, chain=True)
        k.mod_made = m


class Squares:

    def __init__(self, k, T, buffers, *marks):
        self.k, self.T, self.buffers, self.free = k, T, buffers, [None, None]
        self.made, self.bank, self.waiting = 0, None, None
        k.act.wait(*marks)

    def square(self, buf, src, products, mark):
        s = self.made % 2
        self.made += 1
        squares = self.k.fn(buf, src, ACT.Square, mark, self.free[s])
        self.add_last()
        self.waiting = (s, products, squares)

    def tile(self, m, mark):
        T, buf = self.T, self.buffers[self.made % 2]
        self.square(buf[:, 0:T], self.k.X[:, m, 0:T], [(slice(0, T), buf[:, 0:T], m == 0, m == KD - 1)], mark)

    def tokens(self, t, mark):
        buf, cols = self.buffers[self.made % 2], slice(t * P, (t + 1) * P)
        self.square(buf, self.k.X[:, :, cols], [(cols, buf[:, i, :], i == 0, i == KD - 1) for i in range(KD)], mark)

    def add_last(self):
        if self.waiting is None:
            return
        s, products, squares = self.waiting
        k = self.k
        if self.bank is None:
            self.bank = k.g.bank()
            k.g.reserved.add(self.bank)
        for cols, rhs, start, stop in products:
            self.end = k.mm(k.psum[self.bank][:, cols], k.mat(f"ones_{D}"), rhs, start, stop, mark=True, wait=(squares,))
        self.free[s], self.waiting = self.end, None

    def close(self):
        k = self.k
        self.add_last()
        k.g.reserved.remove(self.bank)
        k.stat = k.inverse_root(self.bank, self.T, NORM_EPS, self.end)


class Kernel:
    def __init__(self, nc, ctx, a, stop=None):
        self.nc, self.a, self.stop = nc, a, stop
        self.g = g = Program(nc, ctx)
        self.pe, self.act, self.dve, self.pool, self.sp = g.lanes
        self.ring = Ring(g)

        def sb(name, shape, dt=F32):
            return ctx.enter_context(nc.sbuf_tensor(name, shape, dt))

        self.sb = sb
        self.psum = [ctx.enter_context(nc.psum_tensor(f"bank_{i}", [P, BANK], F32)) for i in range(8)]
        self.layout, ncol = column_layout()
        self.row_at, nrow = row_layout()
        self.cols, self.rows = sb("cols", [P, ncol]), sb("rows", [P, nrow])
        self.mats = sb("mats", [P, len(MATS), P])
        self.X = sb("residual", [P, KD, SEQ + CTX])
        self.A = sb("normed", [P, KD, SEQ + CTX])
        self.rstd = sb("rstd", [P, SEQ + CTX])
        self.mod = sb("mod", [P, 2, N_MOD * KD, 2])
        self.gain = sb("gain", [P, 2, 2, KD, 2])
        self.arena_size = 17600
        self.arena_tensor = sb("arena", [P, self.arena_size])
        self.loads = g.counter("loads")
        self.stat = None

    def col(self, name):
        at, shape = self.layout[name]
        view = self.cols[:, at:at + int(np.prod(shape))]
        if len(shape) > 1:
            names = " ".join("abc"[:len(shape)])
            view = view.rearrange(f"p ({names}) -> p {names}", **dict(zip("abc", shape[:-1])))
        return view

    def row(self, name):
        at, n = self.row_at[name]
        return self.rows[:, at:at + n]

    def mat(self, name):
        return self.mats[:, MATS.index(name), :]

    def stage(self):
        self.g.meet()
        return Arena(self.arena_tensor, self.arena_size)

    def fetch(self, out, source, *marks, lane=None):
        return (lane or self.act).do(lambda e, i: e.dma_start(out, source), *marks, inc=self.loads)

    def mm(self, out, lhsT, rhs, start, stop, mark=False, inc=None, wait=(), shared=False):
        return self.pe.do(lambda e, i: e.matmul(out, lhsT, rhs, start=start, stop=stop, skip_group_check=shared),
                          *wait, inc=inc, mark=mark)

    def product(self, out, lhs, rhs, n_k, last=None, wait=(), tiles=None):
        self.pe.wait(*wait)
        for k in range(n_k):
            self.pe.wait(*(tiles[k:k + 1] if tiles else ()))
            end = k == n_k - 1
            m = self.mm(out, lhs(k), rhs(k), k == 0, end, mark=end, inc=last if end else None)
        return m

    def turn(self, out, in_, rows=P, mark=False, wait=()):
        return self.pe.do(lambda e, i: e.transpose(out, in_, self.mats[0:rows, 0, 0:rows]), *wait, mark=mark)

    def tt(self, lane, out, a, b, op, *marks, chain=False):
        f = lane.chain if chain else lane.do
        return f(lambda e, i: e.tensor_tensor(out, a, b, op), *marks)

    def ts(self, lane, out, a, s1, s2, op0, op1, *marks, chain=False):
        f = lane.chain if chain else lane.do
        if s2 is None:
            return f(lambda e, i: e.tensor_scalar(out, a, s1, None, op0), *marks)
        return f(lambda e, i: e.tensor_scalar(out, a, s1, s2, op0, op1), *marks)

    def stt(self, out, a, s, b, op0, op1, *marks, chain=False):
        f = self.dve.chain if chain else self.dve.do
        return f(lambda e, i: e.scalar_tensor_tensor(out, a, s, b, op0, op1), *marks)

    def fn(self, out, a, func, *marks, bias=0.0, scale=1.0, total=None, chain=False):
        f = self.act.chain if chain else self.act.do
        return f(lambda e, i: e.activation(out, a, func, bias=bias, scale=scale, accum_out=total), *marks)

    def copy(self, lane, out, a, *marks, chain=False):
        f = lane.chain if chain else lane.do
        if lane is self.act:
            return f(lambda e, i: e.activation(out, a, ACT.Copy), *marks)
        return f(lambda e, i: e.tensor_copy(out, a), *marks)

    def mean_square(self, src, n_k, T, width, eps, scratch, *marks):
        g, b = self.g, self.g.bank()
        out = self.psum[b][:, 0:T]
        ones = self.mat(f"ones_{width}")
        for k in range(n_k):
            m = self.fn(scratch[:, k, 0:T], src[:, k, 0:T], ACT.Square, *marks)
            end = self.mm(out, ones, scratch[:, k, 0:T], k == 0, k == n_k - 1, mark=k == n_k - 1, wait=(m,))
        return self.inverse_root(b, T, eps, end)

    def inverse_root(self, b, T, eps, end):
        m = self.ts(self.dve, self.rstd[:, 0:T], self.psum[b][:, 0:T], eps, None, ALU.add, None, end)
        self.g.bank_free[b] = [m]
        m = self.fn(self.rstd[:, 0:T], self.rstd[:, 0:T], ACT.Sqrt, m)
        return self.dve.do(lambda e, i: e.reciprocal(self.rstd[:, 0:T], self.rstd[:, 0:T]), m)

    def scaled(self, dst, src, gain, T, n_k, stat):
        return [self.stt(dst[:, k, 0:T], src[:, k, 0:T], gain[:, k:k + 1], self.rstd[:, 0:T],
                         ALU.mult, ALU.mult, stat) for k in range(n_k)]

    def residual_stat(self, T, scratch):
        stat, self.stat = self.stat, None
        return stat or self.mean_square(self.X, KD, T, D, NORM_EPS, scratch)

    def modulated(self, layer, which, T, between=lambda: None):
        stat = self.residual_stat(T, self.A)
        stat_pe = self.pe.done.now()
        between()
        self.act.wait(self.mod_made)
        shift = 0 if which == 0 else 3
        marks = []
        for k in range(KD):
            for c in range(T // SEQ):
                cols = slice(c * SEQ, (c + 1) * SEQ)
                m = self.stt(self.A[:, k, cols], self.X[:, k, cols], self.gain[:, layer, which, k, c:c + 1],
                             self.rstd[:, cols], ALU.mult, ALU.mult, stat, stat_pe)
                last = self.fn(self.A[:, k, cols], self.A[:, k, cols], ACT.Identity, m,
                               bias=self.mod[:, layer, shift * KD + k, c:c + 1])
            marks.append(last)
        return marks

    def simple_norm(self, gain, dst=None, T=SEQ):
        dst = self.A if dst is None else dst
        stat = self.residual_stat(T, dst)
        return self.scaled(dst, self.X, gain, T, KD, stat)

    def weights(self, source, n_k, first, n):
        w = source.rearrange("(k p) n -> p k n", p=P)[:, :, first:first + n]
        (view,), mark = self.ring.load(((n_k, n), 0, lambda i: w))
        return view, mark

    def linear(self, source, n_k, n_out, rhs, T, evac, *marks, width=512, inputs=None):
        for first in range(0, n_out, width):
            w, landed = self.weights(source, n_k, first, min(width, n_out - first))
            tiles = min(width, n_out - first) // P
            for t in range(tiles):
                b = self.g.bank()
                out = self.psum[b][:, 0:T]
                m = self.product(out, lambda k: w[:, k, t * P:(t + 1) * P], rhs, n_k,
                                 last=self.ring.free if t == tiles - 1 else None, wait=(landed, *marks),
                                 tiles=inputs)
                self.g.bank_free[b] = [evac(first // P + t, out, m)]

    def add_gated(self, layer, j, squares):
        def evac(m, out, mark):
            for c in range(out.shape[1] // SEQ):
                cols = slice(c * SEQ, (c + 1) * SEQ)
                last = self.stt(self.X[:, m, cols], out[:, cols], self.mod[:, layer, j * KD + m, c:c + 1],
                                self.X[:, m, cols], ALU.mult, ALU.add, mark)
            squares.tile(m, last)
            return last
        return evac

    def add_plain(self, squares):
        def evac(m, out, mark):
            last = self.tt(self.dve, self.X[:, m, 0:SEQ], out, self.X[:, m, 0:SEQ], ALU.add, mark)
            squares.tile(m, last)
            return last
        return evac

    def squares(self, *marks):
        return Squares(self, SEQ, [self.rstd[:, 0:SEQ], self.rstd[:, SEQ:]], self.dve.done.now(), *marks)

    def start(self):
        a = self.a
        self.fetch(self.cols[:, :], a["cols"])
        self.fetch(self.mats[:, :, :], a["mats"])
        self.fetch(self.rows[:, :], a["rows"].broadcast_to([P, a["rows"].shape[1]]))
        self.fetch(self.X[:, :, 0:SEQ], a["xT"].rearrange("(k p) t -> p k t", p=P), lane=self.sp)
        m = self.fetch(self.X[:, :, SEQ:SEQ + CTX], a["ctxT"].rearrange("(k p) t -> p k t", p=P), lane=self.sp)
        for lane in (self.pe, self.act, self.dve, self.pool):
            lane.wait(m)
        cond = self.col("cond")
        self.silu_cond = self.sb("silu_cond", [P, KD, 2])
        self.pe.wait(self.fn(self.silu_cond[:, :, :], cond, ACT.Silu))

    def mla(self):
        g, a, T = self.g, self.a, SEQ + CTX
        ar = self.stage()
        CQ = ar.take(4, T)
        ar.at = 0
        score_buf = [ar.take(BANK) for _ in range(4)]
        CKV, KPE, QN, QR = ar.take(2, T), ar.take(2, T), ar.take(MLA_HEADS, T), ar.take(MLA_HEADS // 2, T)
        V, KN, PT = ar.take(4, MLA_HEADS * P), ar.take(2, T), ar.take(4, SEQ)
        PTC = ar.take(2, CTX)
        tables_both, rot = ar.take(2 * SEQ), ar.take(P)
        cos, sin = tables_both[:, 0:SEQ], tables_both[:, SEQ:2 * SEQ]
        small = ar.take(3, 8)
        raw = KN[:, 0, :]
        tables = self.fetch(cos, a["tables"][:, 0:SEQ], self.act.done.now(), self.dve.done.now(), self.pe.done.now())
        self.fetch(sin, a["tables"][:, SEQ:2 * SEQ])
        tables = self.fetch(rot, a["tables"][:, 2 * SEQ:2 * SEQ + P])
        scale = float(MLA_NOPE + MLA_ROPE) ** -0.5
        zero = self.pool.do(lambda e, i: e.memset(KPE, 0.0))
        halves = lambda v: [v.rearrange("p a b -> p (a b)")[:, n * 512:(n + 1) * 512] for n in range(2)]
        first = Modulation(self, 0)
        first.use(halves(PT))

        def shift_and_scale():
            first.steps(4)
            first.close()
        ready = self.modulated(0, 0, T, shift_and_scale)
        rest = Modulation(self, 0, first=4)
        rest.use(halves(PT), self.pe.done.now())
        rhs = lambda k: self.A[:, k, :]

        self.linear(a["mla_w_dq"][0], KD, MLA_Q_LORA, rhs, T,
                    lambda m, out, mark: self.copy(self.dve, CQ[:, m, :], out, mark), inputs=ready)
        wd = a["mla_w_dkv"][0].rearrange("(k p) n -> p k n", p=P)
        n_kv = MLA_KV_LORA
        pe_cols = lambda i: wd[:, :, n_kv:n_kv + MLA_ROPE]
        (w, w_pe, _), landed = self.ring.load(
            ((KD, n_kv), 0, lambda i: wd[:, :, 0:n_kv]),
            ((KD, P), KD * n_kv, pe_cols, lambda v: v[:, :, 0:MLA_ROPE]),
            ((KD, P), KD * n_kv, pe_cols, lambda v: v[:, :, MLA_ROPE:P]))
        for m in range(3):
            b = g.bank()
            out = self.psum[b][:, :]
            if m < 2:
                end = self.product(out, lambda k: w[:, k, m * P:(m + 1) * P], rhs, KD, wait=(landed,))
                g.bank_free[b] = [self.copy(self.dve, CKV[:, m, :], out, end)]
            else:
                end = self.product(out, lambda k: w_pe[:, k, :], rhs, KD, last=self.ring.free)
                k_raw = self.copy(self.act, raw, out, end)
                g.bank_free[b] = [k_raw]

        kv_done, squares_read = self.dve.done.now(), None
        for buf, n_k, gain in ((CQ, 4, "g_q"), (CKV, 2, "g_kv")):
            stat = self.mean_square(buf, n_k, T, n_k * P, NORM_EPS, QN, kv_done, squares_read)
            rest.steps(1)
            *_, done = self.scaled(buf, buf, self.col(gain), T, n_k, stat)
            squares_read = self.pe.done.now()
        self.act.wait(squares_read)
        self.dve.wait(squares_read)

        def rotate(src, mark):
            b = g.bank()
            out = self.psum[b][:, 0:SEQ]
            end = self.mm(out, rot, src[:, 0:SEQ], True, True, mark=True, wait=(mark, tables))
            m = self.tt(self.dve, turned[:, :], out, sin, ALU.mult, end, chain=True)
            g.bank_free[b] = [m]
            m2 = self.tt(self.dve, src[:, 0:SEQ], src[:, 0:SEQ], cos, ALU.mult, end)
            return self.tt(self.dve, src[:, 0:SEQ], src[:, 0:SEQ], turned[:, :], ALU.add, chain=True)

        turned = self.rstd[:, 0:SEQ]
        k_rot = rotate(raw, k_raw)
        half = MLA_ROPE
        self.copy(self.dve, KPE[0:half, 0, :], raw[0:half, :], zero, k_rot)
        k_pe = self.copy(self.dve, KPE[half:P, 1, :], raw[half:P, :])

        hw = MLA_NOPE + MLA_ROPE
        wq = a["mla_w_uq"][0].rearrange("(k p) (h c) -> p k h c", p=P, c=hw)
        q_marks = []
        for c in range(2):
            pieces = []
            heads = slice(4 * c, 4 * c + 4)
            for k in range(4):
                pieces.append(((4, 768), 0, lambda i, k=k, heads=heads: wq[:, k, heads, 0:MLA_NOPE],
                               lambda v, k=k: v[:, k, 0:512].rearrange("p (h c) -> p h c", h=4)))
                pieces.append(((4, 768), 0, lambda i, k=k, heads=heads: wq[:, k, heads, MLA_NOPE:hw],
                               lambda v, k=k: v[:, k, 512:768].rearrange("p (h c) -> p h c", h=4)))
            (w, *_), landed = self.ring.load(*pieces)
            for t in range(6):
                b = g.bank()
                out = self.psum[b][:, :]
                end = self.product(out, lambda k: w[:, k, t * P:(t + 1) * P], lambda k: CQ[:, k, :], 4,
                                   last=self.ring.free if t == 5 else None, wait=(landed, done))
                dst = QN[:, 4 * c + t, :] if t < 4 else QR[:, 2 * c + t - 4, :]
                m = self.fn(dst, out, ACT.Copy, end, scale=scale)
                g.bank_free[b] = [m]
                if t >= 4:
                    m = rotate(dst, m)
                q_marks.append(m)
        self.pe.wait(self.act.done.now(), self.dve.done.now())

        rest.steps(1)

        wkv = a["mla_w_ukv"][0].rearrange("(k p) n -> p k n", p=P)
        (w,), landed = self.ring.load(((2, 2 * MLA_HEADS * P), 0, lambda i: wkv))
        w_heads = w.rearrange("p k (h j c) -> p k h j c", j=2, c=P)
        w_heads_free = self.ring.free
        for t in range(T // P):
            for n in range(2):
                b = g.bank()
                end = self.product(self.psum[b][:, :], lambda k: CKV[:, k, t * P:(t + 1) * P],
                                   lambda k: w_heads[:, k, 4 * n:4 * n + 4, 1, :], 2, wait=(landed,))
                v_mark = self.copy(self.act, V[:, t, n * 512:(n + 1) * 512], self.psum[b][:, :], end)
                g.bank_free[b] = [v_mark]

        OT = self.A
        score_free = [None] * 4
        kn_free = [k_pe, k_pe]
        pt_free = [None, None]

        def scores(h):
            b = g.bank()
            kn = KN[:, h % 2, :]
            end = self.product(self.psum[b][:, :], lambda k: w_heads[:, k, h, 0, :], lambda k: CKV[:, k, :], 2,
                               last=w_heads_free if h == MLA_HEADS - 1 else None)
            m = self.copy(self.dve, kn, self.psum[b][:, :], end, kn_free[h % 2])
            g.bank_free[b] = [m]
            self.pe.wait(m)
            probs = []
            for q in range(T // P):
                lat = q < SEQ // P
                keys = slice(0, T) if lat else slice(SEQ, T)
                n = T if lat else CTX
                if q != 3:
                    b = g.bank()
                    g.reserved.add(b)
                at = 0 if q != 3 else CTX
                out = self.psum[b][:, at:at + n]
                self.mm(out, QN[:, h, q * P:(q + 1) * P], kn[:, keys], True, False)
                end = self.mm(out, QR[:, h // 2, q * P:(q + 1) * P], KPE[:, h % 2, keys], False, True, mark=True)
                probs.append((q, b, out, n, end))
            kn_free[h % 2] = end
            return probs

        def softmax(probs):
            marks = []
            for q, b, out, n, e1 in probs:
                e1 = e1 if q < 2 else probs[3][4]
                buf = score_buf[q][:, 0:n]
                top, total, inv = small[:, 0, q:q + 1], small[:, 1, q:q + 1], small[:, 2, q:q + 1]
                m = self.dve.do(lambda e, i, o=top, s=out: e.tensor_reduce(o, s, AX.X, ALU.max, negate=True),
                                e1, self.act.done.now())
                m = self.fn(buf, out, ACT.Exp, m, score_free[q], bias=top, total=total)
                g.bank_free[b] = [m]
                g.reserved.discard(b)
                m = self.dve.do(lambda e, i, o=inv, s=total: e.reciprocal(o, s), m)
                marks.append(self.ts(self.dve, buf, buf, inv, None, ALU.mult, None, chain=True))
            return marks

        def values(h, marks):
            for q in range(2):
                b = g.bank()
                for k in range(4):
                    end = self.turn(self.psum[b][:, k * P:(k + 1) * P], score_buf[q][:, k * P:(k + 1) * P],
                                    mark=k == 3, wait=(marks[q],))
                score_free[q] = end
                m = self.copy(self.act, PT[:, :, q * P:(q + 1) * P],
                              self.psum[b][:, :].rearrange("p (k q) -> p k q", k=4), end, pt_free[0])
                g.bank_free[b] = [m]
            b = g.bank()
            for q in range(2):
                for k in range(2):
                    end = self.turn(self.psum[b][:, (2 * q + k) * P:(2 * q + k + 1) * P],
                                    score_buf[2 + q][:, k * P:(k + 1) * P], mark=k == 1, wait=(marks[2 + q],))
                score_free[2 + q] = end
            mc = self.copy(self.act, PTC.rearrange("p k (q c) -> p q k c", q=2),
                           self.psum[b][:, :].rearrange("p (q k c) -> p q k c", q=2, k=2), end, pt_free[1])
            g.bank_free[b] = [mc]
            b = g.bank()
            for k in range(4):
                self.mm(self.psum[b][:, 0:SEQ], V[:, k, h * P:(h + 1) * P], PT[:, k, :], k == 0, k == 3,
                        wait=(m, v_mark))
            for k in range(2):
                end = self.mm(self.psum[b][:, SEQ:T], V[:, 2 + k, h * P:(h + 1) * P], PTC[:, k, :], k == 0, k == 1,
                              mark=k == 1, wait=(mc,))
            pt_free[0] = pt_free[1] = end
            m = self.copy(self.dve, OT[:, h, :], self.psum[b][:, :], end)
            g.bank_free[b] = [m]
            return m

        rest.use([tables_both, self.rstd], self.dve.done.now())
        marks = softmax(scores(0))
        for h in range(MLA_HEADS):
            after = scores(h + 1) if h + 1 < MLA_HEADS else None
            rest.steps(1 if h < 5 else 0)
            out_mark = values(h, marks)
            marks = softmax(after) if after else None
        rest.close()
        squares = Squares(self, T, [tables_both, self.rstd], self.pe.done.now())
        self.linear(a["mla_w_o"][0], KD, D, lambda k: OT[:, k, :], T, self.add_gated(0, 2, squares), out_mark)
        squares.close()

    def conv_mixer(self):
        g, a, T = self.g, self.a, SEQ
        ar = self.stage()
        B, C, V, Z = ar.take(KD, T), ar.take(KD, T), ar.take(2, T + 2), ar.take(KD, T)
        pads = self.pool.do(lambda e, i: e.memset(V, 0.0))
        ready = self.modulated(1, 0, T)
        taps = self.col("conv_w")
        state = {0: pads, 1: pads}

        def evac(m, out, mark):
            part, m = divmod(m, KD)
            if part < 2:
                m = self.copy(self.act, (B, C)[part][:, m, :], out, mark)
                state["bc"] = m
                return m
            v = V[:, m % 2, :]
            end = self.tt(self.dve, v[:, 1:T + 1], out, C[:, m, :], ALU.mult, mark, state["bc"], state[m % 2])
            z = Z[:, m, :]
            self.ts(self.dve, z, v[:, 0:T], taps[:, m, 0:1], None, ALU.mult, None, chain=True)
            self.stt(z, v[:, 1:T + 1], taps[:, m, 1:2], z, ALU.mult, ALU.add, chain=True)
            self.stt(z, v[:, 2:T + 2], taps[:, m, 2:3], z, ALU.mult, ALU.add, chain=True)
            state["z"] = self.tt(self.dve, z, z, B[:, m, :], ALU.mult, chain=True)
            state[m % 2] = state["z"]
            return end

        self.linear(a["conv_w_in"][0], KD, 3 * D, lambda k: self.A[:, k, 0:T], T, evac, inputs=ready)
        squares = self.squares()
        self.linear(a["conv_w_out"][0], KD, D, lambda k: Z[:, k, :], T, self.add_gated(1, 2, squares), state["z"])
        squares.close()

    def first_max(self, score, order, n, tmp, out):
        top, eq = tmp
        nt = score.shape[1]
        self.dve.chain(lambda e, i: e.tensor_reduce(top, score, AX.X, ALU.max))
        self.tt(self.dve, eq, score, along(top, n), ALU.is_equal, chain=True)
        self.tt(self.dve, eq, eq, across(order, nt), ALU.mult, chain=True)
        self.dve.chain(lambda e, i: e.tensor_reduce(top, eq, AX.X, ALU.max))
        return self.tt(self.dve, out, eq, along(top, n), ALU.is_equal, chain=True)

    def moe(self, layer, T, cap):
        g, a, ring = self.g, self.a, self.ring
        NT = T // P
        n_blocks = -(-T // cap)
        f_rows = self.nc.dram_tensor(f"f_rows_{layer}", [T, D], F32, kind="Internal").ap()
        y_rows = self.nc.dram_tensor(f"y_rows_{layer}", [n_blocks * EXPERTS * cap, D], F32, kind="Internal").ap()
        s_yout = [g.counter(f"y_out_{layer}_{j}") for j in range(2)]
        s_gather = [g.counter(f"gather_{layer}_{j}") for j in range(2)]
        s_back = [g.counter(f"back_{layer}_{j}") for j in range(2)]

        ar = self.stage()
        index_i = ar.take(n_blocks * EXPERTS + 2).bitcast(I32)
        index_u = ar.take(2)
        weight = [ar.take(NT) for _ in range(2)]
        dest = [ar.take(NT) for _ in range(2)]
        flag = self.sb(f"flag_{layer}", [P, 1])
        pos = [ar.take(NT) for _ in range(2)]
        chosen = ar.take(2, NT * EXPERTS)
        work = ar.at
        W = ar.take(KD, GROUPS + EXPERTS)
        router = self.fetch(W[:, :, 0:GROUPS], a["moe_w_group"][layer].rearrange("(k p) n -> p k n", p=P),
                            *[l.done.now() for l in g.lanes[:4]])
        router = self.fetch(W[:, :, GROUPS:], a["moe_w_expert"][layer].rearrange("(k p) n -> p k n", p=P))
        ahead = Modulation(self, layer + 1) if layer == 0 else None

        def fill(n):
            if ahead:
                ahead.steps(n)
        if ahead:
            ahead.use([ar.take(512), ar.take(512)])
        ready = self.modulated(layer, 1, T)
        fill(2)

        n_log = GROUPS + EXPERTS
        b = g.bank()
        for t in range(NT):
            end = self.product(self.psum[b][:, t * n_log:(t + 1) * n_log], lambda k: self.A[:, k, t * P:(t + 1) * P],
                               lambda k: W[:, k, :], KD, wait=(router,), tiles=ready)
        logits = ar.take(NT, n_log)
        m_log = self.copy(self.dve, logits, self.psum[b][:, 0:NT * n_log].rearrange("p (t n) -> p t n", n=n_log), end)
        g.bank_free[b] = [m_log]

        rows = ar.take(2, D)
        sent = []
        for t in range(NT):
            for half in range(2):
                b = g.bank()
                for j in range(4):
                    end = self.turn(self.psum[b][:, j * P:(j + 1) * P],
                                    self.A[:, 4 * half + j, t * P:(t + 1) * P], mark=j == 3)
                at = rows[:, t % 2, half * 512:(half + 1) * 512]
                m = self.copy(self.act, at, self.psum[b][:, :], end, sent[t - 2] if t >= 2 else None)
                g.bank_free[b] = [m]
            sent.append(self.act.do(lambda e, i, t=t: e.dma_start(f_rows[t * P:(t + 1) * P, :], rows[:, t % 2, :]),
                                    m, inc=s_yout[t % 2]))
        rows_out = sent[-2:]

        bias = self.row(f"route_bias_{layer}")
        dve, act = self.dve, self.act

        def softmax(x, n, top, total):
            dve.chain(lambda e, i: e.tensor_reduce(top, x, AX.X, ALU.max))
            m = self.tt(dve, x, x, along(top, n), ALU.subtract, chain=True)
            m = self.fn(x, x, ACT.Exp, m)
            dve.chain(lambda e, i: e.tensor_reduce(total, x, AX.X, ALU.add), m)
            dve.chain(lambda e, i: e.reciprocal(total, total))
            self.tt(dve, x, x, along(total, n), ALU.mult, chain=True)

        def reduced(out, x):
            return dve.chain(lambda e, i: e.tensor_reduce(out, x, AX.X, ALU.add))

        gp, gs, g_hot = logits[:, :, 0:GROUPS], ar.take(NT, GROUPS), ar.take(NT, GROUPS)
        el = logits[:, :, GROUPS:].rearrange("p t (g e) -> p t g e", g=GROUPS)
        top, total, g_w = ar.take(NT), ar.take(NT), ar.take(NT)
        softmax(gp, GROUPS, top, total)
        self.tt(dve, gs, gp, across(bias[:, 0:GROUPS], NT), ALU.add, chain=True)
        eq4 = ar.take(NT, GROUPS)
        self.first_max(gs, self.row("first_4"), GROUPS, (top, eq4), g_hot)
        self.tt(dve, gs, gp, g_hot, ALU.mult, chain=True)
        reduced(g_w, gs)

        picked = ar.take(NT, EXPERTS).rearrange("p t (g e) -> p t g e", g=GROUPS)
        ep, e_bias, e_sc, eq8 = (ar.take(NT, PER_GROUP) for _ in range(4))
        hot = [ar.take(NT, PER_GROUP) for _ in range(2)]
        wide_hot = along(g_hot, PER_GROUP)
        e_rows = across(bias[:, GROUPS:].rearrange("p (g e) -> p g e", g=GROUPS), NT)
        for src, out in ((el, ep), (e_rows, e_bias)):
            self.tt(dve, picked, src, wide_hot, ALU.mult, chain=True)
            reduced(out, picked.rearrange("p t g e -> p t e g"))
        softmax(ep, PER_GROUP, top, total)
        self.tt(dve, e_sc, ep, e_bias, ALU.add, chain=True)
        self.first_max(e_sc, self.row("first_8"), PER_GROUP, (top, eq8), hot[0])
        self.ts(dve, eq8, hot[0], -1.0, 1.0, ALU.mult, ALU.add, chain=True)
        self.tt(dve, e_sc, e_sc, eq8, ALU.mult, chain=True)
        self.stt(e_sc, hot[0], -BIG, e_sc, ALU.mult, ALU.add, chain=True)
        self.first_max(e_sc, self.row("first_8"), PER_GROUP, (top, eq8), hot[1])
        for j in range(2):
            self.tt(dve, eq8, ep, hot[j], ALU.mult, chain=True)
            reduced(weight[j], eq8)
        self.tt(dve, total, weight[0], weight[1], ALU.add, chain=True)
        dve.chain(lambda e, i: e.reciprocal(total, total))
        self.tt(dve, total, total, g_w, ALU.mult, chain=True)
        for j in range(2):
            self.tt(dve, weight[j], weight[j], total, ALU.mult, chain=True)
        for j in range(2):
            out = chosen[:, j, :].rearrange("p (t g e) -> p t g e", t=NT, g=GROUPS)
            self.tt(dve, out, wide_hot, across(hot[j], GROUPS, 2), ALU.mult, chain=True)
        both = ar.take(NT, EXPERTS)
        flat = both.rearrange("p t e -> p (t e)")
        m_both = self.tt(dve, flat, chosen[:, 0, :], chosen[:, 1, :], ALU.add, chain=True)

        fill(5)

        b = g.bank()
        for t in range(NT):
            out = self.psum[b][:, t * EXPERTS:(t + 1) * EXPERTS]
            for s in range(t):
                self.mm(out, self.mat("ones"), both[:, s, :], s == 0, False, wait=(m_both,))
            self.mm(out, self.mat("before"), both[:, t, :], t == 0, True, wait=(m_both,))
        out = self.psum[b][:, NT * EXPERTS:(NT + 1) * EXPERTS]
        for t in range(NT):
            end = self.mm(out, self.mat("ones"), both[:, t, :], t == 0, t == NT - 1, mark=t == NT - 1)
        ranks, loads = ar.take(NT, EXPERTS), ar.take(EXPERTS)
        self.copy(dve, ranks.rearrange("p t e -> p (t e)"), self.psum[b][:, 0:NT * EXPERTS], end)
        m = self.copy(dve, loads, out)
        g.bank_free[b] = [m]
        most = ar.take(1)
        dve.chain(lambda e, i: e.tensor_reduce(most, loads, AX.X, ALU.max))
        self.ts(dve, most, most, -float(cap), 0.0, ALU.add, ALU.max, chain=True)
        flag_mark = self.copy(dve, flag[:, :].bitcast(I32), most, chain=True)
        tmp = ar.take(NT, EXPERTS)
        step = ar.take(NT)
        count = self.row("count")
        for j in range(2):
            mine = chosen[:, j, :].rearrange("p (t e) -> p t e", t=NT)
            self.tt(dve, tmp, ranks, mine, ALU.mult, chain=True)
            reduced(pos[j], tmp)
            self.tt(dve, tmp, mine, across(count[:, 0:EXPERTS], NT), ALU.mult, chain=True)
            reduced(step, tmp)
            self.stt(dest[j], step, float(cap), pos[j], ALU.mult, ALU.add, chain=True)
            for n in range(1, n_blocks):
                self.ts(dve, step, pos[j], float(n * cap), float((EXPERTS - 1) * cap), ALU.is_ge, ALU.mult, chain=True)
                self.tt(dve, dest[j], dest[j], step, ALU.add, chain=True)
            self.copy(dve, dest[j].bitcast(I32), dest[j], chain=True)

        fill(3)

        slot = ar.take(2, NT * cap)
        named = ar.take(2, NT * EXPERTS)
        for j in range(2):
            for t in range(NT):
                mine = chosen[:, j, t * EXPERTS:(t + 1) * EXPERTS]
                self.ts(dve, named[:, j, t * EXPERTS:(t + 1) * EXPERTS], mine, self.col("token")[:, t:t + 1], None,
                        ALU.mult, None)

        def index_block(n):
            for j in range(2):
                for t in range(NT):
                    m = self.ts(dve, slot[:, j, t * cap:(t + 1) * cap], count[:, 0:cap], float(n * cap),
                                pos[j][:, t:t + 1], ALU.add, ALU.is_equal, chain=True)
            b = g.bank()
            out = self.psum[b][0:cap, 0:EXPERTS]
            for j in range(2):
                for t in range(NT):
                    last = j == 1 and t == NT - 1
                    end = self.mm(out, slot[:, j, t * cap:(t + 1) * cap], named[:, j, t * EXPERTS:(t + 1) * EXPERTS],
                                  j == 0 and t == 0, last, mark=last, wait=(m,))
            m = self.copy(dve, index_i[0:cap, n * EXPERTS:(n + 1) * EXPERTS], out, end)
            g.bank_free[b] = [m]
            return m
        zeroed = self.pool.do(lambda e, i: e.memset(index_i, 0))
        self.dve.wait(zeroed)
        index_mark = index_block(0)

        fill(2)
        if ahead:
            ahead.close()

        keep = ar.at
        xe, xt = ar.take(2, D), ar.take(2, KD * cap)
        ht, yb, act_h = ar.take(2, KF * cap), ar.take(2, D), ar.take(KF * cap)
        gate, up = (a[n][layer].rearrange("x (p k) n -> x p k n", p=P) for n in ("moe_w_gate", "moe_w_up"))
        down = a["moe_w_down"][layer].rearrange("x (p k) n -> x p k n", p=P)
        index_buf = index_u.bitcast(I32)
        offset = bass.IndirectOffsetOnAxis
        per_bank = min(KD, BANK // cap)
        n_turned = -(-KD // per_bank)

        def gather(j, column, counter, *marks):
            m = self.pool.do(lambda e, i: e.tensor_copy(index_buf[0:cap, j:j + 1], index_i[0:cap, column(i)]), *marks)
            self.pool.items.append(("op", lambda e, i: e.drain(), None))
            return self.pool.do(lambda e, i: e.indirect_dma_start(
                out=xe[0:cap, j, :], out_offset=None, in_=f_rows,
                in_offset=offset(ap=index_buf[0:cap, j:j + 1].bitcast(U32), axis=0)), inc=counter, loose=True)

        def turned(j, gathered, banks, *marks):
            self.pe.wait(*marks)
            for n, b in enumerate(banks):
                lo, hi = n * per_bank, min(KD, (n + 1) * per_bank)
                for k in range(lo, hi):
                    end = self.turn(self.psum[b][:, (k - lo) * cap:(k - lo + 1) * cap],
                                    xe[0:cap, j, :].rearrange("c (p k) -> c k p", k=KD)[:, k, :], rows=cap, mark=k == hi - 1, wait=(gathered,))
                m = self.copy(dve, xt[:, j, lo * cap:hi * cap], self.psum[b][:, 0:(hi - lo) * cap], end)
            return m, end

        def expert(j, x_ready, w, landed, frees, between, h_before, y_before, stored):
            bg, bu, b0, b1 = 4, 5, 6, 7
            self.pe.wait(x_ready, h_before)
            ends = []
            for which, b in ((0, bg), (1, bu)):
                for n in range(KF):
                    ends.append(self.product(self.psum[b][:, n * cap:(n + 1) * cap],
                                lambda k: w[which][:, k, :].rearrange("p (f n) -> p n f", n=KF)[:, n, :],
                                lambda k: xt[:, j, k * cap:(k + 1) * cap], KD,
                                last=frees[which] if n == KF - 1 else None, wait=(landed[which],)))
            hs = ht[:, j, :]
            m = self.fn(act_h, self.psum[bg][:, 0:KF * cap], ACT.Silu, ends[KF - 1], h_before)
            h_ready = self.tt(dve, hs, act_h, self.psum[bu][:, 0:KF * cap], ALU.mult, m, ends[-1])
            between()
            self.pe.wait(landed[2], h_ready, *y_before)
            out = []
            for n, (b, lane) in enumerate(((b0, dve), (b1, act))):
                end = self.product(self.psum[b][0:cap, :], lambda k: hs[:, k * cap:(k + 1) * cap],
                                   lambda k: w[2][:, k, n * 512:(n + 1) * 512], KF, last=frees[2] if n else None)
                out.append(self.copy(lane, yb[0:cap, j, n * 512:(n + 1) * 512], self.psum[b][0:cap, :], end, stored))
            return h_ready, tuple(out)

        def store(j, row, counter, *marks):
            return act.do(lambda e, i: e.dma_start(y_rows[row(i), :], yb[0:cap, j, :]), *marks, inc=counter)

        tb = [[0, 1][:n_turned], [2, 3][:n_turned]]
        g.meet(*rows_out)
        gathered = gather(0, lambda i: slice(0, 1), s_gather[0], index_mark)
        turned(0, gathered, tb[0])
        gather(1, lambda i: slice(1, 2), s_gather[1])
        g.meet()

        g.loop_begin(EXPERTS // 2)
        carried = {n: Later() for n in ("gathered1", "x_ready0", "turned0", "h1", "y1a", "y1b", "store0", "store1")}
        wait_for = [dict(h_before=carried["h1"], y_before=(carried["y1a"], carried["y1b"]), stored=carried["store0"]),
                    None]
        x_ready = [carried["x_ready0"], None]
        gathered0 = gather(0, lambda i: bass.ds(i[0] * 2 + 2, 1), s_gather[0], carried["turned0"])
        for j in range(2):
            pieces, landed, frees = [], [], []
            for view, shape in ((gate, (KD, FF)), (up, (KD, FF)), (down, (KF, D))):
                (v,), mark = ring.load((shape, 0, lambda i, view=view, j=j:
                                        view[bass.ds(i[0] * 2 + j, 1)].rearrange("x p k n -> p (x k) n")))
                pieces.append(v)
                landed.append(mark)
                frees.append(ring.free)

            def between(j=j):
                if j == 0:
                    x_ready[1], _ = turned(1, carried["gathered1"], tb[1])
                else:
                    m, end = turned(0, gathered0, tb[0])
                    carried["x_ready0"].set(m)
                    carried["turned0"].set(end)

            h, y = expert(j, x_ready[j], pieces, landed, frees, between, **wait_for[j])
            stored = store(j, lambda i, j=j: bass.ds(i[0] * (2 * cap) + j * cap, cap), s_yout[j], *y)
            carried[f"store{j}"].set(stored)
            if j == 0:
                carried["gathered1"].set(gather(1, lambda i: bass.ds(i[0] * 2 + 3, 1), s_gather[1], x_ready[1]))
                wait_for[1] = dict(h_before=h, y_before=y, stored=carried["store1"])
            else:
                carried["h1"].set(h)
                carried["y1a"].set(y[0])
                carried["y1b"].set(y[1])
        g.loop_end()
        y_out = [s_yout[0].now(), s_yout[1].now()]
        g.meet(*y_out, s_gather[0].now(), s_gather[1].now())

        all_free = [f.now() for f in ring.frees]
        before = [lane.done.now() for lane in g.lanes[:4]]
        name = f"more_{layer}"
        for lane in g.lanes:
            lane.wait(flag_mark)
        g.branch_begin(name)
        banks_before, g.bank_free = g.bank_free, [[] for _ in range(8)]
        self.sp.wait(*all_free, *before)
        for n in range(1, n_blocks):
            index_block(n)
        self.copy(act, act_h[:, 0:1], self.col("token")[:, 0:1])
        self.pool.do(lambda e, i: e.memset(xe, 0.0))
        marks = [lane.done.now() for lane in g.lanes[:4]]
        for lane in g.lanes:
            lane.wait(*marks)
        m_landed, m_gather, m_out = (g.counter(f"{name}_{n}") for n in ("landed", "gathered", "y_out"))
        g.loop_begin(n_blocks - 1, EXPERTS)
        products_before = Later()
        self.sp.wait(products_before)
        linear_index = lambda i: i[0] * EXPERTS + i[1]
        views = []
        for slot_no, (view, shape) in enumerate(((gate, (KD, FF)), (up, (KD, FF)), (down, (KF, D)))):
            v = ring.slots[slot_no][:, :].rearrange("p (k n) -> p k n", k=shape[0])
            landed = self.sp.do(lambda e, i, v=v, view=view: e.dma_start(
                v, view[bass.ds(i[1], 1)].rearrange("x p k n -> p (x k) n")), inc=m_landed)
            views.append(v)
        gathered = gather(0, lambda i: bass.ds(linear_index(i) + EXPERTS, 1), m_gather)
        x_mark, _ = turned(0, gathered, tb[0])
        h, y = expert(0, x_mark, views, [landed] * 3, [None] * 3, lambda: None, None, (), None)
        out = store(0, lambda i: bass.ds(linear_index(i) * cap + EXPERTS * cap, cap), m_out, *y)
        products_before.set(self.pe.done.now())
        marks = [lane.done.now() for lane in g.lanes[:4]]
        for lane in g.lanes[:4]:
            lane.wait(*marks, out, gathered)
        g.loop_end()
        g.bank_free = banks_before
        g.branch_end(flag[0:1, 0:1].bitcast(I32))

        ar.at = keep
        ga = [[ar.take(D) for _ in range(2)] for _ in range(2)]
        self.pool.wait(*y_out)
        squares = Squares(self, SEQ, [ar.take(KD, P), ar.take(KD, P)])
        free = [None, None]
        for t in range(NT):
            pair = ga[t % 2]
            for j in range(2):
                def fetch_rows(e, source, j=j, t=t, o=pair[j]):
                    return e.indirect_dma_start(out=o, out_offset=None, in_=source, in_offset=offset(
                        ap=dest[j][:, t:t + 1].bitcast(U32), axis=0))
                back = self.pool.either(lambda e, f=fetch_rows: f(e, y_rows),
                                        lambda e, f=fetch_rows: f(e, y_rows[0:EXPERTS * cap, :]),
                                        free[t % 2], inc=s_back[t % 2])
            self.ts(dve, pair[0], pair[0], weight[0][:, t:t + 1], None, ALU.mult, None, back)
            m = self.stt(pair[0], pair[1], weight[1][:, t:t + 1], pair[0], ALU.mult, ALU.add, chain=True)
            for half in range(2):
                b = g.bank()
                for k in range(4):
                    end = self.turn(self.psum[b][:, k * P:(k + 1) * P],
                                    pair[0][:, (4 * half + k) * P:(4 * half + k + 1) * P], mark=k == 3, wait=(m,))
                for k in range(4):
                    kk = 4 * half + k
                    at = self.X[:, kk, t * P:(t + 1) * P]
                    c = t * P // SEQ
                    m2 = self.stt(at, self.psum[b][:, k * P:(k + 1) * P], self.mod[:, layer, 5 * KD + kk, c:c + 1], at,
                                  ALU.mult, ALU.add, end)
                g.bank_free[b] = [m2]
            free[t % 2] = end
            if t < SEQ // P:
                squares.tokens(t, m2)
        squares.close()

    def ssm(self):
        g, a, T, ring = self.g, self.a, SEQ, self.ring
        dve, act, pool, pe = self.dve, self.act, self.pool, self.pe
        NC = T // CHUNK
        ar = self.stage()
        Z, XBC = ar.take(NC, D_INNER), ar.take(32, T)
        keep = ar.at
        pad_w = SSM_CONV - 1
        PB, acc = ar.take(4, T + pad_w), ar.take(2, T)
        dt, acs, eacs, adt = (ar.take(NC, HEADS) for _ in range(4))
        t1, t2, tail = ar.take(NC, HEADS), ar.take(NC, HEADS), ar.take(HEADS)
        neg_a = ar.take(HEADS)
        pads = pool.do(lambda e, i: e.memset(PB, 0.0))
        ready = self.simple_norm(self.col("a_norm"))
        w_in = a["ssm_w_in_2"][0]
        A = self.A

        for n in range(D_INNER // 512):
            w, landed = self.weights(w_in, KD, n * 512, 512)
            for c in range(NC):
                b = g.bank()
                end = self.product(self.psum[b][:, :], lambda k: A[:, k, c * P:(c + 1) * P], lambda k: w[:, k, :], KD,
                                   last=ring.free if c == NC - 1 else None, wait=(landed,), tiles=ready)
                m = self.fn(Z[:, c, n * 512:(n + 1) * 512], self.psum[b][:, :], ACT.Silu, end)
                g.bank_free[b] = [m]

        taps, cb = self.col("ssm_conv_w"), self.col("ssm_conv_b")
        conv_free, acc_free = [pads] * 4, [None] * 2

        def evac(m, out, mark):
            s = m % 4
            end = self.copy(act, PB[:, s, pad_w:], out, mark, conv_free[s])
            buf = acc[:, m % 2, :]
            self.ts(dve, buf, PB[:, s, 0:T], taps[:, m, 0:1], None, ALU.mult, None, end, acc_free[m % 2])
            for j in range(1, SSM_CONV):
                done = self.stt(buf, PB[:, s, j:j + T], taps[:, m, j:j + 1], buf, ALU.mult, ALU.add, chain=True)
            conv_free[s] = done
            acc_free[m % 2] = self.fn(XBC[:, m, :], buf, ACT.Silu, done, bias=cb[:, m:m + 1])
            return end

        self.linear(w_in[:, D_INNER:], KD, 4096, lambda k: A[:, k, 0:T], T, evac)

        wv = w_in.rearrange("(k p) n -> p k n", p=P)[:, :, D_INNER + 4096:D_INNER + 4096 + HEADS]
        (w,), landed = ring.load(((KD, HEADS), 0, lambda i: wv))
        b = g.bank()
        for c in range(NC):
            end = self.product(self.psum[b][:, c * HEADS:(c + 1) * HEADS], lambda k: A[:, k, c * P:(c + 1) * P],
                               lambda k: w[:, k, :], KD, last=ring.free if c == NC - 1 else None, wait=(landed,))
        raw = self.psum[b][:, 0:NC * HEADS].rearrange("p (c h) -> p c h", c=NC)
        m = self.tt(dve, dt, raw, across(self.row("dt_bias"), NC), ALU.add, end)
        g.bank_free[b] = [m]
        self.ts(dve, t1, dt, -1.0, None, ALU.mult, None, chain=True)
        m = self.tt(dve, t1, t1, dt, ALU.max, chain=True)
        m = self.fn(t1, t1, ACT.Exp, m, scale=-1.0)
        u = self.ts(dve, t2, t1, 1.0, None, ALU.add, None, m)
        m = self.fn(acs, t2, ACT.Ln, u)
        self.ts(dve, adt, t2, -1.0, None, ALU.add, None, chain=True)
        self.tt(dve, adt, t1, adt, ALU.subtract, chain=True)
        dve.chain(lambda e, i: e.reciprocal(t2, t2), m)
        self.tt(dve, adt, adt, t2, ALU.mult, chain=True)
        self.tt(dve, adt, adt, acs, ALU.add, m, chain=True)
        self.stt(dt, dt, 0.0, adt, ALU.max, ALU.add, chain=True)
        ma = self.fn(neg_a, self.row("a_log"), ACT.Exp)
        self.ts(dve, neg_a, neg_a, -1.0, None, ALU.mult, None, ma)
        m_adt = self.tt(dve, adt, dt, across(neg_a, NC), ALU.mult, chain=True)

        b = g.bank()
        flat = lambda v: v.rearrange("p c h -> p (c h)")
        self.mm(self.psum[b][:, 0:NC * HEADS], self.mat("upto"), flat(adt), True, True, wait=(m_adt,))
        end = self.mm(self.psum[b][:, 128:128 + HEADS], self.mat("ones"), adt[:, 0, :], True, True, mark=True)
        m_acs = self.copy(dve, flat(acs), self.psum[b][:, 0:NC * HEADS], end)
        m = self.tt(dve, tail, self.psum[b][:, 128:128 + HEADS], acs[:, 0, :], ALU.subtract, chain=True)
        g.bank_free[b] = [m]
        m_tail = self.fn(tail, tail, ACT.Exp, m)
        m_eacs = self.fn(eacs, acs, ACT.Exp, m_acs)
        conv_done = act.done.now()
        dve_done = dve.done.now()

        g.meet()
        save = (dt, acs, eacs, adt, tail)
        XS = A[:, :, :].rearrange("p k t -> p (k t)").rearrange("p (c n) -> p c n", c=NC)
        BT = PB.rearrange("p a b -> p (a b)")[:, 0:SSM_G * STATE]
        XC = [ar.take(SSM_G, HG * HEAD_P), self.X[:, :, SEQ:]]
        for c in range(NC):
            for q in range(4):
                b = g.bank()
                for j in range(4):
                    end = self.turn(self.psum[b][:, j * P:(j + 1) * P], XBC[:, 4 * q + j, c * P:(c + 1) * P], mark=j == 3)
                m = self.copy(act, XS[:, c, q * 512:(q + 1) * 512], self.psum[b][:, :], end)
                g.bank_free[b] = [m]
            xs = XS[:, c, :].rearrange("p (h d) -> p h d", h=HEADS)
            by_group = lambda v: v.rearrange("p g (h d) -> p g h d", d=HEAD_P)
            m = self.tt(dve, by_group(XC[c]), by_group(XS[:, c, :].rearrange("p (g n) -> p g n", g=SSM_G)),
                        along(dt[:, c, :].rearrange("p (g h) -> p g h", g=SSM_G), HEAD_P), ALU.mult, m)
            m_skip = self.tt(pool, xs, xs, along(self.row("d_skip"), HEAD_P), ALU.mult, m)
        m_xc = m
        for q in range(2):
            b = g.bank()
            for j in range(4):
                end = self.turn(self.psum[b][:, j * P:(j + 1) * P], XBC[:, 16 + 4 * q + j, 0:P], mark=j == 3)
            m_bt = self.copy(act, BT[:, q * 512:(q + 1) * 512], self.psum[b][:, :], end)
            g.bank_free[b] = [m_bt]

        mask = ar.take(CHUNK)
        m_mask = self.fetch(mask, a["ssm_mask"])
        work = XBC[:, 0:16, :].rearrange("p m t -> p (m t)")
        cut = lambda n, w: work[:, n * w:(n + 1) * w]
        R = [cut(0, 512), cut(1, 512)]
        E = [cut(2, 512), cut(3, 512)]
        CB = [cut(16, 128), cut(17, 128)]
        XD, PREV, YO = cut(9, 256), cut(10, 256), cut(11, 256)
        pe.wait(m_xc, m_bt)
        r_free, e_free, cb_free = [None] * 2, [None] * 2, [None] * 2
        step = 0
        xd_free = prev_free = None
        last_turn = pe.done.now()
        for lane in (dve, pool, act):
            lane.wait(last_turn)
        for grp in range(SSM_G):
            hs = slice(grp * HG, (grp + 1) * HG)
            ch = slice(grp * HG * HEAD_P, (grp + 1) * HG * HEAD_P)
            for c in range(NC):
                s = step % 2
                step += 1
                bt, ct = XBC[:, 16 + grp, c * P:(c + 1) * P], XBC[:, 24 + grp, c * P:(c + 1) * P]
                b = g.bank()
                end = self.mm(self.psum[b][:, 0:P], bt, ct, True, True, mark=True)
                m_cb = self.copy(act, CB[s], self.psum[b][:, 0:P], end, cb_free[s])
                g.bank_free[b] = [m_cb]
                r4 = R[s].rearrange("p (h t) -> p h t", h=HG)
                m = self.tt(pool, r4, across(self.mat("upto"), HG), along(adt[:, c, hs], P), ALU.mult, r_free[s])
                b = g.bank()
                end = self.mm(self.psum[b][:, :], self.mat("ones"), R[s], True, True, mark=True, wait=(m,))
                r_free[s] = end
                e4 = E[s].rearrange("p (h t) -> p h t", h=HG)
                m = self.tt(dve, e4, self.psum[b][:, :].rearrange("p (h t) -> p h t", h=HG),
                            along(acs[:, c, hs], P), ALU.subtract, end, e_free[s])
                g.bank_free[b] = [m]
                m = self.tt(dve, e4, e4, across(mask, HG), ALU.add, m_mask, chain=True)
                m = self.fn(E[s], E[s], ACT.Exp, m)
                m = self.tt(dve, e4, e4, across(CB[s], HG), ALU.mult, m, m_cb)
                cb_free[s] = m
                b = g.bank()
                for h in range(HG):
                    end = self.mm(self.psum[b][:, h * HEAD_P:(h + 1) * HEAD_P], E[s][:, h * P:(h + 1) * P],
                                  XC[c][:, grp, h * HEAD_P:(h + 1) * HEAD_P], True, True, mark=h == HG - 1, wait=(m,))
                e_free[s] = end
                y = XS[:, c, ch]
                if c == 0:
                    m = self.tt(dve, y, self.psum[b][:, 0:256], y, ALU.add, end, m_skip)
                    g.bank_free[b] = [m]
                    m = self.tt(dve, XD.rearrange("p (h d) -> p h d", h=HG),
                                XC[0][:, grp, :].rearrange("p (h d) -> p h d", h=HG), along(tail[:, hs], HEAD_P),
                                ALU.mult, m_tail, xd_free)
                    b = g.bank()
                    end = self.mm(self.psum[b][:, 0:256], BT[:, grp * STATE:(grp + 1) * STATE], XD, True, True,
                                  mark=True, wait=(m,))
                    xd_free = end
                    m_prev = self.copy(act, PREV, self.psum[b][:, 0:256], end, prev_free)
                    g.bank_free[b] = [m_prev]
                else:
                    m = self.tt(dve, y, self.psum[b][:, 0:256], y, ALU.add, end, m_skip)
                    g.bank_free[b] = [m]
                    b = g.bank()
                    end = self.mm(self.psum[b][:, 0:256], ct, PREV, True, True, mark=True, wait=(m_prev,))
                    prev_free = end
                    self.tt(dve, YO.rearrange("p (h d) -> p h d", h=HG),
                            self.psum[b][:, 0:256].rearrange("p (h d) -> p h d", h=HG), along(eacs[:, 1, hs], HEAD_P),
                            ALU.mult, end, m_eacs)
                    g.bank_free[b] = [dve.done.now()]
                    self.tt(dve, y, y, YO, ALU.add, chain=True)

        ss = t1.rearrange("p c h -> p (c h)")[:, 0:NC * SSM_G].rearrange("p (c g) -> p c g", c=NC)
        pe_last = pe.done.now()
        for c in range(NC):
            self.tt(dve, XS[:, c, :], XS[:, c, :], Z[:, c, :], ALU.mult, chain=True)
            m = dve.done.now()
            m = self.fn(XC[c], XS[:, c, :].rearrange("p (g n) -> p g n", g=SSM_G), ACT.Square, m, pe_last)
            dve.do(lambda e, i, c=c: e.tensor_reduce(
                ss[:, c, :], XC[c], AX.X, ALU.add), m)
        m = self.ts(dve, ss, ss, 1.0 / 256.0, GATED_EPS, ALU.mult, ALU.add, chain=True)
        dve.do(lambda e, i: e.reciprocal(ss, ss), self.fn(ss, ss, ACT.Sqrt, m))
        for c in range(NC):
            y = XS[:, c, :].rearrange("p (g n) -> p g n", g=SSM_G)
            m = self.tt(dve, y, y, along(ss[:, c, :], 256), ALU.mult, chain=True)
        YT = Z.rearrange("p c n -> p (c n)").rearrange("p (m t) -> p m t", m=16)
        gain = self.col("ssm_norm")
        for q in range(8):
            b = g.bank()
            for j in range(2):
                for c in range(NC):
                    end = self.turn(self.psum[b][:, (2 * j + c) * P:(2 * j + c + 1) * P],
                                    XS[:, c, (2 * q + j) * P:(2 * q + j + 1) * P], mark=j and c, wait=(m,))
            for j in range(2):
                m2 = self.ts(dve, YT[:, 2 * q + j, :], self.psum[b][:, 2 * j * P:(2 * j + 2) * P],
                             gain[:, 2 * q + j:2 * q + j + 1], None, ALU.mult, None, end)
            g.bank_free[b] = [m2]
        squares = self.squares()
        self.linear(a["ssm_w_out_2"][0], 16, D, lambda k: YT[:, k, :], T, self.add_plain(squares), m2, width=256)
        squares.close()

    def ffn(self, layer):
        g, a, T, ring = self.g, self.a, SEQ, self.ring
        dve, act = self.dve, self.act
        ar = self.stage()
        pad = FFN_CONV - 1
        H, PB, acc = ar.take(KFF, T), ar.take(4, 2, T + pad), ar.take(4, 2, T)
        pads = self.pool.do(lambda e, i: e.memset(PB, 0.0))
        ready = self.simple_norm(self.col("ffn_norm")[:, layer, :])
        w_up = a["ffn_w_up_2"][layer].rearrange("(k p) (j n) -> p k j n", p=P, j=2)
        taps = self.col("ffn_conv_w")
        pb_free, acc_free = [pads] * 4, [None] * 4
        for n in range(KFF // 2):
            (wg, wv), landed = ring.load(
                ((KD, 256), 0, lambda i, n=n: w_up[:, :, 0, n * 256:(n + 1) * 256]),
                ((KD, 256), KD * 256, lambda i, n=n: w_up[:, :, 1, n * 256:(n + 1) * 256]))
            for t in range(2):
                m = 2 * n + t
                s = m % 4
                b = g.bank()
                for j, w in enumerate((wg, wv)):
                    end = self.product(self.psum[b][:, j * T:(j + 1) * T], lambda k: w[:, k, t * P:(t + 1) * P],
                                       lambda k: self.A[:, k, 0:T], KD,
                                       last=ring.free if t == 1 and j == 1 else None, wait=(landed,),
                                       tiles=ready)
                mark = self.copy(act, PB[:, s, :, pad:], self.psum[b][:, :].rearrange("p (j t) -> p j t", j=2),
                                 end, pb_free[s])
                g.bank_free[b] = [mark]
                for j in range(2):
                    buf, w3 = acc[:, s, j, :], taps[:, layer, j * KFF + m, :]
                    self.ts(dve, buf, PB[:, s, j, 0:T], w3[:, 0:1], None, ALU.mult, None, mark, acc_free[s])
                    for q in (1, 2):
                        done = self.stt(buf, PB[:, s, j, q:q + T], w3[:, q:q + 1], buf, ALU.mult, ALU.add, chain=True)
                    if j == 0:
                        silu = self.fn(buf, buf, ACT.Silu, done)
                pb_free[s] = done
                acc_free[s] = self.tt(self.pool, H[:, m, :], acc[:, s, 0, :], acc[:, s, 1, :], ALU.mult, silu, done)
        h_ready = acc_free[1], acc_free[(KFF - 1) % 4]
        self.pe.wait(*[m for f in g.bank_free for m in f])
        g.bank_free, g.bank_at = [None] * 8, 0
        squares = self.squares()
        first = 0
        w_down = a["ffn_w_down_2"][layer].rearrange("(k p) n -> p k n", p=P)
        for n_k in [KFF % 4] + [4] * (KFF // 4):
            final = first + n_k == KFF
            (w,), landed = ring.load(((n_k, D), 0, lambda i, f=first, n=n_k: w_down[:, f:f + n, :]))
            for m in range(KD):
                for k in range(n_k):
                    last = m == KD - 1 and k == n_k - 1
                    end = self.mm(self.psum[m][:, 0:T], w[:, k, m * P:(m + 1) * P], H[:, first + k, :],
                                  first + k == 0, first + k == KFF - 1, mark=last or final and k == n_k - 1,
                                  inc=ring.free if last else None, wait=(landed, acc_free[(KFF - 1) % 4]))
                if final:
                    out = self.psum[m][:, 0:T]
                    g.bank_free[m] = [self.tt(self.dve, self.X[:, m, 0:T], out, self.X[:, m, 0:T], ALU.add, end)]
                    squares.tile(m, g.bank_free[m][0])
            first += n_k
        squares.close()

    def dilated(self):
        g, a, T, ring = self.g, self.a, SEQ, self.ring
        dve, act, pool, pe = self.dve, self.act, self.pool, self.pe
        ar = self.stage()
        n_kv = N_PAT * ATT_KV
        Q, K, V = ar.take(N_PAT * ATT_HEADS, T), ar.take(n_kv, T), ar.take(2, n_kv * ATT_D)
        cos, sin, rot = ar.take(2, T), ar.take(2, T), ar.take(P)
        widths = [N_PAT * att_keys(q) for q in range(2)]
        mask = ar.take(sum(widths))
        S = [ar.take(w) for w in widths]
        turned = ar.take(2, T)
        small = ar.take(3, 2)
        A = self.A.rearrange("p k t -> p (k t)")
        AK, AQ = (A[:, j * KD * T:(j + 1) * KD * T].rearrange("p (k t) -> p k t", k=KD) for j in range(2))
        for j in range(2):
            self.fetch(cos[:, j, :], a["tables"][:, 640:640 + T])
            self.fetch(sin[:, j, :], a["tables"][:, 896:896 + T])
        self.fetch(rot, a["tables"][:, 1152:1152 + P])
        tables = self.fetch(mask, a["att_mask"])
        stat = self.residual_stat(T, AK)
        k_ready = self.scaled(AK, self.X, self.col("kv_norm"), T, KD, stat)
        ready = self.scaled(AQ, self.X, self.col("b_norm"), T, KD, stat)
        R = ROPE_DIM

        def rotary(two, mark):
            b = g.bank()
            end = self.mm(self.psum[b][:, :], rot, two.rearrange("p m t -> p (m t)"), True, True, mark=True,
                          wait=(mark, tables))
            out = self.psum[b][0:R, :].rearrange("p (m t) -> p m t", m=2)
            m = self.tt(dve, turned[0:R], out, sin[0:R], ALU.mult, end, chain=True)
            g.bank_free[b] = [m]
            self.tt(dve, two[0:R], two[0:R], cos[0:R], ALU.mult, end)
            return self.tt(dve, two[0:R], two[0:R], turned[0:R], ALU.add, chain=True)

        def heads(w, landed, n, rhs, dst, scale, last):
            for t in range(0, n, 2):
                b = g.bank()
                for j in range(2):
                    end = self.product(self.psum[b][:, j * T:(j + 1) * T], lambda k: w[:, k, (t + j) * P:(t + j + 1) * P],
                                       rhs, KD, last=ring.free if last and t + j == n - 1 else None,
                                       wait=(landed,), tiles=k_ready if rhs is k_rhs else ready)
                two = dst[:, t:t + 2, :]
                m = self.fn(two, self.psum[b][:, :].rearrange("p (m t) -> p m t", m=2), ACT.Copy, end, scale=scale)
                g.bank_free[b] = [m]
                waiting.append((two, m))
                if len(waiting) > 1:
                    rotary(*waiting.pop(0))

        def tokens(w, landed, cols, dst_at, last):
            n = cols.stop - cols.start
            for c in range(2):
                b = g.bank()
                end = self.product(self.psum[b][:, 0:n], lambda k: AK[:, k, c * P:(c + 1) * P], lambda k: w[:, k, cols],
                                   KD, last=ring.free if last and c == 1 else None, wait=(landed,))
                m = self.copy(act, V[:, c, dst_at:dst_at + n], self.psum[b][:, 0:n], end)
                g.bank_free[b] = [m]
            return m

        waiting = []
        k_rhs, q_rhs = (lambda k: AK[:, k, :]), (lambda k: AQ[:, k, :])
        w, landed = self.weights(a["w_kv_2"], KD, 0, 512)
        heads(w, landed, 4, k_rhs, K[:, 0:4, :], 1.0, True)
        w, landed = self.weights(a["w_kv_2"], KD, 512, 512)
        heads(w, landed, 2, k_rhs, K[:, 4:6, :], 1.0, False)
        tokens(w, landed, slice(256, 512), 0, True)
        w, landed = self.weights(a["w_kv_2"], KD, 1024, 512)
        tokens(w, landed, slice(0, 512), 256, True)
        for c in range(6):
            w, landed = self.weights(a["att_w_q_2"][0], KD, c * 512, 512)
            heads(w, landed, 4, q_rhs, Q[:, 4 * c:4 * c + 4, :], float(ATT_D) ** -0.5, True)
        rotary(*waiting.pop(0))
        g.meet()

        OT = AQ
        PT = [AK.rearrange("p k t -> p (k t)")[:, 0:widths[0]], AK.rearrange("p k t -> p (k t)")[:, widths[0]:sum(widths)]]
        s_free, pt_free = [None, None], [None, None]

        def scores(h, q):
            kv, n = h // (ATT_HEADS // ATT_KV), att_keys(q)
            banks, at = [], 0
            for p in range(N_PAT):
                if (at + n) > BANK or p == 0:
                    b, at = g.bank(), 0
                    banks.append([b, p, 0])
                end = self.mm(self.psum[b][:, at:at + n], Q[:, p * ATT_HEADS + h, q * P:(q + 1) * P],
                              K[:, p * ATT_KV + kv, 0:n], True, True, mark=True)
                at += n
                banks[-1][2] = at
            base = 0 if q == 0 else widths[0]
            for b, p, w in banks:
                lo = p * n
                m = self.tt(dve, S[q][:, lo:lo + w], self.psum[b][:, 0:w], mask[:, base + lo:base + lo + w], ALU.add,
                            end, s_free[q])
                g.bank_free[b] = [m]
            top, total, inv = (small[:, j, q:q + 1] for j in range(3))
            m = dve.chain(lambda e, i: e.tensor_reduce(top, S[q], AX.X, ALU.max, negate=True))
            m = self.fn(S[q], S[q], ACT.Exp, m, bias=top, total=total)
            dve.do(lambda e, i: e.reciprocal(inv, total), m)
            return self.ts(dve, S[q], S[q], inv, None, ALU.mult, None, chain=True)

        def values(h, q, mark):
            kv, n_b = h // (ATT_HEADS // ATT_KV), q + 1
            blocks = N_PAT * n_b
            for lo in range(0, blocks, 4):
                b = g.bank()
                hi = min(blocks, lo + 4)
                for j in range(lo, hi):
                    end = self.turn(self.psum[b][:, (j - lo) * P:(j - lo + 1) * P], S[q][:, j * P:(j + 1) * P],
                                    mark=j == hi - 1, wait=(mark,))
                m = self.copy(act, PT[q][:, lo * P:hi * P], self.psum[b][:, 0:(hi - lo) * P], end, pt_free[q])
                g.bank_free[b] = [m]
            s_free[q] = end
            b = g.bank()
            for j in range(blocks):
                p, c = divmod(j, n_b)
                at = (p * ATT_KV + kv) * ATT_D
                end = self.mm(self.psum[b][:, 0:P], V[:, c, at:at + ATT_D], PT[q][:, j * P:(j + 1) * P],
                              j == 0, j == blocks - 1, mark=j == blocks - 1, wait=(m,))
            pt_free[q] = end
            m = self.copy(dve, OT[:, h, q * P:(q + 1) * P], self.psum[b][:, 0:P], end)
            g.bank_free[b] = [m]
            return m

        order = [(h, q) for h in range(ATT_HEADS) for q in range(2)]
        before = scores(*order[0])
        for n, (h, q) in enumerate(order):
            after = scores(*order[n + 1]) if n + 1 < len(order) else None
            out_mark = values(h, q, before)
            before = after
        squares = self.squares()
        self.linear(a["att_w_o_2"][0], KD, D, lambda k: OT[:, k, :], T, self.add_plain(squares), out_mark)
        squares.close()

    def finish(self):
        self.stage()
        m = self.simple_norm(self.col("final_2"))[-1]
        out = self.g.counter("result")
        y = self.a["y"].rearrange("(k p) t -> p k t", p=P)
        m = self.act.do(lambda e, i: e.dma_start(y, self.A[:, :, 0:SEQ]), m, inc=out)
        for lane in self.g.lanes:
            lane.wait(m)

    def between_networks(self):
        ar = self.stage()
        stat = self.residual_stat(SEQ, self.A)
        marks = self.scaled(self.X, self.X, self.col("final_1"), SEQ, KD, stat)
        squares = Squares(self, SEQ, [ar.take(SEQ), ar.take(SEQ)])
        for m, mark in enumerate(marks):
            squares.tile(m, mark)
        squares.close()

    def emit(self):
        with self.nc.Block() as block:
            for name, lane in zip(("tensor", "scalar", "vector", "gpsimd", "sync"), self.g.lanes):
                {"tensor": block.tensor, "scalar": block.scalar, "vector": block.vector,
                 "gpsimd": block.gpsimd, "sync": block.sync}[name](lambda e, lane=lane: lane.replay(e))


def build(nc, a, stop=None):
    with ExitStack() as ctx:
        k = Kernel(nc, ctx, a)
        k.start()
        stages = [k.mla, lambda: k.moe(0, SEQ + CTX, CAP[0]), lambda: None, k.conv_mixer,
                  lambda: k.moe(1, SEQ, CAP[1]), k.between_networks, k.ssm, lambda: k.ffn(0), k.dilated,
                  lambda: k.ffn(1), k.finish]
        for f in stages[:stop]:
            f()
        if stop is not None:
            k.stage()
            out = k.g.counter("dump")
            m = k.act.do(lambda e, i: e.dma_start(a["dump"].rearrange("(k p) t -> p k t", p=P), k.X[:, :, :]), inc=out)
            for lane in k.g.lanes:
                lane.wait(m)
        k.emit()


_WEIGHTS = ["w_mod", "mla_w_dq", "mla_w_uq", "mla_w_dkv", "mla_w_ukv", "mla_w_o", "conv_w_in", "conv_w_out",
            "moe_w_group", "moe_w_expert", "moe_w_gate", "moe_w_up", "moe_w_down", "ssm_w_in_2", "ssm_w_out_2",
            "w_kv_2", "att_w_q_2", "att_w_o_2", "ffn_w_up_2", "ffn_w_down_2"]


def _constants():
    f = np.float32
    i = np.arange(P)
    mats = np.stack([np.eye(P, dtype=f), np.full((P, P), 1 / 1024, f), np.full((P, P), 1 / 512, f),
                     np.full((P, P), 1 / 256, f), np.ones((P, P), f), (i[:, None] < i[None, :]).astype(f),
                     (i[:, None] <= i[None, :]).astype(f)], axis=1)
    t = np.arange(SEQ)
    tables = np.zeros((P, 1280), f)

    def rotary(at, d, pos, inv_freq, x, half):
        angle = pos.astype(f) * inv_freq[x % half]
        tables[d, at:at + SEQ] = np.cos(angle)
        tables[d, at + SEQ:at + 2 * SEQ] = np.sin(angle)
        if x < half:
            tables[d + half, at + 2 * SEQ + d] = -1
        else:
            tables[d - half, at + 2 * SEQ + d] = 1

    half = MLA_ROPE // 4
    inv = (f(ROPE_THETA) ** (-np.arange(half, dtype=f) / half)).astype(f)
    for d in range(P):
        x = d % MLA_ROPE
        rotary(0, d, t // GRID_W if x < MLA_ROPE // 2 else t % GRID_W, inv, x % (2 * half), half)
    half = ROPE_DIM // 2
    inv = (f(ROPE_THETA_2) ** (-np.arange(0, ROPE_DIM, 2, dtype=f) / ROPE_DIM)).astype(f)
    for d in range(ROPE_DIM):
        rotary(640, d, t, inv, d, half)
    masks = []
    for q in range(2):
        back = (q * P + i)[:, None] - np.arange(att_keys(q))[None, :]
        for window, dilation in PATTERNS:
            masks.append(np.where((back >= 0) & (back <= window) & (back % dilation == 0), 0, NEG))
    return {"mats": mats, "tables": tables, "att_mask": np.concatenate(masks, axis=1).astype(f),
            "ssm_mask": np.where(i[:, None] <= i[None, :], 0, NEG).astype(f)}


def _vectors(v):
    f = np.float32
    tiles = lambda x: np.moveaxis(x.reshape(*x.shape[:-1], -1, P), -1, 0)
    taps = lambda x: np.moveaxis(tiles(x), -2, -1)
    parts = {"cond": np.stack([tiles(v["c"][0]), tiles(v["c_ctx"])], -1), "b_mod": tiles(v["b_mod"]),
             "norm_mix": tiles(v["norm_mix_g"]), "norm_ffn": tiles(v["norm_ffn_g"]), "g_q": tiles(v["mla_g_q"][0]),
             "g_kv": tiles(v["mla_g_kv"][0]), "conv_w": taps(v["conv_w"][0]), "final_1": tiles(v["final_norm_g"]),
             "a_norm": tiles(v["a_norm_2"][0]), "ssm_conv_w": taps(v["ssm_conv_w_2"][0]),
             "ssm_conv_b": tiles(v["ssm_conv_b_2"][0]), "ssm_norm": tiles(v["ssm_norm_2"][0]),
             "kv_norm": tiles(v["kv_norm_2"]), "b_norm": tiles(v["b_norm_2"][0]), "ffn_norm": tiles(v["ffn_norm_2"]),
             "ffn_conv_w": taps(v["ffn_conv_w_2"]), "final_2": tiles(v["final_norm_2"]),
             "token": np.arange(P * 4, dtype=f).reshape(4, P).T}
    cols = np.concatenate([parts[n].reshape(P, -1) for n in column_layout()[0]], axis=1)
    rows = {"first_4": np.arange(GROUPS, 0, -1, dtype=f), "first_8": np.arange(PER_GROUP, 0, -1, dtype=f),
            "count": np.arange(P, dtype=f), "dt_bias": v["ssm_dt_bias_2"][0], "a_log": v["ssm_a_log_2"][0],
            "d_skip": v["ssm_d_2"][0]}
    for j in range(2):
        rows[f"route_bias_{j}"] = np.concatenate([v["moe_b_group"][j], v["moe_b_expert"][j]])
    return cols, np.concatenate([rows[n] for n in row_layout()[0]])[None, :]


def arrays_of(inputs):
    v = {k: np.asarray(x) for k, x in inputs.items()}
    arrays = {n: v[n] for n in _WEIGHTS}
    arrays |= _constants()
    arrays["cols"], arrays["rows"] = _vectors(v)
    arrays["xT"], arrays["ctxT"] = v["x"][0].T, v["ctx"][0].T
    return {k: np.ascontiguousarray(x) for k, x in arrays.items()}


def kernel(**inputs):
    import concourse.bacc as bacc
    from concourse.bass_utils import run_bass_kernel_spmd

    nc = bacc.Bacc("TRN2", target_bir_lowering=False, num_devices=1)
    arrays, a = {}, {}
    for name, x in arrays_of(inputs).items():
        arrays[f"in_{name}"] = x
        a[name] = nc.dram_tensor(f"in_{name}", x.shape, mybir.dt.from_np(x.dtype), kind="ExternalInput").ap()
    a["y"] = nc.dram_tensor("y", [D, SEQ], F32, kind="ExternalOutput").ap()
    build(nc, a)
    got = run_bass_kernel_spmd(nc, [arrays], core_ids=[0]).results[0]["y"]
    return np.ascontiguousarray(np.asarray(got).T)[None]
```

```python
from contextlib import ExitStack

import numpy as np

import concourse.bass as bass
from concourse import mybir
from concourse.alu_op_type import AluOpType as ALU

F32 = mybir.dt.float32
F32R = mybir.dt.float32r
I32 = mybir.dt.int32
U32 = mybir.dt.uint32
ACT = mybir.ActivationFunctionType
AX = mybir.AxisListType

P = 128
BANK = 512
SLOT = 4096
RING = 6

D = 1024
KD = D // P
SEQ = 256
CTX = 256
N_MOD = 6
GRID_W = 64
MLA_HEADS = 8
MLA_NOPE = 128
MLA_ROPE = 64
MLA_V = 128
MLA_Q_LORA = 512
MLA_KV_LORA = 256
ROPE_THETA = 10000.0
NORM_EPS = 1e-6
GROUPS = 4
PER_GROUP = 8
EXPERTS = GROUPS * PER_GROUP
FF = 512
KF = FF // P
CONV_W = 3
D_INNER = 2048
HEAD_P = 64
HEADS = D_INNER // HEAD_P
SSM_G = 8
STATE = 128
HG = HEADS // SSM_G
SSM_CONV = 4
CHUNK = 128
GATED_EPS = 1e-5
PATTERNS = ((128, 1), (512, 4), (2048, 16))
N_PAT = len(PATTERNS)
ATT_HEADS = 8
ATT_KV = 2
ATT_D = 128
ROPE_DIM = ATT_D // 4
ROPE_THETA_2 = 500000.0
FFN = 2816
KFF = FFN // P
FFN_CONV = 3
CAP = (96, 80)
NEG = -1e30
BIG = 3.0e38


def column_layout():
    parts = [("cond", (KD, 2)), ("b_mod", (2, N_MOD * KD)), ("norm_mix", (2, KD)), ("norm_ffn", (2, KD)),
             ("g_q", (MLA_Q_LORA // P,)), ("g_kv", (MLA_KV_LORA // P,)), ("conv_w", (KD, CONV_W)),
             ("final_1", (KD,)), ("a_norm", (KD,)), ("ssm_conv_w", (32, SSM_CONV)), ("ssm_conv_b", (32,)),
             ("ssm_norm", (16,)), ("kv_norm", (KD,)), ("b_norm", (KD,)), ("ffn_norm", (2, KD)),
             ("ffn_conv_w", (2, 2 * KFF, FFN_CONV)), ("final_2", (KD,)), ("token", (4,))]
    at, out = 0, {}
    for name, shape in parts:
        out[name] = (at, shape)
        at += int(np.prod(shape))
    return out, at


def row_layout():
    parts = [("route_bias_0", GROUPS + EXPERTS), ("route_bias_1", GROUPS + EXPERTS), ("first_4", GROUPS),
             ("first_8", PER_GROUP), ("count", P), ("dt_bias", HEADS), ("a_log", HEADS), ("d_skip", HEADS)]
    at, out = 0, {}
    for name, n in parts:
        out[name] = (at, n)
        at += n
    return out, at


MATS = ["ident", "ones_1024", "ones_512", "ones_256", "ones", "before", "upto"]


def att_keys(qt):
    return (qt + 1) * P


class Counter:

    def __init__(self, sem, step=1):
        self.sem, self.step, self.n, self.base, self.per, self.loop = sem, step, 0, 0, 0, None

    def raised(self, loop):
        self.enter(loop)
        self.n += self.step
        return Mark(self, self.n, self.loop)

    def enter(self, loop):
        if self.loop is not loop:
            assert loop is not None
            self.loop, self.base, self.n = loop, self.n, 0
            loop.counters.append(self)

    def now(self):
        return Mark(self, self.n, self.loop)


class Mark:

    def __init__(self, counter, off, loop):
        self.counter, self.off, self.loop = counter, off, loop

    def value(self, index, shift):
        if self.loop is None:
            return self.off
        base, per = self.loop.frames[self.counter]
        if index is None:
            return base + self.off + per * (self.loop.trips - 1)
        const = base + self.off + per * shift
        assert const > 0, self.counter.sem
        return index * per + const if per else const


class Later:

    mark = None

    def set(self, mark):
        self.mark = mark


class Loop:

    def __init__(self, shape):
        self.shape, self.trips = shape, int(np.prod(shape))
        self.counters, self.frames = [], {}


class Lane:

    def __init__(self, program, name, sem):
        self.program, self.name, self.items, self.done = program, name, [], Counter(sem)
        self.in_order = name in ("act", "dve", "pool")
        self.waited = {}

    def wait(self, *marks):
        for m in marks:
            if m is None:
                continue
            if isinstance(m, Later):
                self.items.append(("wait", m, -1))
                continue
            key = (m.counter, m.loop)
            if m.off <= self.waited.get(key, 0):
                continue
            self.waited[key] = m.off
            self.items.append(("wait", m, 0))

    def do(self, fn, *marks, inc=None, mark=True, loose=False):
        self.wait(*marks)
        if self.in_order and not loose:
            self.wait(self.done.now())
        counter = (inc or self.done) if mark else None
        self.items.append(("op", fn, counter))
        return counter.raised(self.program.loop) if counter else None

    def chain(self, fn, *marks, inc=None):
        return self.do(fn, *marks, self.done.now(), inc=inc)

    def replay(self, engine, items=None, index=None, indices=None):
        for item in (self.items if items is None else items):
            kind = item[0]
            if kind == "wait":
                mark = item[1].mark if isinstance(item[1], Later) else item[1]
                here = index if mark.loop is not None and mark.loop is self.running else None
                value = mark.value(here, item[2])
                if isinstance(value, int) and value <= 0:
                    continue
                engine.wait_ge(mark.counter.sem, value)
            elif kind == "op":
                got = item[1](engine, indices)
                if item[2] is not None:
                    got.then_inc(item[2].sem, item[2].step)
            elif kind == "loop":
                _, loop, body = item
                outer, self.running = self.running, loop
                if len(loop.shape) == 1:
                    with engine.Fori(0, loop.shape[0], 1) as i:
                        self.replay(engine, body, i, (i,))
                else:
                    with engine.Fori(0, loop.shape[0], 1) as a:
                        with engine.Fori(0, loop.shape[1], 1) as b:
                            self.replay(engine, body, a * loop.shape[1] + b, (a, b))
                self.running = outer
            elif kind == "if":
                _, flag, body = item
                self.flag = value = engine.value_load(flag, min_val=0, max_val=4096)
                with engine.If(value > 0):
                    self.replay(engine, body)

            elif kind == "either":
                _, yes, no, counter = item
                with engine.If(self.flag > 0):
                    yes(engine).then_inc(counter.sem, counter.step)
                with engine.Else():
                    no(engine).then_inc(counter.sem, counter.step)

    def either(self, yes, no, *marks, inc):
        self.wait(*marks, self.done.now())
        self.items.append(("either", yes, no, inc))
        return inc.raised(self.program.loop)

    running = None
    flag = None


class Program:

    def __init__(self, nc, ctx):
        self.nc, self.ctx, self.loop = nc, ctx, None
        self.pe, self.act, self.dve, self.pool, self.sp = (
            Lane(self, n, self.semaphore("done_" + n)) for n in ("pe", "act", "dve", "pool", "sp"))
        self.lanes = [self.pe, self.act, self.dve, self.pool, self.sp]
        self.bank_at = 0
        self.bank_free = [[] for _ in range(8)]
        self.reserved = set()

    def semaphore(self, name):
        return self.ctx.enter_context(self.nc.semaphore(name))

    def twins(self, name, shape):
        at = -(-self.nc.sbuf_base // 32) * 32
        plain = self.ctx.enter_context(self.nc.sbuf_tensor(name, shape, F32))
        return plain, self.nc.alloc_sbuf_tensor_at(name + "_rounded", shape, F32, offset=at)

    def counter(self, name, step=16):
        return Counter(self.semaphore(name), step)

    def meet(self, *extra):
        marks = [lane.done.now() for lane in self.lanes[:4]]
        for lane in self.lanes[:4]:
            lane.wait(*marks, *extra)
        self.bank_free = [[] for _ in range(8)]

    def bank(self):
        while self.bank_at in self.reserved:
            self.bank_at = (self.bank_at + 1) % 8
        b = self.bank_at
        self.bank_at = (b + 1) % 8
        assert self.bank_free[b] is not None, "its readers aren't queued yet"
        self.pe.wait(*self.bank_free[b])
        self.bank_free[b] = None
        return b

    def loop_begin(self, *shape):
        assert self.loop is None
        self.loop = Loop(shape)
        self.outer = [lane.items for lane in self.lanes]
        for lane in self.lanes:
            lane.items, lane.waited = [], {}
            if lane.in_order:
                lane.last = Later()
                lane.wait(lane.last)
        return self.loop

    def loop_end(self):
        loop, self.loop = self.loop, None
        for lane in self.lanes:
            if lane.in_order:
                lane.last.set(lane.done.now())
        for c in loop.counters:
            loop.frames[c] = (c.base, c.n)
            c.per, c.n, c.loop = c.n, c.base + c.n * loop.trips, None
        for lane, items in zip(self.lanes, self.outer):
            body, lane.items, lane.waited = lane.items, items, {}
            if body:
                items.append(("loop", loop, body))

    def branch_begin(self, name):
        self.saved = [(lane.items, lane.done, lane.waited) for lane in self.lanes]
        for lane in self.lanes:
            lane.items, lane.waited = [], {}
            lane.done = Counter(self.semaphore(name + "_" + lane.name))

    def branch_end(self, flag):
        for lane, (items, done, waited) in zip(self.lanes, self.saved):
            body, lane.items, lane.done, lane.waited = lane.items, items, done, waited
            items.append(("if", flag, body))


class Ring:

    def __init__(self, g):
        self.g = g
        nc = g.nc
        self.slots, self.rounded = zip(*[g.twins(f"ring_{i}", [P, SLOT]) for i in range(RING)])
        self.landed = [g.counter(f"landed_{i}") for i in range(RING)]
        self.frees = [g.counter(f"ring_free_{i}", 1) for i in range(RING)]
        self.free = None
        self.total, self.loop, self.here = 0, None, 0

    def load(self, *pieces):
        g = self.g
        if g.loop is not self.loop:
            self.total += self.here * (self.loop.trips if self.loop else 1)
            self.loop, self.here = g.loop, 0
        number = self.total + self.here
        slot = number % RING
        self.free = self.frees[slot]
        if g.loop is not None:
            assert self.here < RING
            self.free.enter(g.loop)
        else:
            assert self.free.n == number // RING, "the slot's last reader isn't queued yet"
        if number >= RING:
            g.sp.items.append(("wait", self.free.now(), 0))
        views = []
        for shape, first, source, *part in pieces:
            n = int(np.prod(shape))
            view = self.slots[slot][:, first:first + n]
            if len(shape) > 1:
                names = " ".join("abc"[:len(shape)])
                view = view.rearrange(f"p ({names}) -> p {names}", **dict(zip("abc", shape[:-1])))
            to = part[0](view) if part else view
            mark = g.sp.do(lambda e, i, v=to, s=source: e.dma_start(v, s(i)), inc=self.landed[slot])
            views.append(view)
        self.here += 1
        self.slot = slot
        return views, mark

    def beside(self):
        slot = (self.slot + 1) % RING
        self.here += 1
        assert self.g.loop is None
        return slot, self.frees[slot].now()


class Arena:

    def __init__(self, tensor, size, rounded):
        self.tensor, self.size, self.at, self.rounded = tensor, size, 0, rounded

    def take_twins(self, *shape):
        at = self.at
        plain = self.take(*shape)
        self.at = at
        return plain, self.take(*shape, tensor=self.rounded)

    def take_rounded(self, *shape):
        return self.take(*shape, tensor=self.rounded)

    def take(self, *shape, tensor=None):
        n = int(np.prod(shape))
        view = (tensor or self.tensor)[:, self.at:self.at + n]
        self.at += n
        assert self.at <= self.size, (self.at, self.size)
        if len(shape) > 1:
            names = " ".join("abc"[:len(shape)])
            view = view.rearrange(f"p ({names}) -> p {names}", **dict(zip("abc", shape[:-1])))
        return view


def along(ap, n):
    return ap.unsqueeze(len(ap.shape)).broadcast_to([*ap.shape, n])


def across(ap, n, dim=1):
    shape = list(ap.shape)
    return ap.unsqueeze(dim).broadcast_to([*shape[:dim], n, *shape[dim:]])


class Modulation:

    def __init__(self, k, layer, first=0):
        self.k, self.layer, self.first, self.at = k, layer, first, first
        self.rows, self.rows_free, self.waiting = [], [], None
        self.bank = k.g.bank()
        k.g.reserved.add(self.bank)

    def use(self, rows, *marks):
        self.turn_last()
        self.rows, self.rows_free = rows, [None, None]
        self.k.act.wait(*marks)

    def steps(self, n):
        k, g = self.k, self.k.g
        for _ in range(n):
            at = self.at
            self.at += 1
            w, landed = k.weights(k.a["w_mod"][self.layer], KD, at * 512, 512)
            b = g.bank()
            end = k.product(k.psum[b][0:2, :], lambda i: k.silu_cond[:, i, :], lambda i: w[:, i, :], KD,
                            last=k.ring.free, wait=(landed,))
            row = self.rows[at % 2]
            m = k.copy(k.act, row[0:2, :], k.psum[b][0:2, :], end, self.rows_free[at % 2])
            g.bank_free[b] = [m]
            self.turn_last()
            self.waiting = (at, row, m)

    def turn_last(self):
        k = self.k
        if self.waiting is None:
            return
        at, row, m = self.waiting
        for t in range(4):
            tile = (4 * at + t) * 2
            self.end = k.turn(k.psum[self.bank][:, tile:tile + 2], row[0:2, t * P:(t + 1) * P], rows=2,
                              mark=t == 3, wait=(m,))
        self.rows_free[at % 2] = self.end
        self.waiting = None

    def close(self):
        k, g = self.k, self.k.g
        self.turn_last()
        tiles = slice(4 * self.first, 4 * self.at)
        out = k.psum[self.bank][:, 2 * tiles.start:2 * tiles.stop].rearrange("p (m c) -> p m c", c=2)
        mod = k.mod[:, self.layer, :, :]
        m = k.tt(k.dve, mod[:, tiles, :], out, along(k.col("b_mod")[:, self.layer, tiles], 2), ALU.add, self.end)
        g.bank_free[self.bank] = [m]
        g.reserved.remove(self.bank)
        for which, (j, norm) in enumerate(((1, "norm_mix"), (4, "norm_ffn"))):
            if tiles.start <= j * KD and (j + 1) * KD <= tiles.stop:
                k.stt(k.gain[:, self.layer, which, :, :], mod[:, j * KD:(j + 1) * KD, :], 1.0,
                      along(k.col(norm)[:, self.layer, :], 2), ALU.add, ALU.mult, chain=True)
        k.mod_made = m


class Squares:

    def __init__(self, k, T, buffers, *marks):
        self.k, self.T, self.buffers, self.free = k, T, buffers, [None, None]
        self.made, self.bank, self.waiting = 0, None, None
        k.act.wait(*marks)

    def square(self, buf, src, products, mark):
        s = self.made % 2
        self.made += 1
        squares = self.k.fn(buf, src, ACT.Square, mark, self.free[s])
        self.add_last()
        self.waiting = (s, products, squares)

    def tile(self, m, mark):
        T, buf = self.T, self.buffers[self.made % 2]
        self.square(buf[:, 0:T], self.k.X[:, m, 0:T], [(slice(0, T), buf[:, 0:T], m == 0, m == KD - 1)], mark)

    def tokens(self, t, mark):
        buf, cols = self.buffers[self.made % 2], slice(t * P, (t + 1) * P)
        self.square(buf, self.k.X[:, :, cols], [(cols, buf[:, i, :], i == 0, i == KD - 1) for i in range(KD)], mark)

    def add_last(self):
        if self.waiting is None:
            return
        s, products, squares = self.waiting
        k = self.k
        if self.bank is None:
            self.bank = k.g.bank()
            k.g.reserved.add(self.bank)
        for cols, rhs, start, stop in products:
            self.end = k.mm(k.psum[self.bank][:, cols], k.mat(f"ones_{D}"), rhs, start, stop, mark=True, wait=(squares,))
        self.free[s], self.waiting = self.end, None

    def close(self):
        k = self.k
        self.add_last()
        k.g.reserved.remove(self.bank)
        k.stat = k.inverse_root(self.bank, self.T, NORM_EPS, self.end)


class Kernel:
    def __init__(self, nc, ctx, a, stop=None):
        self.nc, self.a, self.stop = nc, a, stop
        self.g = g = Program(nc, ctx)
        self.pe, self.act, self.dve, self.pool, self.sp = g.lanes
        self.ring = Ring(g)

        def sb(name, shape, dt=F32):
            return ctx.enter_context(nc.sbuf_tensor(name, shape, dt))

        self.sb = sb
        self.psum = [ctx.enter_context(nc.psum_tensor(f"bank_{i}", [P, BANK], F32)) for i in range(8)]
        self.layout, ncol = column_layout()
        self.row_at, nrow = row_layout()
        self.cols, self.rows = sb("cols", [P, ncol]), sb("rows", [P, nrow])
        self.mats = sb("mats", [P, len(MATS), P])
        self.X = sb("residual", [P, KD, SEQ + CTX])
        self.A, self.A_rounded = g.twins("normed", [P, KD, SEQ + CTX])
        self.rstd = sb("rstd", [P, SEQ + CTX])
        self.mod = sb("mod", [P, 2, N_MOD * KD, 2])
        self.gain = sb("gain", [P, 2, 2, KD, 2])
        self.arena_size = 17600
        self.arena_tensor, self.arena_rounded = g.twins("arena", [P, self.arena_size])
        self.loads = g.counter("loads")
        self.stat, self.prepared = None, None

    def col(self, name):
        at, shape = self.layout[name]
        view = self.cols[:, at:at + int(np.prod(shape))]
        if len(shape) > 1:
            names = " ".join("abc"[:len(shape)])
            view = view.rearrange(f"p ({names}) -> p {names}", **dict(zip("abc", shape[:-1])))
        return view

    def row(self, name):
        at, n = self.row_at[name]
        return self.rows[:, at:at + n]

    def mat(self, name):
        return self.mats[:, MATS.index(name), :]

    def stage(self):
        self.g.meet()
        return Arena(self.arena_tensor, self.arena_size, self.arena_rounded)

    def fetch(self, out, source, *marks, lane=None):
        return (lane or self.act).do(lambda e, i: e.dma_start(out, source), *marks, inc=self.loads)

    def mm(self, out, lhsT, rhs, start, stop, mark=False, inc=None, wait=(), shared=False):
        return self.pe.do(lambda e, i: e.matmul(out, lhsT, rhs, start=start, stop=stop, skip_group_check=shared),
                          *wait, inc=inc, mark=mark)

    def product(self, out, lhs, rhs, n_k, last=None, wait=(), tiles=None):
        self.pe.wait(*wait)
        for k in range(n_k):
            self.pe.wait(*(tiles[k:k + 1] if tiles else ()))
            end = k == n_k - 1
            m = self.mm(out, lhs(k), rhs(k), k == 0, end, mark=end, inc=last if end else None)
        return m

    def product3(self, out, stationary, moving, n_k, wait=(), tiles=None, frees=(None, None), weights_move=False,
                 start=True, stop=True):
        self.pe.wait(*wait)
        passes = [(0, 0), (1, 0), (0, 1)] if weights_move else [(0, 0), (0, 1), (1, 0)]
        for n, (s, m) in enumerate(passes):
            part = s if weights_move else m
            for k in range(n_k):
                if tiles:
                    self.pe.wait(tiles[part][k])
                end = k == n_k - 1
                inc = frees[n - 1] if n and end else None
                last = self.mm(out, stationary[s](k).bitcast(F32R), moving[m](k).bitcast(F32R),
                               start and n == 0 and k == 0, stop and n == 2 and end,
                               mark=inc is not None or n == 2 and end, inc=inc)
        return last

    def split(self, *pieces):
        ring = self.ring
        _, landed = ring.load(*pieces)
        n = max(first + int(np.prod(shape)) for shape, first, *_ in pieces)
        slot, free_low = ring.slot, ring.free
        beside, free = ring.beside()
        raw, low, high = ring.slots[slot][:, 0:n], ring.rounded[slot][:, 0:n], ring.rounded[beside][:, 0:n]
        m_high = self.copy(self.act, high.bitcast(F32R), raw, landed, free)
        m_low = self.tt(self.dve, low.bitcast(F32R), raw, high, ALU.subtract, m_high)
        parts = []
        for source in (high, low):
            part = []
            for shape, first, *_ in pieces:
                v = source[:, first:first + int(np.prod(shape))]
                names = " ".join("abc"[:len(shape)])
                part.append(v.rearrange(f"p ({names}) -> p {names}", **dict(zip("abc", shape[:-1]))))
            parts.append(part)
        return parts, (m_high, m_low), (ring.frees[beside], free_low)

    def split_weights(self, source, n_k, first, n):
        w = source.rearrange("(k p) n -> p k n", p=P)[:, :, first:first + n]
        return self.split(((n_k, n), 0, lambda i: w))

    def prepare(self, first_chunk):
        self.prepared = first_chunk()
        return self.prepared

    def take_prepared(self, first_chunk):
        chunk, self.prepared = self.prepared or first_chunk(), None
        return chunk

    def halved(self, value, high, low, mark, lane=None):
        m_high = self.copy(self.act, high.bitcast(F32R), value, mark)
        return m_high, self.tt(lane or self.dve, low.bitcast(F32R), value, high, ALU.subtract, m_high)

    def norm_parts(self, value, gain, stat, high, low):
        marks = ([], [])
        for k in range(KD):
            m = self.stt(value(k), self.X[:, k, 0:SEQ], gain[:, k:k + 1], self.rstd[:, 0:SEQ], ALU.mult, ALU.mult, stat)
            h = self.copy(self.act, high(k).bitcast(F32R), value(k), m)
            marks[0].append(h)
            if k:
                marks[1].append(self.tt(self.dve, low(k - 1).bitcast(F32R), value(k - 1), high(k - 1), ALU.subtract,
                                        marks[0][k - 1]))
        k = KD - 1
        marks[1].append(self.tt(self.dve, low(k).bitcast(F32R), value(k), high(k), ALU.subtract, marks[0][k]))
        return marks

    def parts_of_A(self):
        return (lambda k: self.A_rounded[:, k, SEQ:]), (lambda k: self.A_rounded[:, k, 0:SEQ])

    def linear3(self, source, n_k, n_out, parts, T, evac, *marks, width=512, inputs=None, first_chunk=None, then=None,
                order=None):
        starts = order or list(range(0, n_out, width))
        make = lambda first: self.split_weights(source, n_k, first, min(width, n_out - first))
        chunk = first_chunk or make(0)
        for n, first in enumerate(starts):
            after = make(starts[n + 1]) if n + 1 < len(starts) else then() if then else None
            ((high,), (low,)), ready, frees = chunk
            tiles = min(width, n_out - first) // P
            for t in range(tiles):
                b = self.g.bank()
                out = self.psum[b][:, 0:T]
                cols = slice(t * P, (t + 1) * P)
                m = self.product3(out, (lambda k: high[:, k, cols], lambda k: low[:, k, cols]), parts, n_k,
                                  wait=(*ready, *marks), tiles=inputs, frees=frees if t == tiles - 1 else (None, None))
                self.g.bank_free[b] = [evac(first // P + t, out, m)]
            chunk = after
        return chunk

    def turn(self, out, in_, rows=P, mark=False, wait=()):
        return self.pe.do(lambda e, i: e.transpose(out, in_, self.mats[0:rows, 0, 0:rows]), *wait, mark=mark)

    def tt(self, lane, out, a, b, op, *marks, chain=False):
        f = lane.chain if chain else lane.do
        return f(lambda e, i: e.tensor_tensor(out, a, b, op), *marks)

    def ts(self, lane, out, a, s1, s2, op0, op1, *marks, chain=False):
        f = lane.chain if chain else lane.do
        if s2 is None:
            return f(lambda e, i: e.tensor_scalar(out, a, s1, None, op0), *marks)
        return f(lambda e, i: e.tensor_scalar(out, a, s1, s2, op0, op1), *marks)

    def stt(self, out, a, s, b, op0, op1, *marks, chain=False):
        f = self.dve.chain if chain else self.dve.do
        return f(lambda e, i: e.scalar_tensor_tensor(out, a, s, b, op0, op1), *marks)

    def fn(self, out, a, func, *marks, bias=0.0, scale=1.0, total=None, chain=False):
        f = self.act.chain if chain else self.act.do
        return f(lambda e, i: e.activation(out, a, func, bias=bias, scale=scale, accum_out=total), *marks)

    def copy(self, lane, out, a, *marks, chain=False):
        f = lane.chain if chain else lane.do
        if lane is self.act:
            return f(lambda e, i: e.activation(out, a, ACT.Copy), *marks)
        return f(lambda e, i: e.tensor_copy(out, a), *marks)

    def mean_square(self, src, n_k, T, width, eps, scratch, *marks):
        b = self.g.bank()
        out = self.psum[b][:, 0:T]
        ones = self.mat(f"ones_{width}")
        for k in range(n_k):
            m = self.fn(scratch[:, k, 0:T], src[:, k, 0:T], ACT.Square, *marks)
            end = self.mm(out, ones, scratch[:, k, 0:T], k == 0, k == n_k - 1, mark=k == n_k - 1, wait=(m,))
        return self.inverse_root(b, T, eps, end)

    def inverse_root(self, b, T, eps, end):
        m = self.ts(self.dve, self.rstd[:, 0:T], self.psum[b][:, 0:T], eps, None, ALU.add, None, end)
        self.g.bank_free[b] = [m]
        m = self.fn(self.rstd[:, 0:T], self.rstd[:, 0:T], ACT.Sqrt, m)
        return self.dve.do(lambda e, i: e.reciprocal(self.rstd[:, 0:T], self.rstd[:, 0:T]), m)

    def scaled(self, dst, src, gain, T, n_k, stat):
        return [self.stt(dst[:, k, 0:T], src[:, k, 0:T], gain[:, k:k + 1], self.rstd[:, 0:T],
                         ALU.mult, ALU.mult, stat) for k in range(n_k)]

    def residual_stat(self, T, scratch):
        stat, self.stat = self.stat, None
        return stat or self.mean_square(self.X, KD, T, D, NORM_EPS, scratch)

    def modulated(self, layer, which, T, between=lambda: None):
        stat = self.residual_stat(T, self.A)
        stat_pe = self.pe.done.now()
        between()
        self.act.wait(self.mod_made)
        shift = 0 if which == 0 else 3
        marks = []
        for k in range(KD):
            for c in range(T // SEQ):
                cols = slice(c * SEQ, (c + 1) * SEQ)
                m = self.stt(self.A[:, k, cols], self.X[:, k, cols], self.gain[:, layer, which, k, c:c + 1],
                             self.rstd[:, cols], ALU.mult, ALU.mult, stat, stat_pe)
                last = self.fn(self.A[:, k, cols], self.A[:, k, cols], ACT.Identity, m,
                               bias=self.mod[:, layer, shift * KD + k, c:c + 1])
            marks.append(last)
        return marks

    def modulated_parts(self, layer, T, high, low, between=lambda: None):
        stat = self.residual_stat(T, self.A)
        stat_pe = self.pe.done.now()
        between()
        self.act.wait(self.mod_made)
        ready = ([], [])
        halves = [(c, slice(c * SEQ, (c + 1) * SEQ)) for c in range(T // SEQ)]

        def lower(k):
            for c, cols in halves:
                m = self.stt(low(k)[:, cols].bitcast(F32R), self.A[:, k, cols], self.mod[:, layer, k, c:c + 1],
                             high(k)[:, cols], ALU.add, ALU.subtract, ready[0][k])
            ready[1].append(m)

        for k in range(KD):
            at = self.A[:, k, 0:T]
            for c, cols in halves:
                m = self.stt(at[:, cols], self.X[:, k, cols], self.gain[:, layer, 0, k, c:c + 1], self.rstd[:, cols],
                             ALU.mult, ALU.mult, stat, stat_pe)
                h = self.fn(high(k)[:, cols].bitcast(F32R), at[:, cols], ACT.Identity, m,
                            bias=self.mod[:, layer, k, c:c + 1])
            ready[0].append(h)
            if k:
                lower(k - 1)
        lower(KD - 1)
        return ready

    def simple_norm(self, gain, dst=None, T=SEQ):
        dst = self.A if dst is None else dst
        stat = self.residual_stat(T, dst)
        return self.scaled(dst, self.X, gain, T, KD, stat)

    def weights(self, source, n_k, first, n):
        w = source.rearrange("(k p) n -> p k n", p=P)[:, :, first:first + n]
        (view,), mark = self.ring.load(((n_k, n), 0, lambda i: w))
        return view, mark

    def linear(self, source, n_k, n_out, rhs, T, evac, *marks, width=512, inputs=None):
        for first in range(0, n_out, width):
            w, landed = self.weights(source, n_k, first, min(width, n_out - first))
            tiles = min(width, n_out - first) // P
            for t in range(tiles):
                b = self.g.bank()
                out = self.psum[b][:, 0:T]
                m = self.product(out, lambda k: w[:, k, t * P:(t + 1) * P], rhs, n_k,
                                 last=self.ring.free if t == tiles - 1 else None, wait=(landed, *marks),
                                 tiles=inputs)
                self.g.bank_free[b] = [evac(first // P + t, out, m)]

    def add_gated(self, layer, j, squares):
        def evac(m, out, mark):
            for c in range(out.shape[1] // SEQ):
                cols = slice(c * SEQ, (c + 1) * SEQ)
                last = self.stt(self.X[:, m, cols], out[:, cols], self.mod[:, layer, j * KD + m, c:c + 1],
                                self.X[:, m, cols], ALU.mult, ALU.add, mark)
            squares.tile(m, last)
            return last
        return evac

    def add_plain(self, squares):
        def evac(m, out, mark):
            last = self.tt(self.dve, self.X[:, m, 0:SEQ], out, self.X[:, m, 0:SEQ], ALU.add, mark)
            squares.tile(m, last)
            return last
        return evac

    def squares(self, *marks):
        return Squares(self, SEQ, [self.rstd[:, 0:SEQ], self.rstd[:, SEQ:]], self.dve.done.now(), *marks)

    def start(self):
        a = self.a
        self.fetch(self.cols[:, :], a["cols"])
        self.fetch(self.mats[:, :, :], a["mats"])
        self.fetch(self.rows[:, :], a["rows"].broadcast_to([P, a["rows"].shape[1]]))
        self.fetch(self.X[:, :, 0:SEQ], a["xT"].rearrange("(k p) t -> p k t", p=P), lane=self.sp)
        m = self.fetch(self.X[:, :, SEQ:SEQ + CTX], a["ctxT"].rearrange("(k p) t -> p k t", p=P), lane=self.sp)
        for lane in (self.pe, self.act, self.dve, self.pool):
            lane.wait(m)
        cond = self.col("cond")
        self.silu_cond = self.sb("silu_cond", [P, KD, 2])
        self.pe.wait(self.fn(self.silu_cond[:, :, :], cond, ACT.Silu))

    def mla(self):
        g, a, T = self.g, self.a, SEQ + CTX
        ar = self.stage()
        CQ = ar.take(4, T)
        ar.at = 0
        score_buf = [ar.take(BANK) for _ in range(4)]
        CKV, KPE = ar.take(2, T), ar.take(2, T)
        (QN, O_high), QR = ar.take_twins(MLA_HEADS, T), ar.take(MLA_HEADS // 2, T)
        V, V_rounded = ar.take_twins(4, MLA_HEADS * P)
        KN, PT = ar.take(2, T), ar.take(4, SEQ)
        PTC = ar.take(2, CTX)
        tables_both, rot = ar.take(2 * SEQ), ar.take(P)
        cos, sin = tables_both[:, 0:SEQ], tables_both[:, SEQ:2 * SEQ]
        small = ar.take(3, 8)
        raw = KN[:, 0, :]
        tables = self.fetch(cos, a["tables"][:, 0:SEQ], self.act.done.now(), self.dve.done.now(), self.pe.done.now())
        self.fetch(sin, a["tables"][:, SEQ:2 * SEQ])
        tables = self.fetch(rot, a["tables"][:, 2 * SEQ:2 * SEQ + P])
        scale = float(MLA_NOPE + MLA_ROPE) ** -0.5
        zero = self.pool.do(lambda e, i: e.memset(KPE, 0.0))
        halves = lambda v: [v.rearrange("p a b -> p (a b)")[:, n * 512:(n + 1) * 512] for n in range(2)]
        first = Modulation(self, 0)
        first.use(halves(PT))

        chunks = []

        def shift_and_scale():
            first.steps(3)
            chunks.append(self.split_weights(a["mla_w_dq"][0], KD, 0, MLA_Q_LORA))
            first.steps(1)
            first.close()
        x_high = V_rounded.rearrange("p a b -> p (a b)").rearrange("p (k t) -> p k t", k=KD)
        x_parts = (lambda k: x_high[:, k, :]), (lambda k: self.A_rounded[:, k, :])
        ready = self.modulated_parts(0, T, *x_parts, shift_and_scale)
        rest = Modulation(self, 0, first=4)
        rest.use(halves(PT), self.pe.done.now())
        wd = a["mla_w_dkv"][0].rearrange("(k p) n -> p k n", p=P)
        n_kv = MLA_KV_LORA
        pe_cols = lambda i: wd[:, :, n_kv:n_kv + MLA_ROPE]
        kv_chunk = lambda: self.split(
            ((KD, n_kv), 0, lambda i: wd[:, :, 0:n_kv]),
            ((KD, P), KD * n_kv, pe_cols, lambda v: v[:, :, 0:MLA_ROPE]),
            ((KD, P), KD * n_kv, pe_cols, lambda v: v[:, :, MLA_ROPE:P]))
        (kv_high, kv_low), marks, frees = self.linear3(
            a["mla_w_dq"][0], KD, MLA_Q_LORA, x_parts, T, lambda m, out, mark: self.copy(self.dve, CQ[:, m, :], out, mark),
            inputs=ready, first_chunk=chunks[0], then=kv_chunk)
        for m in range(3):
            b = g.bank()
            out = self.psum[b][:, :]
            which, cols = (0, slice(m * P, (m + 1) * P)) if m < 2 else (1, slice(0, P))
            end = self.product3(out, [lambda k, w=w[which]: w[:, k, cols] for w in (kv_high, kv_low)], x_parts, KD,
                                wait=marks, frees=frees if m == 2 else (None, None))
            if m < 2:
                g.bank_free[b] = [self.copy(self.dve, CKV[:, m, :], out, end)]
            else:
                k_raw = self.copy(self.act, raw, out, end)
                g.bank_free[b] = [k_raw]

        kv_done, squares_read = self.dve.done.now(), None
        for buf, n_k, gain in ((CQ, 4, "g_q"), (CKV, 2, "g_kv")):
            stat = self.mean_square(buf, n_k, T, n_k * P, NORM_EPS, QN, kv_done, squares_read)
            rest.steps(1)
            *_, done = self.scaled(buf, buf, self.col(gain), T, n_k, stat)
            squares_read = self.pe.done.now()
        self.act.wait(squares_read)
        self.dve.wait(squares_read)

        def rotate(src, mark):
            b = g.bank()
            out = self.psum[b][:, 0:SEQ]
            end = self.mm(out, rot, src[:, 0:SEQ], True, True, mark=True, wait=(mark, tables))
            m = self.tt(self.dve, turned[:, :], out, sin, ALU.mult, end, chain=True)
            g.bank_free[b] = [m]
            self.tt(self.dve, src[:, 0:SEQ], src[:, 0:SEQ], cos, ALU.mult, end)
            return self.tt(self.dve, src[:, 0:SEQ], src[:, 0:SEQ], turned[:, :], ALU.add, chain=True)

        turned = self.rstd[:, 0:SEQ]
        k_rot = rotate(raw, k_raw)
        half = MLA_ROPE
        self.copy(self.dve, KPE[0:half, 0, :], raw[0:half, :], zero, k_rot)
        k_pe = self.copy(self.dve, KPE[half:P, 1, :], raw[half:P, :])

        hw = MLA_NOPE + MLA_ROPE
        wq = a["mla_w_uq"][0].rearrange("(k p) (h c) -> p k h c", p=P, c=hw)
        q_marks = []
        for c in range(2):
            pieces = []
            heads = slice(4 * c, 4 * c + 4)
            for k in range(4):
                pieces.append(((4, 768), 0, lambda i, k=k, heads=heads: wq[:, k, heads, 0:MLA_NOPE],
                               lambda v, k=k: v[:, k, 0:512].rearrange("p (h c) -> p h c", h=4)))
                pieces.append(((4, 768), 0, lambda i, k=k, heads=heads: wq[:, k, heads, MLA_NOPE:hw],
                               lambda v, k=k: v[:, k, 512:768].rearrange("p (h c) -> p h c", h=4)))
            (w, *_), landed = self.ring.load(*pieces)
            for t in range(6):
                b = g.bank()
                out = self.psum[b][:, :]
                end = self.product(out, lambda k: w[:, k, t * P:(t + 1) * P], lambda k: CQ[:, k, :], 4,
                                   last=self.ring.free if t == 5 else None, wait=(landed, done))
                dst = QN[:, 4 * c + t, :] if t < 4 else QR[:, 2 * c + t - 4, :]
                m = self.fn(dst, out, ACT.Copy, end, scale=scale)
                g.bank_free[b] = [m]
                if t >= 4:
                    m = rotate(dst, m)
                q_marks.append(m)
        self.pe.wait(self.act.done.now(), self.dve.done.now())

        rest.steps(1)

        wkv = a["mla_w_ukv"][0].rearrange("(k p) n -> p k n", p=P)
        (w,), landed = self.ring.load(((2, 2 * MLA_HEADS * P), 0, lambda i: wkv))
        w_heads = w.rearrange("p k (h j c) -> p k h j c", j=2, c=P)
        w_heads_free = self.ring.free
        for t in range(T // P):
            for n in range(2):
                b = g.bank()
                end = self.product(self.psum[b][:, :], lambda k: CKV[:, k, t * P:(t + 1) * P],
                                   lambda k: w_heads[:, k, 4 * n:4 * n + 4, 1, :], 2, wait=(landed,))
                v_mark = self.copy(self.act, V[:, t, n * 512:(n + 1) * 512], self.psum[b][:, :], end)
                g.bank_free[b] = [v_mark]

        O_low, o_ready = self.A_rounded, ([], [])
        score_free = [None] * 4
        kn_free = [k_pe, k_pe]
        pt_free = [None, None]

        def scores(h):
            b = g.bank()
            kn = KN[:, h % 2, :]
            end = self.product(self.psum[b][:, :], lambda k: w_heads[:, k, h, 0, :], lambda k: CKV[:, k, :], 2,
                               last=w_heads_free if h == MLA_HEADS - 1 else None)
            m = self.copy(self.dve, kn, self.psum[b][:, :], end, kn_free[h % 2])
            g.bank_free[b] = [m]
            self.pe.wait(m)
            probs = []
            for q in range(T // P):
                lat = q < SEQ // P
                keys = slice(0, T) if lat else slice(SEQ, T)
                n = T if lat else CTX
                if q != 3:
                    b = g.bank()
                    g.reserved.add(b)
                at = 0 if q != 3 else CTX
                out = self.psum[b][:, at:at + n]
                self.mm(out, QN[:, h, q * P:(q + 1) * P], kn[:, keys], True, False)
                end = self.mm(out, QR[:, h // 2, q * P:(q + 1) * P], KPE[:, h % 2, keys], False, True, mark=True)
                probs.append((q, b, out, n, end))
            kn_free[h % 2] = end
            return probs

        def softmax(probs):
            before, tops, sums, marks = self.act.done.now(), [], [], []
            for q, b, out, n, e1 in probs:
                tops.append(self.dve.do(lambda e, i, o=small[:, 0, q:q + 1], s=out: e.tensor_reduce(
                    o, s, AX.X, ALU.max, negate=True), e1 if q < 2 else probs[3][4], before))
            for (q, b, out, n, _), m in zip(probs, tops):
                m = self.fn(score_buf[q][:, 0:n], out, ACT.Exp, m if q < 2 else tops[3], score_free[q], bias=small[:, 0, q:q + 1],
                            total=small[:, 1, q:q + 1])
                g.bank_free[b] = [m]
                g.reserved.discard(b)
                sums.append(m)
            for (q, _, _, n, _), m in zip(probs, sums):
                buf, inv = score_buf[q][:, 0:n], small[:, 2, q:q + 1]
                self.dve.do(lambda e, i, o=inv, s=small[:, 1, q:q + 1]: e.reciprocal(o, s), m)
                marks.append(self.ts(self.dve, buf, buf, inv, None, ALU.mult, None, chain=True))
            return marks

        def values(h, marks):
            for q in range(2):
                b = g.bank()
                for k in range(4):
                    end = self.turn(self.psum[b][:, k * P:(k + 1) * P], score_buf[q][:, k * P:(k + 1) * P],
                                    mark=k == 3, wait=(marks[q],))
                score_free[q] = end
                m = self.copy(self.act, PT[:, :, q * P:(q + 1) * P],
                              self.psum[b][:, :].rearrange("p (k q) -> p k q", k=4), end, pt_free[0])
                g.bank_free[b] = [m]
            b = g.bank()
            for q in range(2):
                for k in range(2):
                    end = self.turn(self.psum[b][:, (2 * q + k) * P:(2 * q + k + 1) * P],
                                    score_buf[2 + q][:, k * P:(k + 1) * P], mark=k == 1, wait=(marks[2 + q],))
                score_free[2 + q] = end
            mc = self.copy(self.act, PTC.rearrange("p k (q c) -> p q k c", q=2),
                           self.psum[b][:, :].rearrange("p (q k c) -> p q k c", q=2, k=2), end, pt_free[1])
            g.bank_free[b] = [mc]
            b = g.bank()
            for k in range(4):
                self.mm(self.psum[b][:, 0:SEQ], V[:, k, h * P:(h + 1) * P], PT[:, k, :], k == 0, k == 3,
                        wait=(m, v_mark))
            for k in range(2):
                end = self.mm(self.psum[b][:, SEQ:T], V[:, 2 + k, h * P:(h + 1) * P], PTC[:, k, :], k == 0, k == 1,
                              mark=k == 1, wait=(mc,))
            pt_free[0] = pt_free[1] = end
            high = self.copy(self.dve, O_high[:, h, :].bitcast(F32R), self.psum[b][:, :], end)
            m = self.tt(self.dve, O_low[:, h, :].bitcast(F32R), self.psum[b][:, :], O_high[:, h, :], ALU.subtract,
                        chain=True)
            g.bank_free[b] = [m]
            o_ready[0].append(high)
            o_ready[1].append(m)

        rest.use([tables_both, self.rstd], self.dve.done.now())
        marks = softmax(scores(0))
        for h in range(MLA_HEADS):
            after = scores(h + 1) if h + 1 < MLA_HEADS else None
            rest.steps(1 if h < 5 else 0)
            if h == MLA_HEADS - 1:
                chunk = self.split_weights(a["mla_w_o"][0], KD, 0, 512)
            values(h, marks)
            marks = softmax(after) if after else None
        rest.close()
        squares = Squares(self, T, [tables_both, self.rstd], self.pe.done.now())
        self.linear3(a["mla_w_o"][0], KD, D, (lambda k: O_high[:, k, :], lambda k: O_low[:, k, :]), T,
                     self.add_gated(0, 2, squares), inputs=o_ready, first_chunk=chunk)
        squares.close()

    def conv_first(self):
        return self.split_weights(self.a["conv_w_in"][0], KD, D, 512)

    def conv_mixer(self):
        a, T = self.a, SEQ
        ar = self.stage()
        C, V = ar.take(KD, T), ar.take(2, T + 2)
        (Z, Z_rounded), Z_high = ar.take_twins(KD, T), ar.take_rounded(KD, T)
        pads = self.pool.do(lambda e, i: e.memset(V, 0.0))
        w_in, w_out = a["conv_w_in"][0], a["conv_w_out"][0]
        chunk = self.take_prepared(self.conv_first)
        ready = self.modulated_parts(1, T, *self.parts_of_A())
        taps = self.col("conv_w")
        state = {0: pads, 1: pads, "high": [], "low": []}

        waiting = []

        def halve_z(behind=1):
            if len(waiting) > behind:
                m, done = waiting.pop(0)
                for name, mark in zip(("high", "low"), self.halved(Z[:, m, :], Z_high[:, m, :], Z_rounded[:, m, :], done)):
                    state[name].append(mark)

        def evac(m, out, mark):
            part, m = divmod(m, KD)
            z = Z[:, m, :]
            if part == 1:
                state["c"] = self.copy(self.act, C[:, m, :], out, mark)
                return state["c"]
            if part == 0:
                halve_z()
                done = self.tt(self.dve, z, out, z, ALU.mult, mark)
                waiting.append((m, done))
                return done
            v = V[:, m % 2, :]
            end = self.tt(self.dve, v[:, 1:T + 1], out, C[:, m, :], ALU.mult, mark, state["c"], state[m % 2])
            first = self.fn(z, v[:, 0:T], ACT.Copy, end, scale=taps[:, m, 0:1])
            self.stt(z, v[:, 1:T + 1], taps[:, m, 1:2], z, ALU.mult, ALU.add, first)
            state[m % 2] = self.stt(z, v[:, 2:T + 2], taps[:, m, 2:3], z, ALU.mult, ALU.add, chain=True)
            return end

        order = [part * D + half for half in (0, 512) for part in (1, 2, 0)]
        chunk = self.linear3(w_in, KD, 3 * D, self.parts_of_A(), T, evac, inputs=ready, first_chunk=chunk,
                             order=order, then=lambda: self.split_weights(w_out, KD, 0, 512))
        halve_z(0)
        halve_z(0)
        squares = self.squares()
        self.linear3(w_out, KD, D, (lambda k: Z_high[:, k, :], lambda k: Z_rounded[:, k, :]), T,
                     self.add_gated(1, 2, squares), inputs=(state["high"], state["low"]), first_chunk=chunk)
        squares.close()

    def first_max(self, score, order, n, tmp, out):
        top, eq = tmp
        nt = score.shape[1]
        self.dve.chain(lambda e, i: e.tensor_reduce(top, score, AX.X, ALU.max))
        self.tt(self.dve, eq, score, along(top, n), ALU.is_equal, chain=True)
        self.tt(self.dve, eq, eq, across(order, nt), ALU.mult, chain=True)
        self.dve.chain(lambda e, i: e.tensor_reduce(top, eq, AX.X, ALU.max))
        return self.tt(self.dve, out, eq, along(top, n), ALU.is_equal, chain=True)

    def moe(self, layer, T, cap):
        g, a, ring = self.g, self.a, self.ring
        NT = T // P
        n_blocks = -(-T // cap)
        f_rows = self.nc.dram_tensor(f"f_rows_{layer}", [T, D], F32, kind="Internal").ap()
        y_rows = self.nc.dram_tensor(f"y_rows_{layer}", [n_blocks * EXPERTS * cap, D], F32, kind="Internal").ap()
        s_yout = [g.counter(f"y_out_{layer}_{j}") for j in range(2)]
        s_gather = [g.counter(f"gather_{layer}_{j}") for j in range(2)]
        s_back = [g.counter(f"back_{layer}_{t}") for t in range(NT)]

        ar = self.stage()
        index_i = ar.take(n_blocks * EXPERTS + 2).bitcast(I32)
        index_u = ar.take(2)
        weight = [ar.take(NT) for _ in range(2)]
        dest = [ar.take(NT) for _ in range(2)]
        flag = self.sb(f"flag_{layer}", [P, 1])
        pos = [ar.take(NT) for _ in range(2)]
        chosen = ar.take(2, NT * EXPERTS)
        W = ar.take(KD, GROUPS + EXPERTS)
        router = self.fetch(W[:, :, 0:GROUPS], a["moe_w_group"][layer].rearrange("(k p) n -> p k n", p=P),
                            *[l.done.now() for l in g.lanes[:4]])
        router = self.fetch(W[:, :, GROUPS:], a["moe_w_expert"][layer].rearrange("(k p) n -> p k n", p=P))
        ahead = Modulation(self, layer + 1) if layer == 0 else None

        def fill(n):
            if ahead:
                ahead.steps(n)
        if ahead:
            ahead.use([ar.take(512), ar.take(512)])
        ready = self.modulated(layer, 1, T)
        fill(2)

        n_log = GROUPS + EXPERTS
        b = g.bank()
        for t in range(NT):
            end = self.product(self.psum[b][:, t * n_log:(t + 1) * n_log], lambda k: self.A[:, k, t * P:(t + 1) * P],
                               lambda k: W[:, k, :], KD, wait=(router,), tiles=ready)
        logits = ar.take(NT, n_log)
        m_log = self.copy(self.dve, logits, self.psum[b][:, 0:NT * n_log].rearrange("p (t n) -> p t n", n=n_log), end)
        g.bank_free[b] = [m_log]

        rows = ar.take(2, D)
        sent = []
        for t in range(NT):
            for half in range(2):
                b = g.bank()
                for j in range(4):
                    end = self.turn(self.psum[b][:, j * P:(j + 1) * P],
                                    self.A[:, 4 * half + j, t * P:(t + 1) * P], mark=j == 3)
                at = rows[:, t % 2, half * 512:(half + 1) * 512]
                m = self.copy(self.act, at, self.psum[b][:, :], end, sent[t - 2] if t >= 2 else None)
                g.bank_free[b] = [m]
            sent.append(self.act.do(lambda e, i, t=t: e.dma_start(f_rows[t * P:(t + 1) * P, :], rows[:, t % 2, :]),
                                    m, inc=s_yout[t % 2]))
        rows_out = sent[-2:]

        bias = self.row(f"route_bias_{layer}")
        dve, act = self.dve, self.act

        def softmax(x, n, top, total):
            dve.chain(lambda e, i: e.tensor_reduce(top, x, AX.X, ALU.max))
            m = self.tt(dve, x, x, along(top, n), ALU.subtract, chain=True)
            m = self.fn(x, x, ACT.Exp, m)
            dve.chain(lambda e, i: e.tensor_reduce(total, x, AX.X, ALU.add), m)
            dve.chain(lambda e, i: e.reciprocal(total, total))
            self.tt(dve, x, x, along(total, n), ALU.mult, chain=True)

        def reduced(out, x):
            return dve.chain(lambda e, i: e.tensor_reduce(out, x, AX.X, ALU.add))

        gp, gs, g_hot = logits[:, :, 0:GROUPS], ar.take(NT, GROUPS), ar.take(NT, GROUPS)
        el = logits[:, :, GROUPS:].rearrange("p t (g e) -> p t g e", g=GROUPS)
        top, total, g_w = ar.take(NT), ar.take(NT), ar.take(NT)
        softmax(gp, GROUPS, top, total)
        self.tt(dve, gs, gp, across(bias[:, 0:GROUPS], NT), ALU.add, chain=True)
        eq4 = ar.take(NT, GROUPS)
        self.first_max(gs, self.row("first_4"), GROUPS, (top, eq4), g_hot)
        self.tt(dve, gs, gp, g_hot, ALU.mult, chain=True)
        reduced(g_w, gs)

        picked = ar.take(NT, EXPERTS).rearrange("p t (g e) -> p t g e", g=GROUPS)
        ep, e_bias, e_sc, eq8 = (ar.take(NT, PER_GROUP) for _ in range(4))
        hot = [ar.take(NT, PER_GROUP) for _ in range(2)]
        wide_hot = along(g_hot, PER_GROUP)
        e_rows = across(bias[:, GROUPS:].rearrange("p (g e) -> p g e", g=GROUPS), NT)
        for src, out in ((el, ep), (e_rows, e_bias)):
            self.tt(dve, picked, src, wide_hot, ALU.mult, chain=True)
            reduced(out, picked.rearrange("p t g e -> p t e g"))
        softmax(ep, PER_GROUP, top, total)
        self.tt(dve, e_sc, ep, e_bias, ALU.add, chain=True)
        self.first_max(e_sc, self.row("first_8"), PER_GROUP, (top, eq8), hot[0])
        self.ts(dve, eq8, hot[0], -1.0, 1.0, ALU.mult, ALU.add, chain=True)
        self.tt(dve, e_sc, e_sc, eq8, ALU.mult, chain=True)
        self.stt(e_sc, hot[0], -BIG, e_sc, ALU.mult, ALU.add, chain=True)
        self.first_max(e_sc, self.row("first_8"), PER_GROUP, (top, eq8), hot[1])
        for j in range(2):
            self.tt(dve, eq8, ep, hot[j], ALU.mult, chain=True)
            reduced(weight[j], eq8)
        self.tt(dve, total, weight[0], weight[1], ALU.add, chain=True)
        dve.chain(lambda e, i: e.reciprocal(total, total))
        self.tt(dve, total, total, g_w, ALU.mult, chain=True)
        for j in range(2):
            self.tt(dve, weight[j], weight[j], total, ALU.mult, chain=True)
        for j in range(2):
            out = chosen[:, j, :].rearrange("p (t g e) -> p t g e", t=NT, g=GROUPS)
            self.tt(dve, out, wide_hot, across(hot[j], GROUPS, 2), ALU.mult, chain=True)
        both = ar.take(NT, EXPERTS)
        flat = both.rearrange("p t e -> p (t e)")
        m_both = self.tt(dve, flat, chosen[:, 0, :], chosen[:, 1, :], ALU.add, chain=True)

        fill(5)

        b = g.bank()
        for t in range(NT):
            out = self.psum[b][:, t * EXPERTS:(t + 1) * EXPERTS]
            for s in range(t):
                self.mm(out, self.mat("ones"), both[:, s, :], s == 0, False, wait=(m_both,))
            self.mm(out, self.mat("before"), both[:, t, :], t == 0, True, wait=(m_both,))
        out = self.psum[b][:, NT * EXPERTS:(NT + 1) * EXPERTS]
        for t in range(NT):
            end = self.mm(out, self.mat("ones"), both[:, t, :], t == 0, t == NT - 1, mark=t == NT - 1)
        ranks, loads = ar.take(NT, EXPERTS), ar.take(EXPERTS)
        self.copy(dve, ranks.rearrange("p t e -> p (t e)"), self.psum[b][:, 0:NT * EXPERTS], end)
        m = self.copy(dve, loads, out)
        g.bank_free[b] = [m]
        most = ar.take(1)
        dve.chain(lambda e, i: e.tensor_reduce(most, loads, AX.X, ALU.max))
        self.ts(dve, most, most, -float(cap), 0.0, ALU.add, ALU.max, chain=True)
        flag_mark = self.copy(dve, flag[:, :].bitcast(I32), most, chain=True)
        tmp = ar.take(NT, EXPERTS)
        step = ar.take(NT)
        count = self.row("count")
        for j in range(2):
            mine = chosen[:, j, :].rearrange("p (t e) -> p t e", t=NT)
            self.tt(dve, tmp, ranks, mine, ALU.mult, chain=True)
            reduced(pos[j], tmp)
            self.tt(dve, tmp, mine, across(count[:, 0:EXPERTS], NT), ALU.mult, chain=True)
            reduced(step, tmp)
            self.stt(dest[j], step, float(cap), pos[j], ALU.mult, ALU.add, chain=True)
            for n in range(1, n_blocks):
                self.ts(dve, step, pos[j], float(n * cap), float((EXPERTS - 1) * cap), ALU.is_ge, ALU.mult, chain=True)
                self.tt(dve, dest[j], dest[j], step, ALU.add, chain=True)
            self.copy(dve, dest[j].bitcast(I32), dest[j], chain=True)

        fill(3)

        slot = ar.take(2, NT * cap)
        named = ar.take(2, NT * EXPERTS)
        for j in range(2):
            for t in range(NT):
                mine = chosen[:, j, t * EXPERTS:(t + 1) * EXPERTS]
                self.ts(dve, named[:, j, t * EXPERTS:(t + 1) * EXPERTS], mine, self.col("token")[:, t:t + 1], None,
                        ALU.mult, None)

        def index_block(n):
            for j in range(2):
                for t in range(NT):
                    m = self.ts(dve, slot[:, j, t * cap:(t + 1) * cap], count[:, 0:cap], float(n * cap),
                                pos[j][:, t:t + 1], ALU.add, ALU.is_equal, chain=True)
            b = g.bank()
            out = self.psum[b][0:cap, 0:EXPERTS]
            for j in range(2):
                for t in range(NT):
                    last = j == 1 and t == NT - 1
                    end = self.mm(out, slot[:, j, t * cap:(t + 1) * cap], named[:, j, t * EXPERTS:(t + 1) * EXPERTS],
                                  j == 0 and t == 0, last, mark=last, wait=(m,))
            m = self.copy(dve, index_i[0:cap, n * EXPERTS:(n + 1) * EXPERTS], out, end)
            g.bank_free[b] = [m]
            return m
        zeroed = self.pool.do(lambda e, i: e.memset(index_i, 0))
        self.dve.wait(zeroed)
        index_mark = index_block(0)

        fill(2)
        if ahead:
            ahead.close()

        keep = ar.at
        xe, xt = ar.take(2, D), ar.take(2, KD * cap)
        yb, act_h = ar.take(2, D), ar.take(KF * cap)
        h_high, h_low, w_high = ar.take_rounded(KF * cap), ar.take_rounded(KF * cap), ar.take_rounded(KF, D)
        gate, up = (a[n][layer].rearrange("x (p k) n -> x p k n", p=P) for n in ("moe_w_gate", "moe_w_up"))
        down = a["moe_w_down"][layer].rearrange("x (p k) n -> x p k n", p=P)
        index_buf = index_u.bitcast(I32)
        offset = bass.IndirectOffsetOnAxis
        per_bank = min(KD, BANK // cap)
        n_turned = -(-KD // per_bank)

        def gather(j, column, counter, *marks):
            m = self.pool.do(lambda e, i: e.tensor_copy(index_buf[0:cap, j:j + 1], index_i[0:cap, column(i)]), *marks)
            self.pool.items.append(("op", lambda e, i: e.drain(), None))
            return self.pool.do(lambda e, i: e.indirect_dma_start(
                out=xe[0:cap, j, :], out_offset=None, in_=f_rows,
                in_offset=offset(ap=index_buf[0:cap, j:j + 1].bitcast(U32), axis=0)), inc=counter, loose=True)

        def turned(j, gathered, banks, *marks):
            self.pe.wait(*marks)
            for n, b in enumerate(banks):
                lo, hi = n * per_bank, min(KD, (n + 1) * per_bank)
                for k in range(lo, hi):
                    end = self.turn(self.psum[b][:, (k - lo) * cap:(k - lo + 1) * cap],
                                    xe[0:cap, j, :].rearrange("c (p k) -> c k p", k=KD)[:, k, :], rows=cap, mark=k == hi - 1, wait=(gathered,))
                m = self.copy(dve, xt[:, j, lo * cap:hi * cap], self.psum[b][:, 0:(hi - lo) * cap], end)
            return m, end

        def expert(j, x_ready, w, low, landed, frees, between, h_before, y_before, stored):
            bg, bu, b0, b1 = 4, 5, 6, 7
            raw, high = w[2].rearrange("p k n -> p (k n)"), w_high.rearrange("p k n -> p (k n)")
            m_high = self.copy(act, high.bitcast(F32R), raw, landed[2], *y_before)
            self.tt(dve, low.rearrange("p k n -> p (k n)").bitcast(F32R), raw, high, ALU.subtract, m_high)
            self.pe.wait(x_ready, h_before)
            ends = []
            for which, b in ((0, bg), (1, bu)):
                for n in range(KF):
                    ends.append(self.product(self.psum[b][:, n * cap:(n + 1) * cap],
                                lambda k: w[which][:, k, :].rearrange("p (f n) -> p n f", n=KF)[:, n, :],
                                lambda k: xt[:, j, k * cap:(k + 1) * cap], KD,
                                last=frees[which] if n == KF - 1 else None, wait=(landed[which],)))
            m = self.fn(act_h, self.psum[bg][:, 0:KF * cap], ACT.Silu, ends[KF - 1], h_before)
            h_ready = self.tt(dve, act_h, act_h, self.psum[bu][:, 0:KF * cap], ALU.mult, m, ends[-1])
            m_high = self.copy(act, h_high.bitcast(F32R), act_h, h_ready, *y_before)
            m_low = self.tt(dve, h_low.bitcast(F32R), act_h, h_high, ALU.subtract, m_high)
            between()
            self.pe.wait(m_high, *y_before)
            out = []
            parts = ((h_high, w_high), (h_high, low), (h_low, w_high))
            for n, (b, lane) in enumerate(((b0, dve), (b1, act))):
                for q, (h, v) in enumerate(parts):
                    if q == 2:
                        self.pe.wait(m_low)
                    for k in range(KF):
                        final = k == KF - 1 and (q == 2 or n == 1 and q == 1)
                        end = self.mm(self.psum[b][0:cap, :], h[:, k * cap:(k + 1) * cap].bitcast(F32R),
                                      v[:, k, n * 512:(n + 1) * 512].bitcast(F32R), q == 0 and k == 0,
                                      q == 2 and k == KF - 1, mark=final, inc=frees[2] if n == 1 and q == 1 else None)
                out.append(self.copy(lane, yb[0:cap, j, n * 512:(n + 1) * 512], self.psum[b][0:cap, :], end, stored))
            return m_low, tuple(out)

        def store(j, row, counter, *marks):
            return act.do(lambda e, i: e.dma_start(y_rows[row(i), :], yb[0:cap, j, :]), *marks, inc=counter)

        tb = [[0, 1][:n_turned], [2, 3][:n_turned]]
        g.meet(*rows_out)
        gathered = gather(0, lambda i: slice(0, 1), s_gather[0], index_mark)
        turned(0, gathered, tb[0])
        gather(1, lambda i: slice(1, 2), s_gather[1])
        g.meet()

        g.loop_begin(EXPERTS // 2)
        carried = {n: Later() for n in ("gathered1", "x_ready0", "turned0", "h1", "y1a", "y1b", "store0", "store1")}
        wait_for = [dict(h_before=carried["h1"], y_before=(carried["y1a"], carried["y1b"]), stored=carried["store0"]),
                    None]
        x_ready = [carried["x_ready0"], None]
        gathered0 = gather(0, lambda i: bass.ds(i[0] * 2 + 2, 1), s_gather[0], carried["turned0"])
        for j in range(2):
            pieces, landed, frees = [], [], []
            for view, shape in ((gate, (KD, FF)), (up, (KD, FF)), (down, (KF, D))):
                (v,), mark = ring.load((shape, 0, lambda i, view=view, j=j:
                                        view[bass.ds(i[0] * 2 + j, 1)].rearrange("x p k n -> p (x k) n")))
                pieces.append(v)
                landed.append(mark)
                frees.append(ring.free)
            low = ring.rounded[ring.slot][:, :].rearrange("p (k n) -> p k n", k=KF)

            def between(j=j):
                if j == 0:
                    x_ready[1], _ = turned(1, carried["gathered1"], tb[1])
                else:
                    m, end = turned(0, gathered0, tb[0])
                    carried["x_ready0"].set(m)
                    carried["turned0"].set(end)

            h, y = expert(j, x_ready[j], pieces, low, landed, frees, between, **wait_for[j])
            stored = store(j, lambda i, j=j: bass.ds(i[0] * (2 * cap) + j * cap, cap), s_yout[j], *y)
            carried[f"store{j}"].set(stored)
            if j == 0:
                carried["gathered1"].set(gather(1, lambda i: bass.ds(i[0] * 2 + 3, 1), s_gather[1], x_ready[1]))
                wait_for[1] = dict(h_before=h, y_before=y, stored=carried["store1"])
            else:
                carried["h1"].set(h)
                carried["y1a"].set(y[0])
                carried["y1b"].set(y[1])
        g.loop_end()
        y_out = [s_yout[0].now(), s_yout[1].now()]
        g.meet(*y_out, s_gather[0].now(), s_gather[1].now())

        all_free = [f.now() for f in ring.frees]
        before = [lane.done.now() for lane in g.lanes[:4]]
        name = f"more_{layer}"
        for lane in g.lanes:
            lane.wait(flag_mark)
        g.branch_begin(name)
        banks_before, g.bank_free = g.bank_free, [[] for _ in range(8)]
        self.sp.wait(*all_free, *before)
        for n in range(1, n_blocks):
            index_block(n)
        self.copy(act, act_h[:, 0:1], self.col("token")[:, 0:1])
        self.pool.do(lambda e, i: e.memset(xe, 0.0))
        marks = [lane.done.now() for lane in g.lanes[:4]]
        for lane in g.lanes:
            lane.wait(*marks)
        m_landed, m_gather, m_out = (g.counter(f"{name}_{n}") for n in ("landed", "gathered", "y_out"))
        g.loop_begin(n_blocks - 1, EXPERTS)
        products_before = Later()
        self.sp.wait(products_before)
        linear_index = lambda i: i[0] * EXPERTS + i[1]
        views = []
        for slot_no, (view, shape) in enumerate(((gate, (KD, FF)), (up, (KD, FF)), (down, (KF, D)))):
            v = ring.slots[slot_no][:, :].rearrange("p (k n) -> p k n", k=shape[0])
            landed = self.sp.do(lambda e, i, v=v, view=view: e.dma_start(
                v, view[bass.ds(i[1], 1)].rearrange("x p k n -> p (x k) n")), inc=m_landed)
            views.append(v)
        low = ring.rounded[2][:, :].rearrange("p (k n) -> p k n", k=KF)
        gathered = gather(0, lambda i: bass.ds(linear_index(i) + EXPERTS, 1), m_gather)
        x_mark, _ = turned(0, gathered, tb[0])
        h, y = expert(0, x_mark, views, low, [landed] * 3, [None] * 3, lambda: None, None, (), None)
        out = store(0, lambda i: bass.ds(linear_index(i) * cap + EXPERTS * cap, cap), m_out, *y)
        products_before.set(self.pe.done.now())
        marks = [lane.done.now() for lane in g.lanes[:4]]
        for lane in g.lanes[:4]:
            lane.wait(*marks, out, gathered)
        g.loop_end()
        self.sp.wait(self.pe.done.now())
        g.bank_free = banks_before
        g.branch_end(flag[0:1, 0:1].bitcast(I32))

        self.prepare(self.conv_first if layer == 0 else self.ssm_first)

        ar.at = keep
        ga = [[ar.take(D) for _ in range(2)] for _ in range(NT)]
        self.pool.wait(*y_out)
        squares = Squares(self, SEQ, [ar.take(KD, P), ar.take(KD, P)])
        back = []
        for t, pair in enumerate(ga):
            for j in range(2):
                def fetch_rows(e, source, j=j, t=t, o=pair[j]):
                    return e.indirect_dma_start(out=o, out_offset=None, in_=source, in_offset=offset(
                        ap=dest[j][:, t:t + 1].bitcast(U32), axis=0))
                mark = self.pool.either(lambda e, f=fetch_rows: f(e, y_rows),
                                        lambda e, f=fetch_rows: f(e, y_rows[0:EXPERTS * cap, :]), inc=s_back[t])
            back.append(mark)
        for t, pair in enumerate(ga):
            self.ts(dve, pair[0], pair[0], weight[0][:, t:t + 1], None, ALU.mult, None, back[t])
            m = self.stt(pair[0], pair[1], weight[1][:, t:t + 1], pair[0], ALU.mult, ALU.add, chain=True)
            for half in range(2):
                b = g.bank()
                for k in range(4):
                    end = self.turn(self.psum[b][:, k * P:(k + 1) * P],
                                    pair[0][:, (4 * half + k) * P:(4 * half + k + 1) * P], mark=k == 3, wait=(m,))
                for k in range(4):
                    kk = 4 * half + k
                    at = self.X[:, kk, t * P:(t + 1) * P]
                    c = t * P // SEQ
                    m2 = self.stt(at, self.psum[b][:, k * P:(k + 1) * P], self.mod[:, layer, 5 * KD + kk, c:c + 1], at,
                                  ALU.mult, ALU.add, end)
                g.bank_free[b] = [m2]
            if t < SEQ // P:
                squares.tokens(t, m2)
        squares.close()

    def ssm_first(self):
        return self.split_weights(self.a["ssm_w_in_2"][0], KD, 0, 512)

    def ssm(self):
        g, a, T = self.g, self.a, SEQ
        dve, act, pool, pe = self.dve, self.act, self.pool, self.pe
        NC = T // CHUNK
        ar = self.stage()
        (Z, Z_rounded), (XBC, XBC_rounded) = ar.take_twins(NC, D_INNER), ar.take_twins(32, T)
        pad_w = SSM_CONV - 1
        PB, acc = ar.take(4, T + pad_w), ar.take(4, T)
        dt, acs, eacs, adt = (ar.take(NC, HEADS) for _ in range(4))
        t1, t2, tail = ar.take(NC, HEADS), ar.take(NC, HEADS), ar.take(HEADS)
        neg_a = ar.take(HEADS)
        pads = pool.do(lambda e, i: e.memset(PB, 0.0))
        chunk = self.take_prepared(self.ssm_first)
        w_in = a["ssm_w_in_2"][0]
        A = self.A
        x_high, x_low = x_parts = self.parts_of_A()
        ready = self.norm_parts(lambda k: A[:, k, 0:T], self.col("a_norm"), self.residual_stat(T, A), x_high, x_low)

        def by_tokens(c):
            return [lambda k, x=x: x(k)[:, c * P:(c + 1) * P] for x in x_parts]

        for n in range(D_INNER // 512):
            after = self.split_weights(w_in, KD, (n + 1) * 512, 512)
            ((w_high,), (w_low,)), marks, frees = chunk
            chunk = after
            for c in range(NC):
                b = g.bank()
                end = self.product3(self.psum[b][:, :], by_tokens(c), (lambda k: w_high[:, k, :], lambda k: w_low[:, k, :]),
                                    KD, wait=marks, tiles=ready, frees=frees if c == NC - 1 else (None, None),
                                    weights_move=True)
                m = self.fn(Z[:, c, n * 512:(n + 1) * 512], self.psum[b][:, :], ACT.Silu, end)
                g.bank_free[b] = [m]

        taps, cb = self.col("ssm_conv_w"), self.col("ssm_conv_b")
        conv_free, acc_free = [pads] * 4, [None] * 4

        def evac(m, out, mark):
            s = m % 4
            end = self.copy(act, PB[:, s, pad_w:], out, mark, conv_free[s])
            buf = acc[:, m % 4, :]
            done = self.fn(buf, PB[:, s, 0:T], ACT.Copy, end, acc_free[m % 4], scale=taps[:, m, 0:1])
            for j in range(1, SSM_CONV):
                done = self.stt(buf, PB[:, s, j:j + T], taps[:, m, j:j + 1], buf, ALU.mult, ALU.add, done)
            conv_free[s] = done
            waiting.append((m, buf, done))
            activate()
            return end

        waiting = []

        def activate(behind=2):
            if len(waiting) > behind:
                m, buf, done = waiting.pop(0)
                acc_free[m % 4] = self.fn(XBC[:, m, :], buf, ACT.Silu, done, bias=cb[:, m:m + 1])

        dt_weights = w_in.rearrange("(k p) n -> p k n", p=P)[:, :, D_INNER + 4096:D_INNER + 4096 + HEADS]
        chunk = self.linear3(w_in[:, D_INNER:], KD, 4096, x_parts, T, evac, first_chunk=chunk,
                             then=lambda: self.split(((KD, HEADS), 0, lambda i: dt_weights)))
        activate(0)
        activate(0)

        ((w_high,), (w_low,)), marks, frees = chunk
        b = g.bank()
        for c in range(NC):
            end = self.product3(self.psum[b][:, c * HEADS:(c + 1) * HEADS], by_tokens(c),
                                (lambda k: w_high[:, k, :], lambda k: w_low[:, k, :]), KD, wait=marks,
                                frees=frees if c == NC - 1 else (None, None), weights_move=True)
        raw = self.psum[b][:, 0:NC * HEADS].rearrange("p (c h) -> p c h", c=NC)
        m = self.tt(dve, dt, raw, across(self.row("dt_bias"), NC), ALU.add, end)
        g.bank_free[b] = [m]
        self.ts(dve, t1, dt, -1.0, None, ALU.mult, None, chain=True)
        m = self.tt(dve, t1, t1, dt, ALU.max, chain=True)
        m = self.fn(t1, t1, ACT.Exp, m, scale=-1.0)
        u = self.ts(dve, t2, t1, 1.0, None, ALU.add, None, m)
        m = self.fn(acs, t2, ACT.Ln, u)
        self.ts(dve, adt, t2, -1.0, None, ALU.add, None, chain=True)
        self.tt(dve, adt, t1, adt, ALU.subtract, chain=True)
        dve.chain(lambda e, i: e.reciprocal(t2, t2), m)
        self.tt(dve, adt, adt, t2, ALU.mult, chain=True)
        self.tt(dve, adt, adt, acs, ALU.add, m, chain=True)
        self.stt(dt, dt, 0.0, adt, ALU.max, ALU.add, chain=True)
        ma = self.fn(neg_a, self.row("a_log"), ACT.Exp)
        self.ts(dve, neg_a, neg_a, -1.0, None, ALU.mult, None, ma)
        m_adt = self.tt(dve, adt, dt, across(neg_a, NC), ALU.mult, chain=True)

        b = g.bank()
        flat = lambda v: v.rearrange("p c h -> p (c h)")
        self.mm(self.psum[b][:, 0:NC * HEADS], self.mat("upto"), flat(adt), True, True, wait=(m_adt,))
        end = self.mm(self.psum[b][:, 128:128 + HEADS], self.mat("ones"), adt[:, 0, :], True, True, mark=True)
        m_acs = self.copy(dve, flat(acs), self.psum[b][:, 0:NC * HEADS], end)
        m = self.tt(dve, tail, self.psum[b][:, 128:128 + HEADS], acs[:, 0, :], ALU.subtract, chain=True)
        g.bank_free[b] = [m]
        m_tail = self.fn(tail, tail, ACT.Exp, m)
        m_eacs = self.fn(eacs, acs, ACT.Exp, m_acs)

        g.meet()
        XS = A[:, :, :].rearrange("p k t -> p (k t)").rearrange("p (c n) -> p c n", c=NC)
        BT = PB.rearrange("p a b -> p (a b)")[:, 0:SSM_G * STATE]
        XC = [ar.take(SSM_G, HG * HEAD_P), self.X[:, :, SEQ:]]
        for c in range(NC):
            for q in range(4):
                b = g.bank()
                for j in range(4):
                    end = self.turn(self.psum[b][:, j * P:(j + 1) * P], XBC[:, 4 * q + j, c * P:(c + 1) * P], mark=j == 3)
                m = self.copy(act, XS[:, c, q * 512:(q + 1) * 512], self.psum[b][:, :], end)
                g.bank_free[b] = [m]
            xs = XS[:, c, :].rearrange("p (h d) -> p h d", h=HEADS)
            by_group = lambda v: v.rearrange("p g (h d) -> p g h d", d=HEAD_P)
            m = self.tt(dve, by_group(XC[c]), by_group(XS[:, c, :].rearrange("p (g n) -> p g n", g=SSM_G)),
                        along(dt[:, c, :].rearrange("p (g h) -> p g h", g=SSM_G), HEAD_P), ALU.mult, m)
            m_skip = self.tt(pool, xs, xs, along(self.row("d_skip"), HEAD_P), ALU.mult, m)
        m_xc = m
        for q in range(2):
            b = g.bank()
            for j in range(4):
                end = self.turn(self.psum[b][:, j * P:(j + 1) * P], XBC[:, 16 + 4 * q + j, 0:P], mark=j == 3)
            m_bt = self.copy(act, BT[:, q * 512:(q + 1) * 512], self.psum[b][:, :], end)
            g.bank_free[b] = [m_bt]

        mask = ar.take(CHUNK)
        m_mask = self.fetch(mask, a["ssm_mask"])
        work = XBC[:, 0:16, :].rearrange("p m t -> p (m t)")
        cut = lambda n, w: work[:, n * w:(n + 1) * w]
        R = [cut(0, 512), cut(1, 512)]
        E = [cut(2, 512), cut(3, 512)]
        CB = [cut(16, 128), cut(17, 128)]
        XD, PREV, YO = cut(9, 256), cut(10, 256), cut(11, 256)
        pe.wait(m_xc, m_bt)
        r_free, e_free, cb_free = [None] * 2, [None] * 2, [None] * 2
        step = 0
        xd_free = prev_free = None
        last_turn = pe.done.now()
        for lane in (dve, pool, act):
            lane.wait(last_turn)
        for grp in range(SSM_G):
            hs = slice(grp * HG, (grp + 1) * HG)
            ch = slice(grp * HG * HEAD_P, (grp + 1) * HG * HEAD_P)
            for c in range(NC):
                s = step % 2
                step += 1
                bt, ct = XBC[:, 16 + grp, c * P:(c + 1) * P], XBC[:, 24 + grp, c * P:(c + 1) * P]
                b = g.bank()
                end = self.mm(self.psum[b][:, 0:P], bt, ct, True, True, mark=True)
                m_cb = self.copy(act, CB[s], self.psum[b][:, 0:P], end, cb_free[s])
                g.bank_free[b] = [m_cb]
                r4 = R[s].rearrange("p (h t) -> p h t", h=HG)
                m = self.tt(pool, r4, across(self.mat("upto"), HG), along(adt[:, c, hs], P), ALU.mult, r_free[s])
                b = g.bank()
                end = self.mm(self.psum[b][:, :], self.mat("ones"), R[s], True, True, mark=True, wait=(m,))
                r_free[s] = end
                e4 = E[s].rearrange("p (h t) -> p h t", h=HG)
                m = self.tt(dve, e4, self.psum[b][:, :].rearrange("p (h t) -> p h t", h=HG),
                            along(acs[:, c, hs], P), ALU.subtract, end, e_free[s])
                g.bank_free[b] = [m]
                m = self.tt(dve, e4, e4, across(mask, HG), ALU.add, m_mask, chain=True)
                m = self.fn(E[s], E[s], ACT.Exp, m)
                m = self.tt(dve, e4, e4, across(CB[s], HG), ALU.mult, m, m_cb)
                cb_free[s] = m
                b = g.bank()
                for h in range(HG):
                    end = self.mm(self.psum[b][:, h * HEAD_P:(h + 1) * HEAD_P], E[s][:, h * P:(h + 1) * P],
                                  XC[c][:, grp, h * HEAD_P:(h + 1) * HEAD_P], True, True, mark=h == HG - 1, wait=(m,))
                e_free[s] = end
                y = XS[:, c, ch]
                if c == 0:
                    m = self.tt(dve, y, self.psum[b][:, 0:256], y, ALU.add, end, m_skip)
                    g.bank_free[b] = [m]
                    m = self.tt(dve, XD.rearrange("p (h d) -> p h d", h=HG),
                                XC[0][:, grp, :].rearrange("p (h d) -> p h d", h=HG), along(tail[:, hs], HEAD_P),
                                ALU.mult, m_tail, xd_free)
                    b = g.bank()
                    end = self.mm(self.psum[b][:, 0:256], BT[:, grp * STATE:(grp + 1) * STATE], XD, True, True,
                                  mark=True, wait=(m,))
                    xd_free = end
                    m_prev = self.copy(act, PREV, self.psum[b][:, 0:256], end, prev_free)
                    g.bank_free[b] = [m_prev]
                else:
                    m = self.tt(dve, y, self.psum[b][:, 0:256], y, ALU.add, end, m_skip)
                    g.bank_free[b] = [m]
                    b = g.bank()
                    end = self.mm(self.psum[b][:, 0:256], ct, PREV, True, True, mark=True, wait=(m_prev,))
                    prev_free = end
                    self.tt(dve, YO.rearrange("p (h d) -> p h d", h=HG),
                            self.psum[b][:, 0:256].rearrange("p (h d) -> p h d", h=HG), along(eacs[:, 1, hs], HEAD_P),
                            ALU.mult, end, m_eacs)
                    g.bank_free[b] = [dve.done.now()]
                    self.tt(dve, y, y, YO, ALU.add, chain=True)

        ss = t1.rearrange("p c h -> p (c h)")[:, 0:NC * SSM_G].rearrange("p (c g) -> p c g", c=NC)
        pe_last = pe.done.now()
        for c in range(NC):
            self.tt(dve, XS[:, c, :], XS[:, c, :], Z[:, c, :], ALU.mult, chain=True)
            m = dve.done.now()
            m = self.fn(XC[c], XS[:, c, :].rearrange("p (g n) -> p g n", g=SSM_G), ACT.Square, m, pe_last)
            dve.do(lambda e, i, c=c: e.tensor_reduce(
                ss[:, c, :], XC[c], AX.X, ALU.add), m)
        m = self.ts(dve, ss, ss, 1.0 / 256.0, GATED_EPS, ALU.mult, ALU.add, chain=True)
        dve.do(lambda e, i: e.reciprocal(ss, ss), self.fn(ss, ss, ACT.Sqrt, m))
        for c in range(NC):
            y = XS[:, c, :].rearrange("p (g n) -> p g n", g=SSM_G)
            m = self.tt(dve, y, y, along(ss[:, c, :], 256), ALU.mult, chain=True)
        Y_low = Z_rounded.rearrange("p c n -> p (c n)").rearrange("p (m t) -> p m t", m=16)
        Y_high = XBC_rounded[:, 16:32, :]
        y_ready = ([], [])
        gain = self.col("ssm_norm")
        out_chunk = self.split_weights(a["ssm_w_out_2"][0], 16, 0, 256)
        for q in range(8):
            b = g.bank()
            for j in range(2):
                for c in range(NC):
                    end = self.turn(self.psum[b][:, (2 * j + c) * P:(2 * j + c + 1) * P],
                                    XS[:, c, (2 * q + j) * P:(2 * q + j + 1) * P], mark=j and c, wait=(m,))
            for j in range(2):
                n, out = 2 * q + j, self.psum[b][:, 2 * j * P:(2 * j + 2) * P]
                high = self.ts(dve, Y_high[:, n, :].bitcast(F32R), out, gain[:, n:n + 1], None, ALU.mult, None, end)
                m2 = self.stt(Y_low[:, n, :].bitcast(F32R), out, gain[:, n:n + 1], Y_high[:, n, :], ALU.mult,
                              ALU.subtract, chain=True)
                y_ready[0].append(high)
                y_ready[1].append(m2)
            g.bank_free[b] = [m2]
        squares = self.squares()
        self.linear3(a["ssm_w_out_2"][0], 16, D, (lambda k: Y_high[:, k, :], lambda k: Y_low[:, k, :]), T,
                     self.add_plain(squares), width=256, inputs=y_ready, first_chunk=out_chunk,
                     then=lambda: self.prepare(lambda: self.ffn_first(0)))
        squares.close()

    def up_chunk(self, layer, n):
        w_up = self.a["ffn_w_up_2"][layer].rearrange("(k p) (j n) -> p k j n", p=P, j=2)
        return self.split(((KD, 256), 0, lambda i: w_up[:, :, 0, n * 256:(n + 1) * 256]),
                          ((KD, 256), KD * 256, lambda i: w_up[:, :, 1, n * 256:(n + 1) * 256]))

    def ffn_first(self, layer):
        return self.up_chunk(layer, 0)

    def ffn(self, layer):
        g, a, T = self.g, self.a, SEQ
        dve, act = self.dve, self.act
        ar = self.stage()
        pad = FFN_CONV - 1
        (H, H_rounded), H_high = ar.take_twins(KFF, T), ar.take_rounded(KFF, T)
        PB, acc = ar.take(4, 2, T + pad), ar.take(4, 2, T)
        pads = self.pool.do(lambda e, i: e.memset(PB, 0.0))
        h_high, h_low = [], []
        taps = self.col("ffn_conv_w")
        pb_free, acc_free = [pads] * 4, [None] * 4
        w_down = a["ffn_w_down_2"][layer].rearrange("(k p) n -> p k n", p=P)

        def down_chunk(first, n_k):
            return self.split(((n_k, D), 0, lambda i: w_down[:, first:first + n_k, :]))

        waiting = []

        def make_h(behind=1):
            if len(waiting) <= behind:
                return
            m, s, done = waiting.pop(0)
            silu = self.fn(acc[:, s, 0, :], acc[:, s, 0, :], ACT.Silu, done)
            acc_free[s] = self.tt(self.pool, H[:, m, :], acc[:, s, 0, :], acc[:, s, 1, :], ALU.mult, silu, done)
            marks_h = self.halved(H[:, m, :], H_high[:, m, :], H_rounded[:, m, :], acc_free[s], lane=self.pool)
            h_high.append(marks_h[0])
            h_low.append(marks_h[1])

        chunk = self.take_prepared(lambda: self.ffn_first(layer))
        x_high, x_low = self.parts_of_A()
        ready = self.norm_parts(lambda k: self.A[:, k, 0:T], self.col("ffn_norm")[:, layer, :],
                                self.residual_stat(T, self.A), x_high, x_low)
        down = [(0, KFF % 4)] + [(f, 4) for f in range(KFF % 4, KFF, 4)]
        for n in range(KFF // 2):
            after = self.up_chunk(layer, n + 1) if n + 1 < KFF // 2 else down_chunk(*down[0])
            (high, low), marks, frees = chunk
            chunk = after
            for t in range(2):
                m = 2 * n + t
                s = m % 4
                b = g.bank()
                for j in range(2):
                    parts = [lambda k, w=w: w[j][:, k, t * P:(t + 1) * P] for w in (high, low)]
                    end = self.product3(self.psum[b][:, j * T:(j + 1) * T], parts, (x_high, x_low), KD, wait=marks,
                                        tiles=ready, frees=frees if t == 1 and j == 1 else (None, None))
                make_h()
                mark = self.copy(act, PB[:, s, :, pad:], self.psum[b][:, :].rearrange("p (j t) -> p j t", j=2),
                                 end, pb_free[s])
                g.bank_free[b] = [mark]
                for j in range(2):
                    buf, w3 = acc[:, s, j, :], taps[:, layer, j * KFF + m, :]
                    self.ts(dve, buf, PB[:, s, j, 0:T], w3[:, 0:1], None, ALU.mult, None, mark, acc_free[s])
                    for q in (1, 2):
                        done = self.stt(buf, PB[:, s, j, q:q + T], w3[:, q:q + 1], buf, ALU.mult, ALU.add, chain=True)
                pb_free[s] = done
                waiting.append((m, s, done))
        make_h(0)
        make_h(0)
        self.pe.wait(*[m for f in g.bank_free for m in f])
        g.bank_free, g.bank_at = [None] * 8, 0
        squares = self.squares()
        for n, (first, n_k) in enumerate(down):
            final = n + 1 == len(down)
            after = (down_chunk(*down[n + 1]) if not final else
                     self.prepare(self.attention_first) if layer == 0 else None)
            ((high,), (low,)), marks, frees = chunk
            chunk = after
            for m in range(KD):
                parts = [lambda k, w=w: w[:, k, m * P:(m + 1) * P] for w in (high, low)]
                h_parts = [lambda k, h=h: h[:, first + k, :] for h in (H_high, H_rounded)]
                out = self.psum[m][:, 0:T]
                end = self.product3(out, parts, h_parts, n_k, wait=marks, start=n == 0, stop=final,
                                    tiles=(h_high[first:first + n_k], h_low[first:first + n_k]),
                                    frees=frees if m == KD - 1 else (None, None))
                if final:
                    g.bank_free[m] = [self.tt(self.dve, self.X[:, m, 0:T], out, self.X[:, m, 0:T], ALU.add, end)]
                    squares.tile(m, g.bank_free[m][0])
        squares.close()

    def attention_first(self):
        return self.split_weights(self.a["w_kv_2"], KD, 0, 512)

    def dilated(self):
        g, a, T = self.g, self.a, SEQ
        dve, act = self.dve, self.act
        ar = self.stage()
        n_kv = N_PAT * ATT_KV
        Q, K, V = ar.take(N_PAT * ATT_HEADS, T), ar.take(n_kv, T), ar.take(2, n_kv * ATT_D)
        cos, sin, rot = ar.take(2, T), ar.take(2, T), ar.take(P)
        widths = [N_PAT * att_keys(q) for q in range(2)]
        mask = ar.take(sum(widths))
        S = [ar.take(w) for w in widths]
        turned = ar.take(2, T)
        small = ar.take(3, 2)
        plain, rounded = (x.rearrange("p k t -> p (k t)") for x in (self.A, self.A_rounded))
        half = lambda x, j: x[:, j * KD * T:(j + 1) * KD * T].rearrange("p (k t) -> p k t", k=KD)
        AK, AK_low, AK_high = half(plain, 0), half(rounded, 0), half(rounded, 1)
        (AQ, AQ_low), AQ_high = ar.take_twins(KD, T), ar.take_rounded(KD, T)
        tiles_of = lambda *xs: [lambda k, x=x: x[:, k, :] for x in xs]
        k_parts, q_parts = tiles_of(AK_high, AK_low), tiles_of(AQ_high, AQ_low)
        sources = ([(a["w_kv_2"], KD, n * 512, 512) for n in range(3)] +
                   [(a["att_w_q_2"][0], KD, n * 512, 512) for n in range(6)] + [(a["att_w_o_2"][0], KD, 0, 512)])
        chunks = [self.take_prepared(self.attention_first)]

        def next_chunk():
            chunks.append(self.split_weights(*sources[len(chunks)]))
            return chunks[-2]
        for j in range(2):
            self.fetch(cos[:, j, :], a["tables"][:, 640:640 + T])
            self.fetch(sin[:, j, :], a["tables"][:, 896:896 + T])
        self.fetch(rot, a["tables"][:, 1152:1152 + P])
        tables = self.fetch(mask, a["att_mask"])
        stat = self.residual_stat(T, AK)
        k_ready = self.norm_parts(lambda k: AK[:, k, :], self.col("kv_norm"), stat, *k_parts)
        q_ready = self.norm_parts(lambda k: AQ[:, k, :], self.col("b_norm"), stat, *q_parts)
        R = ROPE_DIM

        def rotary(two, mark):
            b = g.bank()
            end = self.mm(self.psum[b][:, :], rot, two.rearrange("p m t -> p (m t)"), True, True, mark=True,
                          wait=(mark, tables))
            out = self.psum[b][0:R, :].rearrange("p (m t) -> p m t", m=2)
            m = self.tt(dve, turned[0:R], out, sin[0:R], ALU.mult, end, chain=True)
            g.bank_free[b] = [m]
            self.tt(dve, two[0:R], two[0:R], cos[0:R], ALU.mult, end)
            return self.tt(dve, two[0:R], two[0:R], turned[0:R], ALU.add, chain=True)

        def heads(chunk, n, rhs, tiles, dst, scale, last):
            ((high,), (low,)), marks, frees = chunk
            for t in range(0, n, 2):
                b = g.bank()
                for j in range(2):
                    cols = slice((t + j) * P, (t + j + 1) * P)
                    end = self.product3(self.psum[b][:, j * T:(j + 1) * T],
                                        (lambda k: high[:, k, cols], lambda k: low[:, k, cols]), rhs, KD, wait=marks,
                                        tiles=tiles, frees=frees if last and t + j == n - 1 else (None, None))
                two = dst[:, t:t + 2, :]
                m = self.fn(two, self.psum[b][:, :].rearrange("p (m t) -> p m t", m=2), ACT.Copy, end, scale=scale)
                g.bank_free[b] = [m]
                waiting.append((two, m))
                if len(waiting) > 1:
                    rotary(*waiting.pop(0))

        def tokens(chunk, cols, dst_at):
            ((high,), (low,)), marks, frees = chunk
            n = cols.stop - cols.start
            for c in range(2):
                b = g.bank()
                end = self.product3(self.psum[b][:, 0:n], [lambda k, x=x: x(k)[:, c * P:(c + 1) * P] for x in k_parts],
                                    (lambda k: high[:, k, cols], lambda k: low[:, k, cols]), KD, wait=marks,
                                    frees=frees if c == 1 else (None, None), weights_move=True)
                m = self.copy(act, V[:, c, dst_at:dst_at + n], self.psum[b][:, 0:n], end)
                g.bank_free[b] = [m]
            return m

        waiting = []
        heads(next_chunk(), 4, k_parts, k_ready, K[:, 0:4, :], 1.0, True)
        chunk = next_chunk()
        heads(chunk, 2, k_parts, k_ready, K[:, 4:6, :], 1.0, False)
        tokens(chunk, slice(256, 512), 0)
        tokens(next_chunk(), slice(0, 512), 256)
        for c in range(6):
            heads(next_chunk(), 4, q_parts, q_ready, Q[:, 4 * c:4 * c + 4, :], float(ATT_D) ** -0.5, True)
        rotary(*waiting.pop(0))
        g.meet()

        O_low, O_high = AK_high, AQ_high
        o_ready = ([], [])
        PT = [AK.rearrange("p k t -> p (k t)")[:, 0:widths[0]], AK.rearrange("p k t -> p (k t)")[:, widths[0]:sum(widths)]]
        s_free, pt_free = [None, None], [None, None]

        def scores(h, q):
            kv, n = h // (ATT_HEADS // ATT_KV), att_keys(q)
            banks, at = [], 0
            for p in range(N_PAT):
                if (at + n) > BANK or p == 0:
                    b, at = g.bank(), 0
                    banks.append([b, p, 0])
                end = self.mm(self.psum[b][:, at:at + n], Q[:, p * ATT_HEADS + h, q * P:(q + 1) * P],
                              K[:, p * ATT_KV + kv, 0:n], True, True, mark=True)
                at += n
                banks[-1][2] = at
            base = 0 if q == 0 else widths[0]
            for b, p, w in banks:
                lo = p * n
                m = self.tt(dve, S[q][:, lo:lo + w], self.psum[b][:, 0:w], mask[:, base + lo:base + lo + w], ALU.add,
                            end, s_free[q])
                g.bank_free[b] = [m]
            top, total, inv = (small[:, j, q:q + 1] for j in range(3))
            m = dve.chain(lambda e, i: e.tensor_reduce(top, S[q], AX.X, ALU.max, negate=True))
            m = self.fn(S[q], S[q], ACT.Exp, m, bias=top, total=total)
            dve.do(lambda e, i: e.reciprocal(inv, total), m)
            return self.ts(dve, S[q], S[q], inv, None, ALU.mult, None, chain=True)

        def values(h, q, mark):
            kv, n_b = h // (ATT_HEADS // ATT_KV), q + 1
            blocks = N_PAT * n_b
            for lo in range(0, blocks, 4):
                b = g.bank()
                hi = min(blocks, lo + 4)
                for j in range(lo, hi):
                    end = self.turn(self.psum[b][:, (j - lo) * P:(j - lo + 1) * P], S[q][:, j * P:(j + 1) * P],
                                    mark=j == hi - 1, wait=(mark,))
                m = self.copy(act, PT[q][:, lo * P:hi * P], self.psum[b][:, 0:(hi - lo) * P], end, pt_free[q])
                g.bank_free[b] = [m]
            s_free[q] = end
            b = g.bank()
            for j in range(blocks):
                p, c = divmod(j, n_b)
                at = (p * ATT_KV + kv) * ATT_D
                end = self.mm(self.psum[b][:, 0:P], V[:, c, at:at + ATT_D], PT[q][:, j * P:(j + 1) * P],
                              j == 0, j == blocks - 1, mark=j == blocks - 1, wait=(m,))
            pt_free[q] = end
            at = O_high[:, h, q * P:(q + 1) * P]
            high = self.copy(dve, at.bitcast(F32R), self.psum[b][:, 0:P], end)
            m = self.tt(dve, O_low[:, h, q * P:(q + 1) * P].bitcast(F32R), self.psum[b][:, 0:P], at, ALU.subtract,
                        chain=True)
            g.bank_free[b] = [m]
            if q == 1:
                o_ready[0].append(high)
                o_ready[1].append(m)

        order = [(h, q) for h in range(ATT_HEADS) for q in range(2)]
        before = scores(*order[0])
        for n, (h, q) in enumerate(order):
            after = scores(*order[n + 1]) if n + 1 < len(order) else None
            values(h, q, before)
            before = after
        squares = self.squares()
        self.linear3(a["att_w_o_2"][0], KD, D, tiles_of(O_high, O_low), T, self.add_plain(squares), inputs=o_ready,
                     first_chunk=chunks[-1], then=lambda: self.prepare(lambda: self.ffn_first(1)))
        squares.close()

    def finish(self):
        self.stage()
        m = self.simple_norm(self.col("final_2"))[-1]
        out = self.g.counter("result")
        y = self.a["y"].rearrange("(k p) t -> p k t", p=P)
        m = self.act.do(lambda e, i: e.dma_start(y, self.A[:, :, 0:SEQ]), m, inc=out)
        for lane in self.g.lanes:
            lane.wait(m)

    def between_networks(self):
        ar = self.stage()
        stat = self.residual_stat(SEQ, self.A)
        marks = self.scaled(self.X, self.X, self.col("final_1"), SEQ, KD, stat)
        squares = Squares(self, SEQ, [ar.take(SEQ), ar.take(SEQ)])
        for m, mark in enumerate(marks):
            squares.tile(m, mark)
        squares.close()

    def emit(self):
        with self.nc.Block() as block:
            for name, lane in zip(("tensor", "scalar", "vector", "gpsimd", "sync"), self.g.lanes):
                {"tensor": block.tensor, "scalar": block.scalar, "vector": block.vector,
                 "gpsimd": block.gpsimd, "sync": block.sync}[name](lambda e, lane=lane: lane.replay(e))


def build(nc, a, stop=None):
    with ExitStack() as ctx:
        k = Kernel(nc, ctx, a)
        k.start()
        stages = [k.mla, lambda: k.moe(0, SEQ + CTX, CAP[0]), k.conv_mixer,
                  lambda: k.moe(1, SEQ, CAP[1]), k.between_networks, k.ssm, lambda: k.ffn(0), k.dilated,
                  lambda: k.ffn(1), k.finish]
        for f in stages[:stop]:
            f()
        if stop is not None:
            k.stage()
            out = k.g.counter("dump")
            m = k.act.do(lambda e, i: e.dma_start(a["dump"].rearrange("(k p) t -> p k t", p=P), k.X[:, :, :]), inc=out)
            for lane in k.g.lanes:
                lane.wait(m)
        k.emit()


_WEIGHTS = ["w_mod", "mla_w_dq", "mla_w_uq", "mla_w_dkv", "mla_w_ukv", "mla_w_o", "conv_w_in", "conv_w_out",
            "moe_w_group", "moe_w_expert", "moe_w_gate", "moe_w_up", "moe_w_down", "ssm_w_in_2", "ssm_w_out_2",
            "w_kv_2", "att_w_q_2", "att_w_o_2", "ffn_w_up_2", "ffn_w_down_2"]


def _constants():
    f = np.float32
    i = np.arange(P)
    mats = np.stack([np.eye(P, dtype=f), np.full((P, P), 1 / 1024, f), np.full((P, P), 1 / 512, f),
                     np.full((P, P), 1 / 256, f), np.ones((P, P), f), (i[:, None] < i[None, :]).astype(f),
                     (i[:, None] <= i[None, :]).astype(f)], axis=1)
    t = np.arange(SEQ)
    tables = np.zeros((P, 1280), f)

    def rotary(at, d, pos, inv_freq, x, half):
        angle = pos.astype(f) * inv_freq[x % half]
        tables[d, at:at + SEQ] = np.cos(angle)
        tables[d, at + SEQ:at + 2 * SEQ] = np.sin(angle)
        if x < half:
            tables[d + half, at + 2 * SEQ + d] = -1
        else:
            tables[d - half, at + 2 * SEQ + d] = 1

    half = MLA_ROPE // 4
    inv = (f(ROPE_THETA) ** (-np.arange(half, dtype=f) / half)).astype(f)
    for d in range(P):
        x = d % MLA_ROPE
        rotary(0, d, t // GRID_W if x < MLA_ROPE // 2 else t % GRID_W, inv, x % (2 * half), half)
    half = ROPE_DIM // 2
    inv = (f(ROPE_THETA_2) ** (-np.arange(0, ROPE_DIM, 2, dtype=f) / ROPE_DIM)).astype(f)
    for d in range(ROPE_DIM):
        rotary(640, d, t, inv, d, half)
    masks = []
    for q in range(2):
        back = (q * P + i)[:, None] - np.arange(att_keys(q))[None, :]
        for window, dilation in PATTERNS:
            masks.append(np.where((back >= 0) & (back <= window) & (back % dilation == 0), 0, NEG))
    return {"mats": mats, "tables": tables, "att_mask": np.concatenate(masks, axis=1).astype(f),
            "ssm_mask": np.where(i[:, None] <= i[None, :], 0, NEG).astype(f)}


def _vectors(v):
    f = np.float32
    tiles = lambda x: np.moveaxis(x.reshape(*x.shape[:-1], -1, P), -1, 0)
    taps = lambda x: np.moveaxis(tiles(x), -2, -1)
    parts = {"cond": np.stack([tiles(v["c"][0]), tiles(v["c_ctx"])], -1), "b_mod": tiles(v["b_mod"]),
             "norm_mix": tiles(v["norm_mix_g"]), "norm_ffn": tiles(v["norm_ffn_g"]), "g_q": tiles(v["mla_g_q"][0]),
             "g_kv": tiles(v["mla_g_kv"][0]), "conv_w": taps(v["conv_w"][0]), "final_1": tiles(v["final_norm_g"]),
             "a_norm": tiles(v["a_norm_2"][0]), "ssm_conv_w": taps(v["ssm_conv_w_2"][0]),
             "ssm_conv_b": tiles(v["ssm_conv_b_2"][0]), "ssm_norm": tiles(v["ssm_norm_2"][0]),
             "kv_norm": tiles(v["kv_norm_2"]), "b_norm": tiles(v["b_norm_2"][0]), "ffn_norm": tiles(v["ffn_norm_2"]),
             "ffn_conv_w": taps(v["ffn_conv_w_2"]), "final_2": tiles(v["final_norm_2"]),
             "token": np.arange(P * 4, dtype=f).reshape(4, P).T}
    cols = np.concatenate([parts[n].reshape(P, -1) for n in column_layout()[0]], axis=1)
    rows = {"first_4": np.arange(GROUPS, 0, -1, dtype=f), "first_8": np.arange(PER_GROUP, 0, -1, dtype=f),
            "count": np.arange(P, dtype=f), "dt_bias": v["ssm_dt_bias_2"][0], "a_log": v["ssm_a_log_2"][0],
            "d_skip": v["ssm_d_2"][0]}
    for j in range(2):
        rows[f"route_bias_{j}"] = np.concatenate([v["moe_b_group"][j], v["moe_b_expert"][j]])
    return cols, np.concatenate([rows[n] for n in row_layout()[0]])[None, :]


def arrays_of(inputs):
    v = {k: np.asarray(x) for k, x in inputs.items()}
    arrays = {n: v[n] for n in _WEIGHTS}
    arrays |= _constants()
    arrays["cols"], arrays["rows"] = _vectors(v)
    arrays["xT"], arrays["ctxT"] = v["x"][0].T, v["ctx"][0].T
    return {k: np.ascontiguousarray(x) for k, x in arrays.items()}


def kernel(**inputs):
    import concourse.bacc as bacc
    from concourse.bass_utils import run_bass_kernel_spmd

    nc = bacc.Bacc("TRN2", target_bir_lowering=False, num_devices=1)
    arrays, a = {}, {}
    for name, x in arrays_of(inputs).items():
        arrays[f"in_{name}"] = x
        a[name] = nc.dram_tensor(f"in_{name}", x.shape, mybir.dt.from_np(x.dtype), kind="ExternalInput").ap()
    a["y"] = nc.dram_tensor("y", [D, SEQ], F32, kind="ExternalOutput").ap()
    build(nc, a)
    got = run_bass_kernel_spmd(nc, [arrays], core_ids=[0]).results[0]["y"]
    return np.ascontiguousarray(np.asarray(got).T)[None]
```
